# Optimizing a Trainium2 kernel written in Bass

```python
import math
import jax, jax.numpy as jnp
from jax import lax
import numpy as np

D_MODEL = 1024
BATCH = 1
SEQ = 256
DEPTH = 1

HG_HEADS = 4
HG_DK = 128
HG_DV = 128
HG_WIDTH = HG_HEADS * HG_DK
HG_VWIDTH = HG_HEADS * HG_DV
HG_CHUNK = 64
MB_HEADS = 8
MB_DH = 64
MB_WIDTH = MB_HEADS * MB_DH
MB_BLOCK = 256
MB_TOPK = 3
MB_QCHUNK = 64
REL_BUCKETS = 32
REL_MAX_DIST = 2048
MEM_LEN = 256
X_HEADS = 4
X_DH = D_MODEL // X_HEADS
PEER_HEADS = 8
PEER_NKEYS = 128
PEER_EXPERTS = PEER_NKEYS * PEER_NKEYS
PEER_TOPK = 16
PEER_DKEY = 256
PEER_HALF = PEER_DKEY // 2
PEER_TOK_CHUNK = 512
EPS = 1e-6
IN_SPLITS = [HG_WIDTH, HG_WIDTH, HG_VWIDTH, HG_VWIDTH, MB_WIDTH, MB_WIDTH, MB_WIDTH, D_MODEL, D_MODEL]
IN_COLS = int(sum(IN_SPLITS))
IN_OFFSETS = [int(o) for o in np.cumsum(IN_SPLITS)[:-1]]

kernel_name = "hybrid_hgrn2_moba_peer_block"

def rmsnorm(x, g):
    xf = x.astype(jnp.float32)
    xf = xf * lax.rsqrt(jnp.mean(xf * xf, axis=-1, keepdims=True) + EPS)
    return (xf * g.astype(jnp.float32)).astype(x.dtype)

def t5_bucket(dist):
    max_exact = REL_BUCKETS // 2
    is_small = dist < max_exact
    scaled = jnp.log(jnp.maximum(dist, 1).astype(jnp.float32) / max_exact) / math.log(REL_MAX_DIST / max_exact)
    large = max_exact + (scaled * (REL_BUCKETS - max_exact)).astype(jnp.int32)
    large = jnp.minimum(large, REL_BUCKETS - 1)
    return jnp.where(is_small, dist, large)

def hgrn2(q, f_logit, i, g, lb, norm_gain):
    B, S, _ = q.shape
    nc = S // HG_CHUNK
    f = lb + (1.0 - lb) * jax.nn.sigmoid(f_logit.astype(jnp.float32))
    log_f = jnp.log(f)
    k = 1.0 - f

    def chunks(t, d):
        return t.astype(jnp.float32).reshape(B, nc, HG_CHUNK, HG_HEADS, d).transpose(1, 0, 3, 2, 4)

    causal = jnp.tril(jnp.ones((HG_CHUNK, HG_CHUNK), dtype=bool))[:, :, None]

    def step(state, inp):
        qq, kk, lf, vv = inp
        b = jnp.cumsum(lf, axis=2)
        diff = b[:, :, :, None, :] - b[:, :, None, :, :]
        decay = jnp.exp(jnp.where(causal, diff, -jnp.inf))
        a = jnp.einsum('bhtd,bhsd,bhtsd->bhts', qq, kk, decay)
        o = jnp.einsum('bhts,bhse->bhte', a, vv) + jnp.einsum('bhtd,bhde->bhte', qq * jnp.exp(b), state)
        b_end = b[:, :, -1:, :]
        state = jnp.exp(b_end[:, :, 0, :, None]) * state + jnp.einsum('bhsd,bhse->bhde', kk * jnp.exp(b_end - b), vv)
        return state, o

    init = jnp.zeros((B, HG_HEADS, HG_DK, HG_DV), jnp.float32)
    _, o = lax.scan(step, init, (chunks(q, HG_DK), chunks(k, HG_DK), chunks(log_f, HG_DK), chunks(i, HG_DV)))
    o = o.transpose(1, 0, 3, 2, 4).reshape(B, S, HG_HEADS, HG_DV)
    o = o * lax.rsqrt(jnp.mean(o * o, axis=-1, keepdims=True) + EPS)
    o = o.reshape(B, S, HG_VWIDTH) * norm_gain.astype(jnp.float32) * jax.nn.silu(g.astype(jnp.float32))
    return o.astype(q.dtype)

def moba(q, k, v, rel_bias):
    B, S, _ = q.shape
    Sp = -(-S // MB_BLOCK) * MB_BLOCK
    pad = Sp - S

    def heads(t):
        t = jnp.pad(t, ((0, 0), (0, pad), (0, 0)))
        return t.reshape(B, Sp, MB_HEADS, MB_DH).transpose(0, 2, 1, 3)

    q, k, v = heads(q), heads(k), heads(v)
    nb = Sp // MB_BLOCK
    kb = k.reshape(B, MB_HEADS, nb, MB_BLOCK, MB_DH)
    vb = v.reshape(B, MB_HEADS, nb, MB_BLOCK, MB_DH)
    gate = jnp.einsum('bhsd,bhnd->bhsn', q, jnp.mean(kb, axis=3)).astype(jnp.float32)
    pos = jnp.arange(Sp)
    fully_past = jnp.arange(nb)[None, :] < (pos // MB_BLOCK)[:, None]
    gate = jnp.where(fully_past, gate, -jnp.inf)
    n_sel = min(MB_TOPK, nb)
    sel_score, sel_idx = lax.top_k(gate, n_sel)
    sel_valid = jnp.isfinite(sel_score)
    nqc = Sp // MB_QCHUNK

    def qchunks(t):
        return jnp.moveaxis(t.reshape((B, MB_HEADS, nqc, MB_QCHUNK) + t.shape[3:]), 2, 0)

    scale = MB_DH ** -0.5
    bias_tab = rel_bias.T
    b_ix = jnp.arange(B)[:, None, None, None]
    h_ix = jnp.arange(MB_HEADS)[None, :, None, None]

    def one_chunk(args):
        c, qc, ic, vc = args
        q0 = c * MB_QCHUNK
        qpos = q0 + jnp.arange(MB_QCHUNK)
        ks = kb[b_ix, h_ix, ic]
        vs = vb[b_ix, h_ix, ic]
        s_sel = jnp.einsum('bhqd,bhqnld->bhqnl', qc, ks).astype(jnp.float32) * scale
        kpos = ic[..., None] * MB_BLOCK + jnp.arange(MB_BLOCK)
        dist = qpos[:, None, None] - kpos
        s_sel = s_sel + bias_tab[h_ix[..., None], t5_bucket(jnp.maximum(dist, 0))].astype(jnp.float32)
        s_sel = jnp.where(vc[..., None], s_sel, -jnp.inf).reshape(B, MB_HEADS, MB_QCHUNK, n_sel * MB_BLOCK)
        blk0 = (q0 // MB_BLOCK) * MB_BLOCK
        k_own = lax.dynamic_slice_in_dim(k, blk0, MB_BLOCK, axis=2)
        v_own = lax.dynamic_slice_in_dim(v, blk0, MB_BLOCK, axis=2)
        dist_own = qpos[:, None] - (blk0 + jnp.arange(MB_BLOCK))[None, :]
        s_own = jnp.einsum('bhqd,bhld->bhql', qc, k_own).astype(jnp.float32) * scale
        s_own = s_own + bias_tab[:, t5_bucket(jnp.maximum(dist_own, 0))].astype(jnp.float32)
        s_own = jnp.where(dist_own >= 0, s_own, -jnp.inf)
        p = jax.nn.softmax(jnp.concatenate([s_sel, s_own], axis=-1), axis=-1).astype(v.dtype)
        p_sel = p[..., :n_sel * MB_BLOCK].reshape(B, MB_HEADS, MB_QCHUNK, n_sel, MB_BLOCK)
        p_own = p[..., n_sel * MB_BLOCK:]
        return jnp.einsum('bhqnl,bhqnld->bhqd', p_sel, vs) + jnp.einsum('bhql,bhld->bhqd', p_own, v_own)

    outs = lax.map(one_chunk, (jnp.arange(nqc), qchunks(q), qchunks(sel_idx), qchunks(sel_valid)))
    out = jnp.moveaxis(outs, 0, 2).reshape(B, MB_HEADS, Sp, MB_DH)[:, :, :S]
    return out.transpose(0, 2, 1, 3).reshape(B, S, MB_WIDTH)

def cross_attn(h, mem_n, wq, wk, wv, wo):
    B, S, _ = h.shape
    M = mem_n.shape[1]
    q = (h @ wq).reshape(B, S, X_HEADS, X_DH)
    k = (mem_n @ wk).reshape(B, M, X_HEADS, X_DH)
    v = (mem_n @ wv).reshape(B, M, X_HEADS, X_DH)
    s = jnp.einsum('bshd,bmhd->bhsm', q, k).astype(jnp.float32) * (X_DH ** -0.5)
    p = jax.nn.softmax(s, axis=-1).astype(v.dtype)
    o = jnp.einsum('bhsm,bmhd->bshd', p, v).reshape(B, S, D_MODEL)
    return o @ wo

def peer(h, w_query, sub_keys, expert_u, expert_v):
    B, S, D = h.shape
    T = B * S
    Tp = -(-T // PEER_TOK_CHUNK) * PEER_TOK_CHUNK
    xt = jnp.pad(h.reshape(T, D), ((0, Tp - T), (0, 0))).reshape(Tp // PEER_TOK_CHUNK, PEER_TOK_CHUNK, D)

    def chunk_fn(xc):
        tc = xc.shape[0]
        qh = (xc @ w_query).reshape(tc, PEER_HEADS, 2, PEER_HALF)
        sc = jnp.einsum('thcd,hcnd->thcn', qh, sub_keys).astype(jnp.float32)
        s_top, i_top = lax.top_k(sc, PEER_TOPK)
        cand = (s_top[..., 0, :, None] + s_top[..., 1, None, :]).reshape(tc, PEER_HEADS, PEER_TOPK * PEER_TOPK)
        cand_idx = (i_top[..., 0, :, None] * PEER_NKEYS + i_top[..., 1, None, :]).reshape(tc, PEER_HEADS, PEER_TOPK * PEER_TOPK)
        s_fin, pos = lax.top_k(cand, PEER_TOPK)
        e_idx = jnp.take_along_axis(cand_idx, pos, axis=-1)
        w = jax.nn.softmax(s_fin, axis=-1)
        u = expert_u[e_idx]
        act = jax.nn.gelu(jnp.einsum('td,thkd->thk', xc, u).astype(jnp.float32))
        coef = (w * act).astype(xc.dtype)
        return jnp.einsum('thk,thkd->td', coef, expert_v[e_idx])

    y = lax.map(chunk_fn, xt).reshape(Tp, D)[:T]
    return y.reshape(B, S, D)

def setup_inputs(seed: int = 0) -> dict:
    key = jax.random.key(seed)
    ks = jax.random.split(key, 24)
    f32 = jnp.float32
    nrm = lambda k, shape, s: jax.random.normal(k, shape, f32) * s
    gain = lambda k, shape: 1.0 + 0.01 * jax.random.normal(k, shape, f32)
    return {
        "x": nrm(ks[0], (BATCH, SEQ, D_MODEL), 1.0),
        "mem": nrm(ks[1], (BATCH, MEM_LEN, D_MODEL), 1.0),
        "rel_bias": nrm(ks[2], (REL_BUCKETS, MB_HEADS), 0.5),
        "ln_mix": gain(ks[3], (DEPTH, D_MODEL)),
        "w_in": nrm(ks[4], (DEPTH, D_MODEL, IN_COLS), D_MODEL ** -0.5),
        "hg_lower": nrm(ks[5], (DEPTH + 1, HG_WIDTH), 0.5),
        "hg_norm": gain(ks[6], (DEPTH, HG_VWIDTH)),
        "w_up_a": nrm(ks[7], (DEPTH, HG_VWIDTH, D_MODEL), HG_VWIDTH ** -0.5),
        "w_up_b": nrm(ks[8], (DEPTH, MB_WIDTH, D_MODEL), MB_WIDTH ** -0.5),
        "w_out": nrm(ks[9], (DEPTH, D_MODEL, D_MODEL), D_MODEL ** -0.5),
        "ln_cross": gain(ks[10], (DEPTH, D_MODEL)),
        "ln_mem": gain(ks[11], (DEPTH, D_MODEL)),
        "wq_x": nrm(ks[12], (DEPTH, D_MODEL, D_MODEL), D_MODEL ** -0.5),
        "wk_x": nrm(ks[13], (DEPTH, D_MODEL, D_MODEL), D_MODEL ** -0.5),
        "wv_x": nrm(ks[14], (DEPTH, D_MODEL, D_MODEL), D_MODEL ** -0.5),
        "wo_x": nrm(ks[15], (DEPTH, D_MODEL, D_MODEL), D_MODEL ** -0.5),
        "ln_ffn": gain(ks[16], (DEPTH, D_MODEL)),
        "peer_query": nrm(ks[17], (DEPTH, D_MODEL, PEER_HEADS * PEER_DKEY), D_MODEL ** -0.5),
        "peer_subkeys": nrm(ks[18], (DEPTH, PEER_HEADS, 2, PEER_NKEYS, PEER_HALF), PEER_HALF ** -0.5),
        "peer_u": nrm(ks[19], (DEPTH, PEER_EXPERTS, D_MODEL), D_MODEL ** -0.5),
        "peer_v": nrm(ks[20], (DEPTH, PEER_EXPERTS, D_MODEL), 0.5),
        "ln_final": gain(ks[21], (D_MODEL,)),
    }

def reference(x, mem, rel_bias, ln_mix, w_in, hg_lower, hg_norm, w_up_a, w_up_b, w_out,
              ln_cross, ln_mem, wq_x, wk_x, wv_x, wo_x, ln_ffn,
              peer_query, peer_subkeys, peer_u, peer_v, ln_final):
    lb_all = jnp.cumsum(jax.nn.softmax(hg_lower.astype(jnp.float32), axis=0), axis=0)
    for l in range(DEPTH):
        h = rmsnorm(x, ln_mix[l])
        proj = h @ w_in[l]
        hq, hf, hi, hg, mq, mk, mv, ga, gb = jnp.split(proj, IN_OFFSETS, axis=-1)
        ya = hgrn2(hq, hf, hi, hg, lb_all[l], hg_norm[l])
        yb = moba(mq, mk, mv, rel_bias)
        z = jax.nn.sigmoid(ga) * (ya @ w_up_a[l]) + jax.nn.sigmoid(gb) * (yb @ w_up_b[l])
        x = x + z @ w_out[l]
        h = rmsnorm(x, ln_cross[l])
        x = x + cross_attn(h, rmsnorm(mem, ln_mem[l]), wq_x[l], wk_x[l], wv_x[l], wo_x[l])
        h = rmsnorm(x, ln_ffn[l])
        x = x + peer(h, peer_query[l], peer_subkeys[l], peer_u[l], peer_v[l])
    return rmsnorm(x, ln_final)


_drawn_inputs = setup_inputs


def setup_inputs(seed=0):
    import zlib

    import numpy as np

    out = dict(_drawn_inputs(seed))
    spreads = {}
    factors = {'hg_norm': 3.82, 'ln_cross': 8.0, 'ln_mem': 6.067, 'ln_final': 30.134, 'ln_ffn': 8.0}
    for name, (base, spread) in spreads.items():
        noise = np.random.default_rng([zlib.crc32(name.encode()), seed]).standard_normal(out[name].shape)
        drawn = base * np.exp(spread * noise) if base else spread * noise
        out[name] = __import__('jax').numpy.asarray(drawn.astype(out[name].dtype))
    for name, factor in factors.items():
        out[name] = (out[name] * factor).astype(out[name].dtype)
    return out
```

```python
import numpy as np
import concourse.bass as bass
from concourse import mybir
from contextlib import ExitStack

D = 1024
T = 256
P = 128
KD = D // P
TT = T // P
HG_H, HG_D = 4, 128
CHUNK = 64
MB_H, MB_D = 8, 64
X_H, X_D = 4, 256
PH, PK = 8, 16
NKEY = 128
NEXP = NKEY * NKEY
EPS = 1e-6
BUCKETS, MAX_DIST = 32, 2048
ROW = 384
NEG = -1e30
LOWEST = -3e38
LEVELS = [1, 2, 4, 8, 16, 32, 64]
WSLOT = 4096
NW = 3
NG = 4
GROUP = 2
NS = 4


def hybrid_layer(nc, x, mem, rel_bias, w_in, w_up_a, w_up_b, w_out, wq_x, wk_x, wv_x, wo_x,
                 peer_query, subkeys, peer_u, peer_v, gains, hg_lower, hg_norm, ln_final,
                 onehot, masks, iota, out):
    f32, u32 = mybir.dt.float32, mybir.dt.uint32
    ALU, ACT, AX = mybir.AluOpType, mybir.ActivationFunctionType, mybir.AxisListType

    chunks = []
    for name, src, c0, n, form in [
            ("hf", w_in, 1, 1, "T"), ("hq", w_in, 0, 1, "T"), ("mq", w_in, 4, 1, "T"), ("mk", w_in, 5, 1, "T"),
            ("hi", w_in, 2, 1, "N"), ("hg", w_in, 3, 1, "N"), ("mv", w_in, 6, 1, "N"),
            ("ga", w_in, 7, 2, "T"), ("gb", w_in, 9, 2, "T"), ("kx", wk_x, 0, 2, "T"), ("vx", wv_x, 0, 2, "N"),
            ("upa", w_up_a, 0, 1, "U"), ("upb", w_up_b, 0, 1, "U"), ("out", w_out, 0, 2, "N"),
            ("qx", wq_x, 0, 2, "T"), ("wo", wo_x, 0, 2, "N"), ("pq", peer_query, 0, 4, "T")]:
        for c in range(n):
            chunks.append((f"{name}{c}", src[c0 + c], form))
    chunk_no = {c[0]: n for n, c in enumerate(chunks)}
    banks_of = {"T": 2, "N": 2, "U": 4}
    bank_no, bank_reader, seen = {}, [], {}
    for name, _, form in chunks:
        bank_no[name] = len(bank_reader)
        for _ in range(banks_of[form]):
            fam = name[:-1]
            seen[fam] = seen.get(fam, 0) + 1
            bank_reader.append((f"{fam}_read", seen[fam]))
    aux_uses = [("bias0", "bias_read", 1), ("bias1", "bias_read", 2), ("bias2", "bias_read", 3), ("bias3", "bias_read", 4),
                ("tx0", "hT_ready", 1), ("tx1", "hT_ready", 2), ("Ldiag", "level_read", 1), ("L1", "level_read", 2),
                ("S0", "biased", 2), ("S1a", "biased", 4), ("S1b", "biased", 6),
                ("L2", "level_read", 3), ("L4", "level_read", 4), ("L8", "level_read", 5), ("L16", "level_read", 6),
                ("L32", "level_read", 7), ("L64", "level_read", 8), ("L128", "far_read", 1),
                ("PTa", "PT_read", 1), ("PTb", "PT_read", 2), ("PTc", "PT_read", 3), ("PV", "ybT_ready", 1),
                ("O", "o_read", 1), ("tm0", "hT_ready", 3), ("tm1", "hT_ready", 4), ("TY", "yaT_ready", 1),
                ("tc0", "hT_ready", 5), ("tc1", "hT_ready", 6), ("CS0", "xexp", 4), ("CS1", "xexp", 8),
                ("CT0", "CPT_read", 1), ("CT1", "CPT_read", 2), ("CV0", "oxT_ready", 1), ("CV1", "oxT_ready", 2),
                ("tf0", "hT_ready", 7), ("tf1", "hT_ready", 8),
                ("PS0", "sc_read", 1), ("PS1", "sc_read", 2), ("PS2", "sc_read", 3), ("PS3", "sc_read", 4),
                ("TR", "IJW_ready", 1)]
    aux_no = {n: i for i, (n, _, _) in enumerate(aux_uses)}

    ctx = ExitStack()
    with ctx:
        def sb(name, shape, dt=f32):
            return ctx.enter_context(nc.sbuf_tensor(name, shape, dt))

        def sem(name):
            return ctx.enter_context(nc.semaphore(name))

        x_sb = sb("x_sb", [P, TT, D])
        hT = sb("hT", [P, KD, T])
        ident = sb("ident", [P, P])
        gain_sb = sb("gain_sb", [P, 4, KD])
        hgn_sb = sb("hgn_sb", [P, HG_H])
        low_sb = sb("low_sb", [P, 2, HG_H])
        lb = sb("lb", [P, 2, HG_H])
        tiny = sb("tiny", [P, 4, HG_H])
        stat = sb("stat", [P, 6, 16])
        smx = sb("smx", [P, 6, 16])
        relb = sb("relb", [BUCKETS + 1, MB_H])
        onehot_sb = sb("onehot_sb", [BUCKETS + 1, ROW])
        iota_sb = sb("iota_sb", [P, NKEY])
        arena = sb("arena", [P, 48128])

        def at_(off, *dims):
            n = int(np.prod(dims))
            v = arena[:, off:off + n]
            if len(dims) == 1:
                return v
            names = "abcd"[:len(dims)]
            return v.rearrange(f"p ({' '.join(names)}) -> p {' '.join(names)}", **dict(zip(names, dims)))

        wring = [at_(s * WSLOT, WSLOT) for s in range(NW)]
        kxT = at_(12288, KD, T)
        vx = at_(14336, TT, D)
        o = 16384

        def take(*dims):
            nonlocal o
            v = at_(o, *dims)
            o += int(np.prod(dims))
            return v
        hqT = take(HG_H, T)
        kT = take(HG_H, T)
        bsum = take(HG_H * T)
        E_ = take(HG_H * T)
        DI = take(HG_H * T)
        sgB = at_(o, KD, T)
        QE = [take(HG_H, T) for _ in range(2)]
        AT01 = at_(o, HG_H, P)
        yaT = at_(o, HG_H, T)
        KE = [take(HG_H, T) for _ in range(2)]
        ATd = take(HG_H * TT, P)
        hi_sb = take(TT, HG_H * HG_D)
        hg_sb = take(TT, HG_H * HG_D)
        mask_sb = take(len(LEVELS), P)
        mqT = take(MB_H // 2, T)
        mkT = take(MB_H // 2, T)
        mv_sb = take(TT, MB_H * MB_D)
        bias_rows = take(MB_H, ROW)
        biasB = take(MB_H, T)
        S0 = take(MB_H, P)
        S1 = take(MB_H, T)
        ybT = take(MB_H // 2, T)
        sgA = take(KD, T)
        zT = take(KD, T)
        hn = take(TT, D)
        assert o <= 48128, o
        PT = bias_rows
        PT0 = bias_rows.rearrange("p a b -> p (a b)")[:, 0:2048].rearrange("p (h q) -> p h q", h=MB_H)
        PT1 = bias_rows.rearrange("p a b -> p (a b)")[:, 2048:3072].rearrange("p (h q) -> p h q", h=MB_H)
        relbb = ybT.rearrange("p a b -> p (a b)").rearrange("p (h q) -> p h q", h=MB_H)
        hgtmp = sgA.rearrange("p a b -> p (a b)")[:, HG_H * T:].rearrange("p (t q) -> p t q", t=TT)
        restart = sgA.rearrange("p a b -> p (a b)")[:, 0:HG_H * T]
        mem_sb = zT.rearrange("p a b -> p (a b)").rearrange("p (t d) -> p t d", t=TT)
        osb = E_.rearrange("p (t h e) -> p t h e", t=TT, h=HG_H)
        osq = DI.rearrange("p (t h e) -> p t h e", t=TT, h=HG_H)
        qxT = at_(16384, KD, T)
        CS = at_(18432, TT, X_H, T)
        CPT = at_(20480, TT, X_H, T)
        oxT = at_(22528, KD, T)
        qhT = at_(16384, 2 * PH, T)
        subT = at_(20480, 2 * PH, NKEY)
        sc = at_(22528, TT, 2 * PH, NKEY)
        sc2 = at_(26624, TT, 2 * PH, NKEY)
        cand = at_(0, PH, PK * PK)
        cand2 = at_(2048, PH, PK * PK)
        eq = at_(4096, PH * PK, PK)
        eq2 = at_(6144, PH * PK, PK)
        sv = at_(8192, TT, 2 * PH, PK)
        si = at_(8704, TT, 2 * PH, PK)
        sif = at_(9216, TT, 2 * PH, PK)
        fv = at_(9728, TT, PH, PK)
        pos = at_(9984, TT, PH, PK)
        ab = at_(10240, 2, PH * PK)
        abf = at_(10496, 2, PH * PK)
        rIJW = at_(10752, 3, TT, P)
        wsum = at_(11520, TT, PH)
        gate = at_(0, NKEY, T)
        uring = [at_(32768 + 1024 * s, KD, P) for s in range(NS)]
        vring = [at_(36864 + 1024 * s, D) for s in range(NS)]
        actr = [at_(40960 + 256 * s, T) for s in range(2)]
        coef = [at_(41472 + 256 * s, T) for s in range(2)]
        NL = 8
        ohL = [at_(41984 + 128 * s, NKEY) for s in range(NL)]
        ohR = [at_(43008 + 128 * s, NKEY) for s in range(NL)]
        IJW = at_(44032, 3, T)
        fgain = at_(44800, D)
        yfin = at_(45824, TT, D)

        bias_d = nc.dram_tensor("bias_rows_dram", (MB_H, P, ROW), f32, kind="Internal")

        gb_ = [ctx.enter_context(nc.psum_tensor(f"proj{i}", [P, 512], f32)) for i in range(NG)]
        aux = [ctx.enter_context(nc.psum_tensor(f"aux{i}", [P, 1024], f32)) for i in range(2)]

        sems = {}

        def S(name):
            if name not in sems:
                sems[name] = ctx.enter_context(nc.semaphore(name))
            return sems[name]

        w_here = [S(f"w_here{s}") for s in range(NW)]
        u_here = [S(f"u_here{s}") for s in range(NS // GROUP)]
        v_here = [S(f"v_here{s}") for s in range(NS // GROUP)]
        x_here, mem_here, const_here, masks_here = S("x_here"), S("mem_here"), S("const_here"), S("masks_here")
        proj_full, aux_full = S("proj_full"), S("aux_full")
        u_done, v_done, gelu_done, coef_done = S("u_done"), S("v_done"), S("gelu_done"), S("coef_done")
        onehots, spread_done, spread_out = S("onehots_ready"), S("spread_done"), S("spread_out")
        for _, r, _ in aux_uses:
            S(r)
        for r, _ in bank_reader:
            S(r)
        for n in ["bias_rows_out", "bias_here", "sub_here", "fgain_here", "out_done", "cleared", "restart_ones",
                  "restart_ready", "neg_ready", "relbb_ready", "ssq", "var", "root", "hn_ready",
                  "low_ready", "low_exp", "k_ready", "lf_ready", "b_ready", "diff", "decay", "QK",
                  "mb_max", "mb_exp", "mb_prob", "silu_ready", "sig_ready", "z_ready", "x_new",
                  "o_ready", "x_max", "x_prob", "w_diff", "w_exp", "rIJW_ready", "y_ready",
                  "dve_chain", "act_chain"]:
            S(n)
        block = ctx.enter_context(nc.Block())

        def bank_end(name):
            n = chunk_no[name]
            return bank_no[name] + banks_of[chunks[n][2]]

        @block.sync
        def _(sp):
            sp.dma_start(x_sb[:, :, :], x.rearrange("(t p) d -> p t d", p=P)).then_inc(x_here, 16)
            sp.wait_ge(S("neg_ready"), 1)
            sp.dma_start(relb[0:BUCKETS, :], rel_bias).then_inc(const_here, 16)
            sp.dma_start(onehot_sb[:, :], onehot).then_inc(const_here, 16)
            sp.dma_start(ident[:, :], masks[len(LEVELS)]).then_inc(const_here, 16)
            sp.dma_start(gain_sb[:, :, :], gains).then_inc(const_here, 16)
            sp.dma_start(hgn_sb[:, :], hg_norm).then_inc(const_here, 16)
            sp.dma_start(low_sb[:, :, :], hg_lower).then_inc(const_here, 16)
            sp.dma_start(iota_sb[:, :], iota).then_inc(const_here, 16)

            def load_w(n):
                if n >= NW:
                    sp.wait_ge(proj_full, bank_end(chunks[n - NW][0]))
                sp.dma_start(wring[n % NW], chunks[n][1]).then_inc(w_here[n % NW], 16)
            for n in range(NW):
                load_w(n)
            sp.dma_start(mem_sb, mem.rearrange("(t p) d -> p t d", p=P)).then_inc(mem_here, 16)
            sp.dma_start(mask_sb, masks[0:len(LEVELS)].rearrange("l s t -> s l t")).then_inc(masks_here, 16)
            sp.wait_ge(S("bias_read"), 4)
            sp.dma_start(bias_d.ap().rearrange("h p r -> p h r"), bias_rows).then_inc(S("bias_rows_out"), 16)
            sp.wait_ge(S("bias_rows_out"), 16)
            skew = bass.AP(tensor=bias_d, offset=P - 1, ap=[[ROW - 1, P], [P * ROW, MB_H], [1, T]])
            sp.dma_start(biasB, skew).then_inc(S("bias_here"), 16)
            for n in range(NW, len(chunks)):
                load_w(n)
            sp.wait_ge(aux_full, aux_no["CV1"] + 1)
            sp.dma_start(subT, subkeys).then_inc(S("sub_here"), 16)

            def load_u(g, s):
                sp.dma_start(at_(32768 + 2048 * s, 2048),
                             peer_u[g].rearrange("o p c -> (o p) c")).then_inc(u_here[s], 16)

            def load_v(g, s):
                sp.dma_start(at_(36864 + 2048 * s, GROUP, D),
                             peer_v[g].rearrange("o (a p) d -> p (o a) d", a=GROUP)).then_inc(v_here[s], 16)
            sp.wait_ge(S("hT_ready"), 8)
            for s in range(2):
                load_u(slice(s, s + 1), s)
                load_v(slice(s, s + 1), s)
            sp.dma_start(fgain, ln_final.partition_broadcast(P)).then_inc(S("fgain_here"), 16)
            with sp.Fori(1, NEXP // P // NS) as r:
                for s in range(2):
                    sp.wait_ge(u_done, NS * r + GROUP * s + GROUP - NS)
                    load_u(bass.ds(2 * r + s, 1), s)
                    sp.wait_ge(v_done, NS * r + GROUP * s + GROUP - NS)
                    load_v(bass.ds(2 * r + s, 1), s)
            sp.wait_ge(S("y_ready"), 2)
            sp.dma_start(out.rearrange("(t p) d -> p t d", p=P), yfin).then_inc(S("out_done"), 16)
            sp.wait_ge(S("out_done"), 16)

        @block.gpsimd
        def _(pool):
            nc.gpsimd.memset(relb[:, :], NEG).then_inc(S("neg_ready"), 1)
            nc.gpsimd.memset(restart, 1.0).then_inc(S("restart_ones"), 1)
            for b in (QE[0], QE[1], KE[0], KE[1], ATd):
                nc.gpsimd.memset(b, 0.0).then_inc(S("cleared"), 1)
            pool.wait_ge(S("restart_ones"), 1)
            nc.gpsimd.memset(restart.rearrange("p (n c) -> p n c", c=CHUNK)[:, :, 0:1], 0.0).then_inc(S("restart_ready"), 1)

        @block.tensor
        def _(pe):
            def aux_open(name):
                n = aux_no[name]
                if n >= 2:
                    pe.wait_ge(S(aux_uses[n - 2][1]), aux_uses[n - 2][2])
                return aux[n % 2]

            def mm(o_, l, r, start, stop):
                return nc.tensor.matmul(o_, l, r, start=start, stop=stop)

            def project(name, act):
                n, form = chunk_no[name], chunks[chunk_no[name]][2]
                pe.wait_ge(w_here[n % NW], 16 * (n // NW + 1))
                kd = 4 if form == "U" else KD
                w = wring[n % NW].rearrange("p (k c) -> p k c", k=kd)
                for b in range(4 if form == "U" else 2):
                    g = bank_no[name] + b
                    if g >= NG:
                        pe.wait_ge(S(bank_reader[g - NG][0]), bank_reader[g - NG][1])
                    ps = gb_[g % NG]
                    if form == "N":
                        for k in range(kd):
                            last = mm(ps[:, :], act[:, k, b * P:(b + 1) * P], w[:, k, :], k == 0, k == kd - 1)
                    else:
                        for f in range(2):
                            for k in range(kd):
                                c = (2 * b + f) * P
                                last = mm(ps[:, f * T:(f + 1) * T], w[:, k, c:c + P], act[:, k, :], k == 0, k == kd - 1)
                    last.then_inc(proj_full, 1)

            def turn(name, src, ks):
                ps = aux_open(name)
                for i, k in enumerate(ks):
                    for t in range(TT):
                        last = nc.tensor.transpose(ps[:, i * T + t * P:i * T + (t + 1) * P],
                                                   src[:, t, k * P:(k + 1) * P], ident[:, :])
                last.then_inc(aux_full, 1)

            pe.wait_ge(const_here, 16 * 7)
            pe.wait_ge(S("relbb_ready"), 1)
            for n in range(4):
                ps = aux_open(f"bias{n}")
                for j in range(2):
                    last = mm(ps[:, 512 * j:512 * j + ROW], relbb[0:BUCKETS + 1, 2 * n + j, :],
                              onehot_sb[:, :], True, True)
                last.then_inc(aux_full, 1)
            pe.wait_ge(S("hn_ready"), 2)
            turn("tx0", hn, range(0, 4))
            turn("tx1", hn, range(4, 8))
            pe.wait_ge(S("hT_ready"), 2)
            project("hf0", hT)
            project("hq0", hT)
            project("mq0", hT)

            def level(L):
                ps = aux_open(f"L{L}")
                if L == "diag":
                    pe.wait_ge(S("hq_read"), 2)
                    pe.wait_ge(S("k_ready"), 1)
                    q, k = hqT, kT
                else:
                    i = (LEVELS + [128]).index(L)
                    pe.wait_ge(S("QK"), i + 1)
                    i %= 2
                    q, k = QE[i], KE[i]
                for h in range(HG_H):
                    if L == 128:
                        last = mm(ps[:, h * P:(h + 1) * P], k[:, h, 0:P], q[:, h, P:T], True, True)
                    else:
                        for t in range(TT):
                            b = h * TT + t
                            last = mm(ps[:, b * P:(b + 1) * P], k[:, h, t * P:(t + 1) * P],
                                      q[:, h, t * P:(t + 1) * P], True, True)
                last.then_inc(aux_full, 1)

            level("diag")
            project("mk0", hT)
            level(1)
            pe.wait_ge(S("mq_read"), 2)
            pe.wait_ge(S("mk_read"), 2)
            for name, t, heads, nk in (("S0", 0, range(8), P), ("S1a", 1, range(4), T), ("S1b", 1, range(4, 8), T)):
                ps = aux_open(name)
                for i, h in enumerate(heads):
                    r = slice((h % 2) * MB_D, (h % 2 + 1) * MB_D)
                    c = 512 * (h % 2) + (i // 2) * nk
                    last = mm(ps[:, c:c + nk], mqT[r, h // 2, t * P:(t + 1) * P],
                              mkT[r, h // 2, 0:nk], True, True)
                last.then_inc(aux_full, 1)
            project("hi0", hT)
            level(2)
            level(4)
            project("hg0", hT)
            level(8)
            level(16)
            project("mv0", hT)
            level(32)
            level(64)
            level(128)
            pe.wait_ge(S("mb_prob"), 2)
            for name, items in (("PTa", [(S0, S1, h) for h in range(4)]), ("PTb", [(S0, S1, h) for h in range(4, 8)])):
                ps = aux_open(name)
                for i, (p0, p1, h) in enumerate(items):
                    nc.tensor.transpose(ps[:, i * T:i * T + P], p0[:, h, :], ident[:, :])
                    last = nc.tensor.transpose(ps[:, i * T + P:i * T + T], p1[:, h, 0:P], ident[:, :])
                last.then_inc(aux_full, 1)
            ps = aux_open("PTc")
            for h in range(MB_H):
                last = nc.tensor.transpose(ps[:, h * P:(h + 1) * P], S1[:, h, P:T], ident[:, :])
            last.then_inc(aux_full, 1)
            project("ga0", hT)
            pe.wait_ge(S("PT_read"), 3)
            pe.wait_ge(S("mv_read"), 2)
            ps = aux_open("PV")
            for h in range(MB_H):
                r = slice((h % 2) * MB_D, (h % 2 + 1) * MB_D)
                c = (h // 2) * T
                mm(ps[r, c:c + T], mv_sb[:, 0, h * MB_D:(h + 1) * MB_D], PT0[:, h, :], True, False)
                last = mm(ps[r, c + P:c + T], mv_sb[:, 1, h * MB_D:(h + 1) * MB_D], PT1[:, h, :], False, True)
            last.then_inc(aux_full, 1)
            project("ga1", hT)
            pe.wait_ge(S("far_read"), 1)
            pe.wait_ge(S("level_read"), 8)
            pe.wait_ge(S("hi_read"), 2)
            ps = aux_open("O")
            for h in range(HG_H):
                e = slice(h * HG_D, (h + 1) * HG_D)
                mm(ps[:, e], ATd[:, h * TT, :], hi_sb[:, 0, e], True, True)
                e1 = slice(512 + h * HG_D, 512 + (h + 1) * HG_D)
                mm(ps[:, e1], AT01[:, h, :], hi_sb[:, 0, e], True, False)
                last = mm(ps[:, e1], ATd[:, h * TT + 1, :], hi_sb[:, 1, e], False, True)
            last.then_inc(aux_full, 1)
            project("gb0", hT)
            project("gb1", hT)
            pe.wait_ge(S("hn_ready"), 4)
            turn("tm0", hn, range(0, 4))
            turn("tm1", hn, range(4, 8))
            pe.wait_ge(S("hT_ready"), 4)
            project("kx0", hT)
            project("kx1", hT)
            pe.wait_ge(S("o_ready"), 1)
            ps = aux_open("TY")
            for h in range(HG_H):
                for t in range(TT):
                    last = nc.tensor.transpose(ps[:, h * T + t * P:h * T + (t + 1) * P], osb[:, t, h, :], ident[:, :])
            last.then_inc(aux_full, 1)
            project("vx0", hT)
            project("vx1", hT)
            pe.wait_ge(S("yaT_ready"), 1)
            project("upa0", yaT)
            pe.wait_ge(S("ybT_ready"), 1)
            project("upb0", ybT)
            pe.wait_ge(S("z_ready"), 4)
            project("out0", zT)
            project("out1", zT)
            pe.wait_ge(S("hn_ready"), 6)
            turn("tc0", hn, range(0, 4))
            turn("tc1", hn, range(4, 8))
            pe.wait_ge(S("hT_ready"), 6)
            project("qx0", hT)
            project("qx1", hT)
            pe.wait_ge(S("qx_read"), 4)
            pe.wait_ge(S("kx_read"), 4)
            for t in range(TT):
                ps = aux_open(f"CS{t}")
                for h in range(X_H):
                    for k in range(2):
                        last = mm(ps[:, h * T:(h + 1) * T], qxT[:, 2 * h + k, t * P:(t + 1) * P],
                                  kxT[:, 2 * h + k, :], k == 0, k == 1)
                last.then_inc(aux_full, 1)
            pe.wait_ge(S("x_prob"), 2)
            for m in range(TT):
                ps = aux_open(f"CT{m}")
                for h in range(X_H):
                    for t in range(TT):
                        last = nc.tensor.transpose(ps[:, h * T + t * P:h * T + (t + 1) * P],
                                                   CS[:, t, h, m * P:(m + 1) * P], ident[:, :])
                last.then_inc(aux_full, 1)
            pe.wait_ge(S("CPT_read"), 2)
            pe.wait_ge(S("vx_read"), 4)
            for c in range(2):
                ps = aux_open(f"CV{c}")
                for j in range(4):
                    f = 4 * c + j
                    for m in range(TT):
                        last = mm(ps[:, j * T:(j + 1) * T], vx[:, m, f * P:(f + 1) * P], CPT[:, m, f // 2, :], m == 0, m == 1)
                last.then_inc(aux_full, 1)
            pe.wait_ge(S("oxT_ready"), 2)
            project("wo0", oxT)
            project("wo1", oxT)
            pe.wait_ge(S("hn_ready"), 8)
            turn("tf0", hn, range(0, 4))
            turn("tf1", hn, range(4, 8))
            pe.wait_ge(S("hT_ready"), 8)
            for c in range(4):
                project(f"pq{c}", hT)
            pe.wait_ge(S("pq_read"), 8)
            pe.wait_ge(S("sub_here"), 16)
            for n in range(4):
                ps = aux_open(f"PS{n}")
                t = n // 2
                for j in range(8):
                    hc = 8 * (n % 2) + j
                    last = mm(ps[:, j * P:(j + 1) * P], qhT[:, hc, t * P:(t + 1) * P], subT[:, hc, :], True, True)
                last.then_inc(aux_full, 1)
            pe.wait_ge(S("rIJW_ready"), 6)
            ps = aux_open("TR")
            for a in range(3):
                for t in range(TT):
                    last = nc.tensor.transpose(ps[:, a * T + t * P:a * T + (t + 1) * P], rIJW[:, a, t, :], ident[:, :])
            last.then_inc(aux_full, 1)

            def spread(b, q):
                pe.wait_ge(onehots, q + 1)
                for j in range(4):
                    s = 4 * b + j
                    last = mm(gb_[b][:, j * P:(j + 1) * P], ohL[s], ohR[s], True, True)
                last.then_inc(spread_done, 1)
            spread(0, 0)
            spread(1, 1)
            with pe.Fori(1, T // 8) as r:
                for b in range(2):
                    pe.wait_ge(spread_out, 2 * r + b - 1)
                    spread(b, 2 * r + b)
            pe.wait_ge(S("IJW_ready"), 1)

            y = [[aux[t][:, 512 * c:512 * c + 512] for c in range(2)] for t in range(TT)]

            def acts(s, n, wait_group):
                if wait_group is not None:
                    pe.wait_ge(u_here[s // GROUP], wait_group)
                ps = gb_[2 + s % 2]
                for k in range(KD):
                    last = mm(ps[:, 0:T], uring[s][:, k, :], hT[:, k, :], k == 0, k == KD - 1)
                last.then_inc(u_done, 1)

            def outs(s, n, first, final, wait_group):
                if wait_group is not None:
                    pe.wait_ge(v_here[s // GROUP], wait_group)
                pe.wait_ge(coef_done, n + 1)
                for t in range(TT):
                    for c in range(2):
                        last = nc.tensor.matmul(y[t][c], coef[s % 2][:, t * P:(t + 1) * P], vring[s][:, 512 * c:512 * c + 512],
                                                start=first, stop=final, skip_group_check=True)
                last.then_inc(v_done, 1)

            def four(r, first, final):
                for s in range(NS):
                    n = NS * r + s
                    if not (final and s == NS - 1):
                        s1 = (s + 1) % NS
                        if not first or s >= 1:
                            pe.wait_ge(gelu_done, n)
                        grp = None if s1 % GROUP else 16 * r + (16 if s1 else 32)
                        acts(s1, n + 1, grp)
                    outs(s, n, first and s == 0, final and s == NS - 1, None if s % GROUP else 16 * r + 16)
            acts(0, 0, 16)
            four(0, True, False)
            with pe.Fori(1, NKEY // NS - 1) as r:
                four(r, False, False)
            four(NKEY // NS - 1, False, True)

        @block.scalar
        def _(act):
            def bank(name, b):
                g = bank_no[name] + b
                act.wait_ge(proj_full, g + 1)
                return gb_[g % NG], S(bank_reader[g][0])

            def copy_banks(names, dst, func=ACT.Copy, scale=1.0):
                for i, (n, b) in enumerate([(n, b) for n in names for b in range(2)]):
                    ps, read = bank(n, b)
                    nc.scalar.activation(dst(i), ps[:, :], func, scale=scale).then_inc(read, 1)

            def aux_take(name):
                act.wait_ge(aux_full, aux_no[name] + 1)
                return aux[aux_no[name] % 2]

            def aux_copy(name, dst, view=lambda p: p[:, :]):
                nc.scalar.activation(dst, view(aux_take(name)), ACT.Copy).then_inc(S(aux_uses[aux_no[name]][1]), 1)

            def flat(v):
                names = "abc"[:len(v.shape) - 1]
                return v.rearrange(f"p {' '.join(names)} -> p ({' '.join(names)})")

            def halves(v):
                return lambda i: flat(v)[:, 512 * i:512 * (i + 1)]

            def ssq(src, junk_, n):
                for t in range(TT):
                    nc.scalar.activation(junk_[:, t, :], src[:, t, :], ACT.Square,
                                         accum_out=stat[:, n, t:t + 1]).then_inc(S("ssq"), 1)

            def root(n, w, cnt):
                act.wait_ge(S("var"), cnt)
                nc.scalar.activation(stat[:, n, 8:8 + w], stat[:, n, 8:8 + w], ACT.Sqrt).then_inc(S("root"), 1)

            act.wait_ge(x_here, 16)
            ssq(x_sb, hn, 0)
            root(0, 2, 1)
            for n in range(4):
                aux_copy(f"bias{n}", bias_rows[:, 2 * n:2 * n + 2, :],
                         lambda p: p[:, :].rearrange("p (h c) -> p h c", h=2)[:, :, 0:ROW])
            act.wait_ge(mem_here, 16)
            act.wait_ge(aux_full, aux_no["tx1"] + 1)
            ssq(mem_sb, hn, 1)
            root(1, 2, 2)
            nc.scalar.preload_act_table_set("natural_log_exp_and_others")
            act.wait_ge(S("low_ready"), 1)
            nc.scalar.activation(tiny[:, 0:2, :], tiny[:, 0:2, :], ACT.Exp).then_inc(S("low_exp"), 1)
            copy_banks(["hf0"], halves(DI.rearrange("p (a b) -> p a b", a=HG_H)), ACT.Exp, -1.0)
            copy_banks(["hq0"], halves(hqT))
            act.wait_ge(S("k_ready"), 1)
            nc.scalar.activation(E_, E_, ACT.Ln).then_inc(S("lf_ready"), 1)
            copy_banks(["mq0"], halves(mqT))

            def decay(i):
                act.wait_ge(S("diff"), 2 * i + 2 if i < len(LEVELS) else 2 * i + 4)
                if i >= 1:
                    act.wait_ge(S("QK"), i)
                nc.scalar.activation(E_, DI, ACT.Exp).then_inc(S("decay"), 1)
            decay(0)
            copy_banks(["mk0"], halves(mkT))
            decay(1)
            act.wait_ge(S("mb_max"), 2)
            for t, s_ in ((0, S0), (1, S1)):
                for h in range(MB_H):
                    nc.scalar.activation(s_[:, h, :], s_[:, h, :], ACT.Exp, bias=smx[:, t, h:h + 1],
                                         accum_out=smx[:, 2 + t, h:h + 1]).then_inc(S("mb_exp"), 1)
            copy_banks(["hi0"], halves(hi_sb))
            decay(2)
            decay(3)
            for b in range(2):
                g = bank_no["hg0"] + b
                act.wait_ge(proj_full, g + 1)
                nc.scalar.activation(hgtmp[:, b, :], gb_[g % NG][:, :], ACT.Exp, scale=-1.0).then_inc(S("act_chain"), 1)
                nc.scalar.activation(hg_sb[:, b, :], gb_[g % NG][:, :], ACT.Copy).then_inc(S("hg_read"), 1)
            decay(4)
            decay(5)
            copy_banks(["mv0"], halves(mv_sb))
            decay(6)
            decay(7)
            aux_copy("L128", flat(AT01), lambda p: p[:, 0:HG_H * P])
            aux_copy("PTa", flat(PT0[:, 0:4, :]))
            aux_copy("PTb", flat(PT0[:, 4:8, :]))
            aux_copy("PTc", flat(PT1))
            copy_banks(["ga0"], halves(sgA[:, 0:4, :]), ACT.Exp, -1.0)
            aux_copy("PV", flat(ybT))
            act.wait_ge(S("silu_ready"), 1)
            copy_banks(["ga1"], halves(sgA[:, 4:8, :]), ACT.Exp, -1.0)
            aux_copy("O", osb.rearrange("p t h e -> p (t h e)"))
            copy_banks(["gb0", "gb1"], halves(sgB), ACT.Exp, -1.0)
            root(2, 8, 3)
            copy_banks(["kx0", "kx1"], halves(kxT))
            for c in range(2):
                for t in range(TT):
                    ps, read = bank(f"vx{c}", t)
                    nc.scalar.activation(vx[:, t, 512 * c:512 * (c + 1)], ps[:, :], ACT.Copy).then_inc(read, 1)
            act.wait_ge(aux_full, aux_no["tm1"] + 1)
            act.wait_ge(S("x_new"), 4)
            ssq(x_sb, hn, 3)
            root(3, 2, 4)
            copy_banks(["qx0", "qx1"], halves(qxT))
            for t in range(TT):
                act.wait_ge(S("x_max"), t + 1)
                ps = aux_take(f"CS{t}")
                for h in range(X_H):
                    nc.scalar.activation(CS[:, t, h, :], ps[:, h * T:(h + 1) * T], ACT.Exp, bias=smx[:, 4, 4 * t + h:4 * t + h + 1],
                                         scale=X_D ** -0.5, accum_out=smx[:, 5, 4 * t + h:4 * t + h + 1]).then_inc(S("xexp"), 1)
            for m in range(TT):
                aux_copy(f"CT{m}", flat(CPT[:, m]))
            for c in range(2):
                aux_copy(f"CV{c}", flat(oxT[:, 4 * c:4 * c + 4, :]))
            act.wait_ge(aux_full, aux_no["tc1"] + 1)
            act.wait_ge(S("x_new"), 8)
            ssq(x_sb, hn, 4)
            root(4, 2, 5)
            copy_banks([f"pq{c}" for c in range(4)], halves(qhT))
            for n in range(4):
                aux_copy(f"PS{n}", flat(sc[:, n // 2, 8 * (n % 2):8 * (n % 2) + 8, :]))
            for t in range(TT):
                act.wait_ge(S("w_diff"), t + 1)
                nc.scalar.activation(flat(fv[:, t]), flat(fv[:, t]), ACT.Exp).then_inc(S("w_exp"), 1)

            def spread_copy(b, q, t0):
                act.wait_ge(spread_done, q + 1)
                nc.scalar.activation(gate[:, :, t0], gb_[b][:, :].rearrange("p (t i) -> p i t", t=4), ACT.Copy).then_inc(spread_out, 1)
            with act.Fori(0, T // 8) as r:
                for b in range(2):
                    spread_copy(b, 2 * r + b, bass.ds(8 * r + 4 * b, 4))
            nc.scalar.preload_act_table(ACT.Gelu_apprx_tanh)

            def gelu(s, n, first):
                act.wait_ge(u_done, n + 1)
                if not first:
                    act.wait_ge(coef_done, n - 1)
                nc.scalar.activation(actr[s % 2], gb_[2 + s % 2][:, 0:T], ACT.Gelu_apprx_tanh).then_inc(gelu_done, 1)
            for s in range(NS):
                gelu(s, s, s < 2)
            with act.Fori(1, NKEY // NS) as r:
                for s in range(NS):
                    gelu(s, NS * r + s, False)
            act.wait_ge(S("x_new"), 12)
            ssq(x_sb, yfin, 5)
            root(5, 2, 6)

        @block.vector
        def _(dve):
            TTn, TS = nc.vector.tensor_tensor, nc.vector.tensor_scalar
            links = [0]

            def link(ins):
                links[0] += 1
                ins.then_inc(S("dve_chain"), 1)
                dve.wait_ge(S("dve_chain"), links[0])

            def flat(v):
                names = "abc"[:len(v.shape) - 1]
                return v.rearrange(f"p {' '.join(names)} -> p ({' '.join(names)})")

            def over(v, n):
                return v.unsqueeze(len(v.shape)).to_broadcast([*v.shape, n])

            def mean(n, w, scale, ssqs):
                dve.wait_ge(S("ssq"), ssqs)
                TS(stat[:, n, 8:8 + w], stat[:, n, 0:w], scale, EPS, ALU.mult, ALU.add).then_inc(S("var"), 1)

            def normed(src, n, roots):
                dve.wait_ge(S("root"), roots)
                link(nc.vector.reciprocal(stat[:, n, 8:10], stat[:, n, 8:10]))
                for t in range(TT):
                    TS(hn[:, t, :], src[:, t, :], stat[:, n, 8 + t:9 + t], None, ALU.mult).then_inc(S("hn_ready"), 1)

            def aux_take(name):
                dve.wait_ge(aux_full, aux_no[name] + 1)
                return aux[aux_no[name] % 2]

            def turned(names, gain, proj_before):
                if proj_before:
                    dve.wait_ge(proj_full, bank_end(proj_before))
                for i, n in enumerate(names):
                    ps = aux_take(n)
                    TTn(hT[:, 4 * i:4 * i + 4, :], ps[:, :].rearrange("p (k t) -> p k t", k=4),
                        over(gain_sb[:, gain, 4 * i:4 * i + 4], T), ALU.mult).then_inc(S("hT_ready"), 1)

            mean(0, 2, 1.0 / D, 2)
            dve.wait_ge(const_here, 16 * 7)
            nc.vector.tensor_copy(relbb[0:BUCKETS + 1, :, :], over(relb[:, :], P)).then_inc(S("relbb_ready"), 1)
            normed(x_sb, 0, 1)
            link(TTn(tiny[:, 2, :], low_sb[:, 0, :], low_sb[:, 1, :], ALU.max))
            TTn(tiny[:, 0, :], low_sb[:, 0, :], tiny[:, 2, :], ALU.subtract)
            TTn(tiny[:, 1, :], low_sb[:, 1, :], tiny[:, 2, :], ALU.subtract).then_inc(S("low_ready"), 1)
            turned(["tx0", "tx1"], 0, None)
            mean(1, 2, 1.0 / D, 4)
            dve.wait_ge(S("low_exp"), 1)
            link(TTn(tiny[:, 2, :], tiny[:, 0, :], tiny[:, 1, :], ALU.add))
            link(nc.vector.reciprocal(tiny[:, 3, :], tiny[:, 2, :]))
            TTn(lb[:, 0, :], tiny[:, 0, :], tiny[:, 3, :], ALU.mult)
            link(TTn(lb[:, 1, :], tiny[:, 1, :], tiny[:, 3, :], ALU.mult))
            dve.wait_ge(S("hf_read"), 2)
            link(TS(DI, DI, 1.0, None, ALU.add))
            link(nc.vector.reciprocal(DI, DI))
            for h in range(HG_H):
                last = TS(E_[:, h * T:(h + 1) * T], DI[:, h * T:(h + 1) * T], lb[:, 1, h:h + 1], lb[:, 0, h:h + 1], ALU.mult, ALU.add)
            link(last)
            TS(flat(kT), E_, -1.0, 1.0, ALU.mult, ALU.add).then_inc(S("k_ready"), 1)
            dve.wait_ge(S("lf_ready"), 1)
            dve.wait_ge(S("restart_ready"), 1)
            nc.vector.tensor_tensor_scan(bsum, restart, E_, 0.0, ALU.mult, ALU.add).then_inc(S("b_ready"), 1)
            dve.wait_ge(S("b_ready"), 1)

            def level_diff(i):
                if i >= 1:
                    dve.wait_ge(S("decay"), i)
                if i < len(LEVELS):
                    L = LEVELS[i]
                    b = bsum.rearrange("p (n a l) -> p n a l", a=2, l=L)
                    d = DI.rearrange("p (n a l) -> p n a l", a=2, l=L)
                    mid = b[:, :, 0, L - 1:L].to_broadcast([P, T * HG_H // (2 * L), L])
                    if L < CHUNK:
                        TTn(d[:, :, 1, :], b[:, :, 1, :], mid, ALU.subtract).then_inc(S("diff"), 1)
                    else:
                        nc.vector.tensor_copy(d[:, :, 1, :], b[:, :, 1, :]).then_inc(S("diff"), 1)
                    TTn(d[:, :, 0, :], mid, b[:, :, 0, :], ALU.subtract).then_inc(S("diff"), 1)
                else:
                    b = bsum.rearrange("p (h n l) -> p h n l", n=4, l=CHUNK)
                    d = DI.rearrange("p (h n l) -> p h n l", n=4, l=CHUNK)
                    end = [b[:, :, c, CHUNK - 1:CHUNK].to_broadcast([P, HG_H, CHUNK]) for c in range(4)]
                    nc.vector.tensor_copy(d[:, :, 2, :], b[:, :, 2, :]).then_inc(S("diff"), 1)
                    TTn(d[:, :, 3, :], b[:, :, 3, :], end[2], ALU.add).then_inc(S("diff"), 1)
                    TTn(d[:, :, 1, :], end[1], b[:, :, 1, :], ALU.subtract).then_inc(S("diff"), 1)
                    TTn(d[:, :, 0, :], end[0], b[:, :, 0, :], ALU.subtract).then_inc(S("dve_chain"), 1)
                    links[0] += 1
                    dve.wait_ge(S("dve_chain"), links[0])
                    TTn(d[:, :, 0, :], d[:, :, 0, :], end[1], ALU.add).then_inc(S("diff"), 1)

            def level_qk(i):
                dve.wait_ge(S("decay"), i + 1)
                if i == 0:
                    dve.wait_ge(S("cleared"), 5)
                    dve.wait_ge(S("hq_read"), 2)
                if i >= 2:
                    L = (LEVELS + [128])[i - 2]
                    dve.wait_ge(aux_full, aux_no[f"L{L}"] + 1)
                L = (LEVELS + [128])[i]
                half = lambda v, a: v.rearrange("p (n a l) -> p n a l", a=2, l=L)[:, :, a, :]
                TTn(half(flat(QE[i % 2]), 1), half(flat(hqT), 1), half(E_, 1), ALU.mult)
                TTn(half(flat(KE[i % 2]), 0), half(flat(kT), 0), half(E_, 0), ALU.mult).then_inc(S("QK"), 1)

            def level_take(name):
                ps = aux_take(f"L{name}")
                m = ident[:, :] if name == "diag" else mask_sb[:, LEVELS.index(name), :]
                m = m.bitcast(u32).unsqueeze(1).to_broadcast([P, HG_H * TT, P])
                nc.vector.copy_predicated(ATd, m, ps[:, :].rearrange("p (b t) -> p b t", b=HG_H * TT)).then_inc(S("level_read"), 1)
                dve.wait_ge(S("level_read"), ([*["diag"], *LEVELS]).index(name) + 1)

            level_diff(0)
            level_qk(0)
            dve.wait_ge(masks_here, 16)
            level_take("diag")
            level_diff(1)
            level_qk(1)
            level_take(1)
            dve.wait_ge(S("bias_here"), 16)
            for name, s_, bb in (("S0", S0, biasB[:, :, P:T]), ("S1a", S1[:, 0:4, :], biasB[:, 0:4, :]), ("S1b", S1[:, 4:8, :], biasB[:, 4:8, :])):
                ps = aux_take(name)
                for odd in range(2):
                    nc.vector.scalar_tensor_tensor(
                        out=s_[:, odd::2, :], in0=ps[:, 512 * odd:512 * odd + 512].rearrange("p (h k) -> p h k", k=s_.shape[2]),
                        scalar=MB_D ** -0.5, in1=bb[:, odd::2, :], op0=ALU.mult, op1=ALU.add).then_inc(S("biased"), 1)
            dve.wait_ge(S("biased"), 6)
            for t, s_ in ((0, S0), (1, S1)):
                nc.vector.tensor_reduce(smx[:, t, 0:MB_H], s_, AX.X, ALU.max, negate=True).then_inc(S("mb_max"), 1)
            for i, before in ((2, 2), (3, 4), (4, 8)):
                level_diff(i)
                level_qk(i)
                level_take(before)
            dve.wait_ge(S("hg_read"), 2)
            link(TS(flat(hgtmp), flat(hgtmp), 1.0, None, ALU.add))
            link(nc.vector.reciprocal(flat(hgtmp), flat(hgtmp)))
            TTn(flat(hg_sb), flat(hg_sb), flat(hgtmp), ALU.mult).then_inc(S("silu_ready"), 1)
            for i, before in ((5, 16), (6, 32), (7, 64)):
                level_diff(i)
                level_qk(i)
                level_take(before)
            dve.wait_ge(S("mb_exp"), 16)
            link(nc.vector.reciprocal(smx[:, 2:4, 0:MB_H], smx[:, 2:4, 0:MB_H]))
            TTn(S0, S0, over(smx[:, 2, 0:MB_H], P), ALU.mult).then_inc(S("mb_prob"), 1)
            TTn(S1, S1, over(smx[:, 3, 0:MB_H], T), ALU.mult).then_inc(S("mb_prob"), 1)
            normed(mem_sb, 1, 2)

            def sigmoid(v, fam, i):
                dve.wait_ge(S(f"{fam}_read"), 2 * i + 2)
                v = flat(v[:, 4 * i:4 * i + 4, :])
                link(TS(v, v, 1.0, None, ALU.add))
                nc.vector.reciprocal(v, v).then_inc(S("sig_ready"), 1)
            sigmoid(sgA, "ga", 0)
            sigmoid(sgA, "ga", 1)
            dve.wait_ge(S("o_read"), 1)
            link(TTn(osq, osb, osb, ALU.mult))
            nc.vector.tensor_reduce(stat[:, 2, 0:8], osq.rearrange("p t h e -> p (t h) e"), AX.X, ALU.add).then_inc(S("ssq"), 1)
            mean(2, 8, 1.0 / HG_D, 5)
            sigmoid(sgB, "gb", 0)
            sigmoid(sgB, "gb", 1)
            turned(["tm0", "tm1"], 3, "gb1")
            dve.wait_ge(S("root"), 3)
            link(nc.vector.reciprocal(stat[:, 2, 8:16], stat[:, 2, 8:16]))
            o3 = osb.rearrange("p t h e -> p (t h) e")
            dve.wait_ge(S("silu_ready"), 1)
            link(TTn(o3, o3, over(stat[:, 2, 8:16], HG_D), ALU.mult))
            of = osb.rearrange("p t h e -> p (t h e)")
            TTn(of, of, flat(hg_sb), ALU.mult).then_inc(S("o_ready"), 1)
            TTn(yaT, aux_take("TY")[:, :].rearrange("p (h t) -> p h t", h=HG_H), over(hgn_sb[:, :], T), ALU.mult).then_inc(S("yaT_ready"), 1)
            dve.wait_ge(S("sig_ready"), 4)
            for b in range(4):
                g = bank_no["upa0"] + b
                dve.wait_ge(proj_full, g + 1)
                TTn(flat(sgA[:, 2 * b:2 * b + 2, :]), flat(sgA[:, 2 * b:2 * b + 2, :]), gb_[g % NG][:, :], ALU.mult).then_inc(S("upa_read"), 1)
            for b in range(4):
                g = bank_no["upb0"] + b
                dve.wait_ge(proj_full, g + 1)
                TTn(flat(sgB[:, 2 * b:2 * b + 2, :]), flat(sgB[:, 2 * b:2 * b + 2, :]), gb_[g % NG][:, :], ALU.mult).then_inc(S("upb_read"), 1)
                dve.wait_ge(S("upb_read"), b + 1)
                TTn(flat(zT[:, 2 * b:2 * b + 2, :]), flat(sgA[:, 2 * b:2 * b + 2, :]), flat(sgB[:, 2 * b:2 * b + 2, :]), ALU.add).then_inc(S("z_ready"), 1)

            def add_to_x(fam):
                for c in range(2):
                    for t in range(TT):
                        g = bank_no[f"{fam}{c}"] + t
                        dve.wait_ge(proj_full, g + 1)
                        xs = x_sb[:, t, 512 * c:512 * (c + 1)]
                        TTn(xs, xs, gb_[g % NG][:, :], ALU.add).then_inc(S(bank_reader[g][0]), 1)
                dve.wait_ge(S(f"{fam}_read"), 4)
                nc.vector.engine_nop().then_inc(S("x_new"), 4)
            add_to_x("out")
            mean(3, 2, 1.0 / D, 7)
            normed(x_sb, 3, 4)
            turned(["tc0", "tc1"], 1, "vx1")
            for t in range(TT):
                ps = aux_take(f"CS{t}")
                m = smx[:, 4, 4 * t:4 * t + 4]
                link(nc.vector.tensor_reduce(m, ps[:, :].rearrange("p (h m) -> p h m", h=X_H), AX.X, ALU.max, negate=True))
                TS(m, m, X_D ** -0.5, None, ALU.mult).then_inc(S("x_max"), 1)
            for t in range(TT):
                dve.wait_ge(S("xexp"), 4 * t + 4)
                r_ = smx[:, 5, 4 * t:4 * t + 4]
                link(nc.vector.reciprocal(r_, r_))
                TTn(CS[:, t], CS[:, t], over(r_, T), ALU.mult).then_inc(S("x_prob"), 1)
            add_to_x("wo")
            mean(4, 2, 1.0 / D, 9)
            normed(x_sb, 4, 5)
            turned(["tf0", "tf1"], 2, "qx1")

            def top16(rows, src, spare, vals, idx):
                for r in rows:
                    last = nc.vector.max(vals(r)[:, 0:8], src(r))
                link(last)
                for r in rows:
                    nc.vector.max_index(idx(r)[:, 0:8], vals(r)[:, 0:8], src(r))
                    last = nc.vector.match_replace(spare(r), vals(r)[:, 0:8], src(r), LOWEST)
                link(last)
                for r in rows:
                    last = nc.vector.max(vals(r)[:, 8:16], spare(r))
                link(last)
                for r in rows:
                    last = nc.vector.max_index(idx(r)[:, 8:16], vals(r)[:, 8:16], spare(r))
                link(last)

            dve.wait_ge(proj_full, bank_end("pq3"))
            for t in range(TT):
                dve.wait_ge(S("sc_read"), 2 * t + 2)
                top16(range(2 * PH), lambda r: sc[:, t, r, :], lambda r: sc2[:, t, r, :],
                      lambda r: sv[:, t, r, :], lambda r: si[:, t, r, :].bitcast(u32))
                link(nc.vector.tensor_copy(flat(sif[:, t]), flat(si[:, t]).bitcast(u32)))
                s4 = sv[:, t].rearrange("p (h c) k -> p h c k", c=2)
                i4 = sif[:, t].rearrange("p (h c) k -> p h c k", c=2)
                link(TTn(cand.rearrange("p h (a b) -> p h a b", a=PK), over(s4[:, :, 0, :], PK),
                         s4[:, :, 1, :].unsqueeze(2).to_broadcast([P, PH, PK, PK]), ALU.add))
                top16(range(PH), lambda r: cand[:, r, :], lambda r: cand2[:, r, :],
                      lambda r: fv[:, t, r, :], lambda r: pos[:, t, r, :].bitcast(u32))
                m = fv[:, t, :, 0:1]
                nc.vector.tensor_copy(wsum[:, t, :], m.rearrange("p h o -> p (h o)")).then_inc(S("dve_chain"), 1)
                pf = flat(pos[:, t]).bitcast(u32)
                TS(ab[:, 0, :].bitcast(u32), pf, 4, None, ALU.logical_shift_right).then_inc(S("dve_chain"), 1)
                TS(ab[:, 1, :].bitcast(u32), pf, PK - 1, None, ALU.bitwise_and).then_inc(S("dve_chain"), 1)
                links[0] += 3
                dve.wait_ge(S("dve_chain"), links[0])
                TTn(fv[:, t], fv[:, t], over(wsum[:, t, :], PK), ALU.subtract).then_inc(S("w_diff"), 1)
                link(nc.vector.tensor_copy(flat(abf), flat(ab).bitcast(u32)))
                for c in range(2):
                    link(TTn(eq, over(abf[:, c, :], PK), iota_sb[:, 0:PK].unsqueeze(1).to_broadcast([P, PH * PK, PK]), ALU.is_equal))
                    link(TTn(eq2.rearrange("p (h k) a -> p h k a", h=PH), eq.rearrange("p (h k) a -> p h k a", h=PH),
                             i4[:, :, c, :].unsqueeze(2).to_broadcast([P, PH, PK, PK]), ALU.mult))
                    nc.vector.tensor_reduce(rIJW[:, c, t, :], eq2, AX.X, ALU.add).then_inc(S("rIJW_ready"), 1)
                dve.wait_ge(S("w_exp"), t + 1)
                link(nc.vector.tensor_reduce(wsum[:, t, :], fv[:, t], AX.X, ALU.add))
                link(nc.vector.reciprocal(wsum[:, t, :], wsum[:, t, :]))
                TTn(rIJW[:, 2, t, :].rearrange("p (h k) -> p h k", h=PH), fv[:, t], over(wsum[:, t, :], PK), ALU.mult).then_inc(S("rIJW_ready"), 1)
            nc.vector.tensor_copy(flat(IJW), aux_take("TR")[:, 0:3 * T]).then_inc(S("IJW_ready"), 1)
            dve.wait_ge(S("IJW_ready"), 1)

            def rows(b, q, tok):
                for j in range(4):
                    s = 4 * b + j
                    TS(ohR[s], iota_sb[:, :], IJW[:, 0, tok(j)], None, ALU.is_equal)
                    last = TS(ohL[s], iota_sb[:, :], IJW[:, 1, tok(j)], IJW[:, 2, tok(j)], ALU.is_equal, ALU.mult)
                last.then_inc(onehots, 1)
            for b in range(2):
                rows(b, b, lambda j: slice(4 * b + j, 4 * b + j + 1))
            with dve.Fori(1, T // 8) as r:
                for b in range(2):
                    dve.wait_ge(spread_done, 2 * r + b - 1)
                    rows(b, 2 * r + b, lambda j: bass.ds(8 * r + 4 * b + j, 1))

            dve.wait_ge(spread_out, T // 4)

            def weigh(s, n, i, first):
                dve.wait_ge(gelu_done, n + 1)
                if not first:
                    dve.wait_ge(v_done, n - 1)
                TTn(coef[s % 2], actr[s % 2], gate[:, i, :], ALU.mult).then_inc(coef_done, 1)
            for s in range(NS):
                weigh(s, s, s, s < 2)
            with dve.Fori(1, NKEY // NS) as r:
                for s in range(NS):
                    n = NS * r + s
                    dve.wait_ge(gelu_done, n + 1)
                    dve.wait_ge(v_done, n - 1)
                    TTn(coef[s % 2].unsqueeze(1), actr[s % 2].unsqueeze(1), gate[:, bass.ds(n, 1), :], ALU.mult).then_inc(coef_done, 1)
            dve.wait_ge(v_done, NKEY)
            for t in range(TT):
                for c in range(2):
                    xs = x_sb[:, t, 512 * c:512 * (c + 1)]
                    TTn(xs, xs, aux[t][:, 512 * c:512 * (c + 1)], ALU.add).then_inc(S("x_new"), 1)
            mean(5, 2, 1.0 / D, 11)
            dve.wait_ge(S("root"), 6)
            link(nc.vector.reciprocal(stat[:, 5, 8:10], stat[:, 5, 8:10]))
            dve.wait_ge(S("fgain_here"), 16)
            for t in range(TT):
                nc.vector.scalar_tensor_tensor(out=yfin[:, t, :], in0=x_sb[:, t, :], scalar=stat[:, 5, 8 + t:9 + t],
                                               in1=fgain, op0=ALU.mult, op1=ALU.mult).then_inc(S("y_ready"), 1)


def level_masks():
    s, t = np.arange(P)[:, None], np.arange(P)[None, :]
    rows = [(s // (2 * L) == t // (2 * L)) & (s // L % 2 == 0) & (t // L % 2 == 1) for L in LEVELS]
    return np.stack(rows + [s == t]).astype(np.float32)


def bucket_onehot():
    import math
    dist = 255 - np.arange(ROW)
    exact = BUCKETS // 2
    d = np.maximum(dist, 1).astype(np.float32)
    scaled = np.log(d / np.float32(exact)) / np.float32(math.log(MAX_DIST / exact))
    large = np.minimum(exact + (scaled * np.float32(BUCKETS - exact)).astype(np.int32), BUCKETS - 1)
    b = np.where(dist < exact, dist, large)
    b = np.where(dist < 0, BUCKETS, b)
    return (np.arange(BUCKETS + 1)[:, None] == b[None, :]).astype(np.float32)


def kernel(**inputs):
    import concourse.bacc as bacc
    from concourse.bass_utils import run_bass_kernel_spmd

    a = {k: np.asarray(v) for k, v in inputs.items()}

    def chunked(w):
        k, n = w.shape
        c = 512 if k == D else n
        return np.ascontiguousarray(w.reshape(k // P, P, n // c, c).transpose(2, 1, 0, 3)).reshape(n // c, P, WSLOT)

    def columns(v):
        return v.reshape(-1, P).T

    arrays = {
        "x": a["x"][0], "mem": a["mem"][0], "rel_bias": a["rel_bias"],
        "w_in": chunked(a["w_in"][0]), "w_up_a": chunked(a["w_up_a"][0]), "w_up_b": chunked(a["w_up_b"][0]),
        "w_out": chunked(a["w_out"][0]), "wq_x": chunked(a["wq_x"][0]), "wk_x": chunked(a["wk_x"][0]),
        "wv_x": chunked(a["wv_x"][0]), "wo_x": chunked(a["wo_x"][0]), "peer_query": chunked(a["peer_query"][0]),
        "subkeys": a["peer_subkeys"][0].reshape(2 * PH, NKEY, P).transpose(2, 0, 1),
        "peer_u": a["peer_u"][0].reshape(NEXP // P // GROUP, GROUP, P, KD, P).transpose(0, 4, 1, 3, 2).reshape(-1, P, GROUP * D),
        "peer_v": a["peer_v"][0].reshape(NEXP // P // GROUP, GROUP * P, D),
        "gains": np.stack([columns(a[k][0]) for k in ("ln_mix", "ln_cross", "ln_ffn", "ln_mem")], axis=1),
        "hg_lower": np.stack([columns(a["hg_lower"][i]) for i in range(2)], axis=1),
        "hg_norm": columns(a["hg_norm"][0]),
        "ln_final": a["ln_final"],
        "onehot": bucket_onehot(), "masks": level_masks(),
        "iota": np.tile(np.arange(NKEY, dtype=np.float32), (P, 1)),
    }
    nc = bacc.Bacc("TRN2", target_bir_lowering=False, num_devices=1)
    arrays = {k: np.ascontiguousarray(v) for k, v in arrays.items()}
    args = {k: nc.dram_tensor(f"in_{k}", v.shape, mybir.dt.from_np(v.dtype), kind="ExternalInput").ap() for k, v in arrays.items()}
    out = nc.dram_tensor("out", (T, D), mybir.dt.float32, kind="ExternalOutput").ap()
    hybrid_layer(nc, **args, out=out)
    got = run_bass_kernel_spmd(nc, [{f"in_{k}": v for k, v in arrays.items()}], core_ids=[0])
    return got.results[0]["out"].reshape(1, T, D)
```

```python
import numpy as np
import concourse.bass as bass
from concourse import mybir
from contextlib import ExitStack

D = 1024
T = 256
P = 128
KD = D // P
TT = T // P
HG_H, HG_D = 4, 128
CHUNK = 64
MB_H, MB_D = 8, 64
X_H, X_D = 4, 256
PH, PK = 8, 16
NKEY = 128
NEXP = NKEY * NKEY
EPS = 1e-6
BUCKETS, MAX_DIST = 32, 2048
ROW = 384
NEG = -1e30
LOWEST = -3e38
LEVELS = [1, 2, 4, 8, 16, 32, 64]
WSLOT = 4096
NW = 3
NG = 4
NT = NKEY
HALF = D // 2
EARLY = 36
EARLY_A = 20
TOK = 4
ROWS = 4


def hybrid_layer(nc, x, mem, rel_bias, w_in, w_up_a, w_up_b, w_out, wq_x, wk_x, wv_x, wo_x,
                 peer_query, subkeys, peer_u, peer_v, gains, hg_lower, hg_norm, ln_final,
                 onehot, masks, iota, out):
    f32, u32 = mybir.dt.float32, mybir.dt.uint32
    ALU, ACT, AX = mybir.AluOpType, mybir.ActivationFunctionType, mybir.AxisListType

    chunks = []
    for name, src, c0, n, form in [
            ("hf", w_in, 1, 1, "T"), ("hq", w_in, 0, 1, "T"), ("mq", w_in, 4, 1, "T"), ("mk", w_in, 5, 1, "T"),
            ("hi", w_in, 2, 1, "N"), ("hg", w_in, 3, 1, "N"), ("mv", w_in, 6, 1, "N"),
            ("ga", w_in, 7, 2, "T"), ("gb", w_in, 9, 2, "T"),
            ("kx", wk_x, 0, 1, "T"), ("upa", w_up_a, 0, 1, "U"), ("upb", w_up_b, 0, 1, "U"), ("kx", wk_x, 1, 1, "T"),
            ("out", w_out, 0, 2, "N"), ("vx", wv_x, 0, 1, "N"), ("qx", wq_x, 0, 2, "T"), ("vx", wv_x, 1, 1, "N"),
            ("wo", wo_x, 0, 2, "N"), ("pq", peer_query, 0, 4, "T")]:
        for c in range(n):
            chunks.append((f"{name}{c0 + c if name in ('kx', 'vx') else c}", src[c0 + c], form))
    chunk_no = {c[0]: n for n, c in enumerate(chunks)}
    banks_of = {"T": 2, "N": 2, "U": 4}
    bank_no, bank_reader, seen = {}, [], {}
    for name, _, form in chunks:
        bank_no[name] = len(bank_reader)
        for _ in range(banks_of[form]):
            fam = name[:-1]
            seen[fam] = seen.get(fam, 0) + 1
            bank_reader.append((f"{fam}_read", seen[fam]))
    aux_uses = [("bias0", "bias_read", 1), ("bias1", "bias_read", 2), ("bias2", "bias_read", 3), ("bias3", "bias_read", 4),
                ("tx0", "hT_ready", 1), ("tx1", "hT_ready", 2), ("Ldiag", "level_read", 1), ("L1", "level_read", 2),
                ("S0", "biased", 2), ("S1a", "biased", 4), ("S1b", "biased", 6),
                ("L2", "level_read", 3), ("L4", "level_read", 4), ("L8", "level_read", 5), ("L16", "level_read", 6),
                ("L32", "level_read", 7), ("PTa", "PT_read", 1), ("PTb", "PT_read", 2), ("PTc", "PT_read", 3),
                ("L64", "level_read", 8), ("L128", "far_read", 1), ("PV", "ybT_ready", 1),
                ("O", "o_read", 1), ("tm0", "hT_ready", 3), ("tm1", "hT_ready", 4), ("TY", "yaT_ready", 1),
                ("tc0", "hT_ready", 5), ("tc1", "hT_ready", 6), ("CS0", "xexp", 4), ("CS1", "xexp", 8),
                ("CT0", "CPT_read", 1), ("CT1", "CPT_read", 2), ("CV0", "oxT_ready", 1), ("CV1", "oxT_ready", 2),
                ("tf0", "hT_ready", 7), ("tf1", "hT_ready", 8),
                ("PS0", "sc_read", 1), ("PS1", "sc_read", 2), ("PS2", "sc_read", 3), ("PS3", "sc_read", 4),
                ("TR", "IJW_ready", 1)]
    aux_no = {n: i for i, (n, _, _) in enumerate(aux_uses)}

    ctx = ExitStack()
    with ctx:
        def sb(name, shape, dt=f32):
            return ctx.enter_context(nc.sbuf_tensor(name, shape, dt))

        def sem(name):
            return ctx.enter_context(nc.semaphore(name))

        ident = sb("ident", [P, P])
        gain_sb = sb("gain_sb", [P, 4, KD])
        hgn_sb = sb("hgn_sb", [P, HG_H])
        low_sb = sb("low_sb", [P, 2, HG_H])
        lb = sb("lb", [P, 2, HG_H])
        tiny = sb("tiny", [P, 4, HG_H])
        stat = sb("stat", [P, 6, 16])
        smx = sb("smx", [P, 6, 16])
        relb = sb("relb", [BUCKETS + 1, MB_H])
        onehot_sb = sb("onehot_sb", [BUCKETS + 1, ROW])
        iota_sb = sb("iota_sb", [P, NKEY])
        LOW, SIZE = 38144, 51456
        with nc.sbuf_tensor("arena", [P, SIZE], f32) as arena:
            pass
        sb("arena_low", [P, LOW])
        f32r = mybir.dt.float32r
        hTs = sb("hTs", [P, 2, KD, T], f32r)
        Us = sb("Us", [P, 4, 2, HALF], f32r)
        Cs = sb("Cs", [P, 2, 2, T], f32r)
        Vs = sb("Vs", [P, 4, 2, HALF], f32r)

        def at_(off, *dims):
            n = int(np.prod(dims))
            v = arena[:, off:off + n]
            if len(dims) == 1:
                return v
            names = "abcd"[:len(dims)]
            return v.rearrange(f"p ({' '.join(names)}) -> p {' '.join(names)}", **dict(zip(names, dims)))

        wring = [at_(s * WSLOT, WSLOT) for s in range(NW)]
        kxT = at_(12288, KD, T)
        vx = at_(14336, TT, D)
        x_sb = at_(34816, TT, D)
        hT = at_(49408, KD, T)
        o = 16384

        def take(*dims):
            nonlocal o
            if o < 36864 and o + int(np.prod(dims)) > 34816:
                o = 36864
            v = at_(o, *dims)
            o += int(np.prod(dims))
            return v
        hqT = take(HG_H, T)
        kT = take(HG_H, T)
        bsum = take(HG_H * T)
        E_ = take(HG_H * T)
        DI = take(HG_H * T)
        assert o + 4 * HG_H * T <= 34816
        sgB = at_(o, KD, T)
        QE = [take(HG_H, T) for _ in range(2)]
        AT01 = at_(o, HG_H, P)
        yaT = at_(o, HG_H, T)
        KE = [take(HG_H, T) for _ in range(2)]
        ATd = take(HG_H * TT, P)
        hi_sb = take(TT, HG_H * HG_D)
        hg_sb = take(TT, HG_H * HG_D)
        mask_sb = take(len(LEVELS), P)
        mqT = take(MB_H // 2, T)
        mkT = take(MB_H // 2, T)
        mv_sb = take(TT, MB_H * MB_D)
        S0 = take(MB_H, P)
        ybT = take(MB_H // 2, T)
        bias_rows = take(MB_H, ROW)
        biasB = take(MB_H, T)
        S1 = take(MB_H, T)
        sgA = take(KD, T)
        zT = take(KD, T)
        assert o <= 49408, o
        hn = S1.rearrange("p a b -> p (a b)").rearrange("p (t d) -> p t d", t=TT)
        PT = bias_rows
        PT0 = bias_rows.rearrange("p a b -> p (a b)")[:, 0:2048].rearrange("p (h q) -> p h q", h=MB_H)
        PT1 = bias_rows.rearrange("p a b -> p (a b)")[:, 2048:3072].rearrange("p (h q) -> p h q", h=MB_H)
        relbb = ybT.rearrange("p a b -> p (a b)").rearrange("p (h q) -> p h q", h=MB_H)
        hgtmp = sgA.rearrange("p a b -> p (a b)")[:, HG_H * T:].rearrange("p (t q) -> p t q", t=TT)
        restart = sgA.rearrange("p a b -> p (a b)")[:, 0:HG_H * T]
        mem_sb = zT.rearrange("p a b -> p (a b)").rearrange("p (t d) -> p t d", t=TT)
        memT = at_(16384, KD, T)
        osb = E_.rearrange("p (t h e) -> p t h e", t=TT, h=HG_H)
        osq = DI.rearrange("p (t h e) -> p t h e", t=TT, h=HG_H)
        qxT = at_(18432, KD, T)
        CS = at_(20480, TT, X_H, T)
        CPT = at_(22528, TT, X_H, T)
        oxT = at_(24576, KD, T)
        qhT = at_(16384, 2 * PH, T)
        subT = at_(20480, 2 * PH, NKEY)
        sc = at_(22528, TT, 2 * PH, NKEY)
        gate = at_(0, NT, T)
        uraw = [at_(32768 + D * s, D) for s in range(2)]
        vraw = [at_(34816 + D * s, D) for s in range(2)]
        actr = [at_(36864 + T * s, T) for s in range(2)]
        IJW = at_(37376, 3, T)
        apart = at_(36864, TOK, NKEY)
        rows_ = [at_(47360 + 1024 * s, 2, TOK, NKEY) for s in range(ROWS)]
        fgain = at_(32768, D)
        yfin = at_(0, TT, D)
        assert EARLY * T <= 9216
        sc2 = at_(26624, TT, 2 * PH, NKEY)
        cand = at_(9216, PH, PK * PK)
        cand2 = at_(11264, PH, PK * PK)
        eq = at_(13312, PH * PK, PK)
        eq2 = at_(15360, PH * PK, PK)
        at_small = 17408
        sv = at_(at_small, TT, 2 * PH, PK)
        si = at_(at_small + 512, TT, 2 * PH, PK)
        sif = at_(at_small + 1024, TT, 2 * PH, PK)
        fv = at_(at_small + 1536, TT, PH, PK)
        pos = at_(at_small + 1792, TT, PH, PK)
        ab = at_(at_small + 2048, 2, PH * PK)
        abf = at_(at_small + 2304, 2, PH * PK)
        rIJW = at_(at_small + 2560, 3, TT, P)
        wsum = at_(at_small + 3328, TT, PH)

        bias_d = nc.dram_tensor("bias_rows_dram", (MB_H, P, ROW), f32, kind="Internal")

        gb_ = [ctx.enter_context(nc.psum_tensor(f"proj{i}", [P, 512], f32)) for i in range(NG)]
        aux = [ctx.enter_context(nc.psum_tensor(f"aux{i}", [P, 1024], f32)) for i in range(2)]

        sems = {}

        def S(name):
            if name not in sems:
                sems[name] = ctx.enter_context(nc.semaphore(name))
            return sems[name]

        w_here = [S(f"w_here{s}") for s in range(NW)]
        u_here = [S(f"u_here{s}") for s in range(4)]
        v_here = [S(f"v_here{s}") for s in range(4)]
        x_here, mem_here, const_here, masks_here = S("x_here"), S("mem_here"), S("const_here"), S("masks_here")
        proj_full, aux_full = S("proj_full"), S("aux_full")
        u_high, u_low, u_used = S("u_high"), S("u_low"), S("u_used")
        v_high, v_low, v_used = S("v_high"), S("v_low"), S("v_used")
        gelu_done, product, coef_done = S("gelu_done"), S("product"), S("coef_done")
        h_high, h_low, injected, weighted, early_gated = map(S, ["h_high", "h_low", "injected", "weighted", "early_gated"])
        onehots, spread_done, spread_out = S("onehots_ready"), S("spread_done"), S("spread_out")
        for _, r, _ in aux_uses:
            S(r)
        for r, _ in bank_reader:
            S(r)
        for n in ["bias_rows_out", "bias_here", "sub_here", "fgain_here", "out_done", "cleared", "restart_ones",
                  "restart_ready", "neg_ready", "relbb_ready", "ssq", "var", "root", "hn_ready",
                  "low_ready", "low_exp", "k_ready", "lf_ready", "b_ready", "diff", "decay", "QK",
                  "mb_max", "mb_exp", "mb_prob", "silu_ready", "sig_ready", "z_ready", "x_new",
                  "o_ready", "x_max", "x_prob", "w_diff", "w_exp", "rIJW_ready", "y_ready",
                  "dve_chain", "act_chain", "coef_high", "apart_ready", "first_ready"]:
            S(n)
        block = ctx.enter_context(nc.Block())

        def bank_end(name):
            n = chunk_no[name]
            return bank_no[name] + banks_of[chunks[n][2]]

        @block.sync
        def _(sp):
            sp.dma_start(x_sb[:, :, :], x.rearrange("(t p) d -> p t d", p=P)).then_inc(x_here, 16)
            sp.wait_ge(S("neg_ready"), 1)
            sp.dma_start(relb[0:BUCKETS, :], rel_bias).then_inc(const_here, 16)
            sp.dma_start(onehot_sb[:, :], onehot).then_inc(const_here, 16)
            sp.dma_start(ident[:, :], masks[len(LEVELS)]).then_inc(const_here, 16)
            sp.dma_start(gain_sb[:, :, :], gains).then_inc(const_here, 16)
            sp.dma_start(hgn_sb[:, :], hg_norm).then_inc(const_here, 16)
            sp.dma_start(low_sb[:, :, :], hg_lower).then_inc(const_here, 16)
            sp.dma_start(iota_sb[:, :], iota).then_inc(const_here, 16)

            def load_w(n):
                if n >= NW:
                    sp.wait_ge(proj_full, bank_end(chunks[n - NW][0]))
                sp.dma_start(wring[n % NW], chunks[n][1]).then_inc(w_here[n % NW], 16)
            for n in range(NW):
                load_w(n)
            sp.dma_start(mem_sb, mem.rearrange("(t p) d -> p t d", p=P)).then_inc(mem_here, 16)
            sp.dma_start(mask_sb, masks[0:len(LEVELS)].rearrange("l s t -> s l t")).then_inc(masks_here, 16)
            sp.wait_ge(S("bias_read"), 4)
            sp.dma_start(bias_d.ap().rearrange("h p r -> p h r"), bias_rows).then_inc(S("bias_rows_out"), 16)
            sp.wait_ge(S("bias_rows_out"), 16)
            skew = bass.AP(tensor=bias_d, offset=P - 1, ap=[[ROW - 1, P], [P * ROW, MB_H], [1, T]])
            sp.dma_start(biasB, skew).then_inc(S("bias_here"), 16)
            for n in range(NW, len(chunks)):
                load_w(n)
            sp.wait_ge(aux_full, aux_no["CV1"] + 1)
            sp.dma_start(subT, subkeys).then_inc(S("sub_here"), 16)

            def load_u(n, s, c):
                h = slice(HALF * c, HALF * (c + 1))
                sp.dma_start(uraw[s][:, h], peer_u[n].rearrange("o p c -> (o p) c")[:, h]).then_inc(u_here[2 * s + c], 16)

            def load_v(n, s, c):
                h = slice(HALF * c, HALF * (c + 1))
                sp.dma_start(vraw[s][:, h], peer_v[n].rearrange("o p d -> (o p) d")[:, h]).then_inc(v_here[2 * s + c], 16)
            sp.wait_ge(S("hT_ready"), 8)
            for s in range(2):
                for c in range(2):
                    load_u(slice(s, s + 1), s, c)

            def more_u(n, s):
                for c in range(2):
                    sp.wait_ge(u_low, 2 * n - 3 + c)
                    load_u(bass.ds(n, 1), s, c)

            def more_v(n, s):
                for c in range(2):
                    sp.wait_ge(v_low, 2 * n - 3 + c)
                    load_v(bass.ds(n, 1), s, c)
            with sp.Fori(1, (EARLY + 4) // 2) as r:
                for s in range(2):
                    more_u(2 * r + s, s)
            sp.wait_ge(injected, 1)
            for s in range(2):
                for c in range(2):
                    load_v(slice(s, s + 1), s, c)
            with sp.Fori(1, (EARLY + 2) // 2) as r:
                for s in range(2):
                    more_v(2 * r + s, s)
            with sp.Fori((EARLY + 2) // 2, (NT - 2) // 2) as r:
                for s in range(2):
                    more_u(2 * r + 2 + s, s)
                    more_v(2 * r + s, s)
            for n in range(NT - 2, NT):
                for c in range(2):
                    sp.wait_ge(v_low, 2 * n - 3 + c)
                    load_v(slice(n, n + 1), n % 2, c)
            sp.wait_ge(u_low, 2 * NT)
            sp.dma_start(fgain, ln_final.partition_broadcast(P)).then_inc(S("fgain_here"), 16)
            sp.wait_ge(S("y_ready"), 2)
            sp.dma_start(out.rearrange("(t p) d -> p t d", p=P), yfin).then_inc(S("out_done"), 16)
            sp.wait_ge(S("out_done"), 16)

        @block.gpsimd
        def _(pool):
            nc.gpsimd.memset(relb[:, :], NEG).then_inc(S("neg_ready"), 1)
            nc.gpsimd.memset(restart, 1.0).then_inc(S("restart_ones"), 1)
            for b in (QE[0], QE[1], KE[0], KE[1], ATd):
                nc.gpsimd.memset(b, 0.0).then_inc(S("cleared"), 1)
            pool.wait_ge(S("restart_ones"), 1)
            nc.gpsimd.memset(restart.rearrange("p (n c) -> p n c", c=CHUNK)[:, :, 0:1], 0.0).then_inc(S("restart_ready"), 1)
            pool.wait_ge(h_high, 1)
            nc.gpsimd.tensor_tensor(hTs[:, 1], hT, hTs[:, 0].bitcast(f32), ALU.subtract).then_inc(h_low, 1)

            def low(k, h):
                pool.wait_ge(u_high, h + 1)
                nc.gpsimd.tensor_tensor(Us[:, k, 1, :], uraw[k // 2][:, HALF * (k % 2):HALF * (k % 2 + 1)],
                                        Us[:, k, 0, :].bitcast(f32), ALU.subtract).then_inc(u_low, 1)
            with pool.Fori(0, (EARLY + 2) // 2) as r:
                for k in range(4):
                    low(k, 4 * r + k)

            def weigh_rows(g, q, tok):
                pool.wait_ge(onehots, q + 1)
                rows = rows_[g][:, 1]
                nc.gpsimd.tensor_tensor(rows, rows, IJW[:, 2, tok].unsqueeze(2).to_broadcast([P, TOK, NKEY]),
                                        ALU.mult).then_inc(weighted, 1)
            with pool.Fori(0, T // TOK // ROWS) as r:
                for g in range(ROWS):
                    weigh_rows(g, ROWS * r + g, bass.ds(TOK * (ROWS * r + g), TOK))
            with pool.Fori((EARLY + 2) // 2, NT // 2) as r:
                for k in range(4):
                    low(k, 4 * r + k)

        @block.tensor
        def _(pe):
            def aux_open(name):
                n = aux_no[name]
                if n >= 2:
                    pe.wait_ge(S(aux_uses[n - 2][1]), aux_uses[n - 2][2])
                return aux[n % 2]

            def mm(o_, l, r, start, stop):
                return nc.tensor.matmul(o_, l, r, start=start, stop=stop)

            def project(name, act):
                n, form = chunk_no[name], chunks[chunk_no[name]][2]
                pe.wait_ge(w_here[n % NW], 16 * (n // NW + 1))
                kd = 4 if form == "U" else KD
                w = wring[n % NW].rearrange("p (k c) -> p k c", k=kd)
                for b in range(4 if form == "U" else 2):
                    g = bank_no[name] + b
                    if g >= NG:
                        pe.wait_ge(S(bank_reader[g - NG][0]), bank_reader[g - NG][1])
                    ps = gb_[g % NG]
                    if form == "N":
                        for k in range(kd):
                            last = mm(ps[:, :], act[:, k, b * P:(b + 1) * P], w[:, k, :], k == 0, k == kd - 1)
                    else:
                        for f in range(2):
                            for k in range(kd):
                                c = (2 * b + f) * P
                                last = mm(ps[:, f * T:(f + 1) * T], w[:, k, c:c + P], act[:, k, :], k == 0, k == kd - 1)
                    last.then_inc(proj_full, 1)

            def turn(name, src, ks):
                ps = aux_open(name)
                for i, k in enumerate(ks):
                    for t in range(TT):
                        last = nc.tensor.transpose(ps[:, i * T + t * P:i * T + (t + 1) * P],
                                                   src[:, t, k * P:(k + 1) * P], ident[:, :])
                last.then_inc(aux_full, 1)

            pe.wait_ge(const_here, 16 * 7)
            pe.wait_ge(S("relbb_ready"), 1)
            for n in range(4):
                ps = aux_open(f"bias{n}")
                for j in range(2):
                    last = mm(ps[:, 512 * j:512 * j + ROW], relbb[0:BUCKETS + 1, 2 * n + j, :],
                              onehot_sb[:, :], True, True)
                last.then_inc(aux_full, 1)
            pe.wait_ge(S("hn_ready"), 2)
            turn("tx0", hn, range(0, 4))
            turn("tx1", hn, range(4, 8))
            pe.wait_ge(S("hT_ready"), 2)
            project("hf0", hT)
            project("hq0", hT)
            project("mq0", hT)

            def level(L):
                ps = aux_open(f"L{L}")
                if L == "diag":
                    pe.wait_ge(S("hq_read"), 2)
                    pe.wait_ge(S("k_ready"), 1)
                    q, k = hqT, kT
                else:
                    i = (LEVELS + [128]).index(L)
                    pe.wait_ge(S("QK"), i + 1)
                    i %= 2
                    q, k = QE[i], KE[i]
                for h in range(HG_H):
                    if L == 128:
                        last = mm(ps[:, h * P:(h + 1) * P], k[:, h, 0:P], q[:, h, P:T], True, True)
                    else:
                        for t in range(TT):
                            b = h * TT + t
                            last = mm(ps[:, b * P:(b + 1) * P], k[:, h, t * P:(t + 1) * P],
                                      q[:, h, t * P:(t + 1) * P], True, True)
                last.then_inc(aux_full, 1)

            level("diag")
            project("mk0", hT)
            level(1)
            pe.wait_ge(S("mq_read"), 2)
            pe.wait_ge(S("mk_read"), 2)
            for name, t, heads, nk in (("S0", 0, range(8), P), ("S1a", 1, range(4), T), ("S1b", 1, range(4, 8), T)):
                ps = aux_open(name)
                for i, h in enumerate(heads):
                    r = slice((h % 2) * MB_D, (h % 2 + 1) * MB_D)
                    c = 512 * (h % 2) + (i // 2) * nk
                    last = mm(ps[:, c:c + nk], mqT[r, h // 2, t * P:(t + 1) * P],
                              mkT[r, h // 2, 0:nk], True, True)
                last.then_inc(aux_full, 1)
            project("hi0", hT)
            level(2)
            project("hg0", hT)
            level(4)
            project("mv0", hT)
            level(8)
            project("ga0", hT)
            level(16)
            project("ga1", hT)
            level(32)
            pe.wait_ge(S("mb_prob"), 2)
            for name, items in (("PTa", [(S0, S1, h) for h in range(4)]), ("PTb", [(S0, S1, h) for h in range(4, 8)])):
                ps = aux_open(name)
                for i, (p0, p1, h) in enumerate(items):
                    nc.tensor.transpose(ps[:, i * T:i * T + P], p0[:, h, :], ident[:, :])
                    last = nc.tensor.transpose(ps[:, i * T + P:i * T + T], p1[:, h, 0:P], ident[:, :])
                last.then_inc(aux_full, 1)
            ps = aux_open("PTc")
            for h in range(MB_H):
                last = nc.tensor.transpose(ps[:, h * P:(h + 1) * P], S1[:, h, P:T], ident[:, :])
            last.then_inc(aux_full, 1)
            level(64)
            level(128)
            project("gb0", hT)
            pe.wait_ge(S("PT_read"), 3)
            pe.wait_ge(S("mv_read"), 2)
            ps = aux_open("PV")
            for h in range(MB_H):
                r = slice((h % 2) * MB_D, (h % 2 + 1) * MB_D)
                c = (h // 2) * T
                mm(ps[r, c:c + T], mv_sb[:, 0, h * MB_D:(h + 1) * MB_D], PT0[:, h, :], True, False)
                last = mm(ps[r, c + P:c + T], mv_sb[:, 1, h * MB_D:(h + 1) * MB_D], PT1[:, h, :], False, True)
            last.then_inc(aux_full, 1)
            pe.wait_ge(S("far_read"), 1)
            pe.wait_ge(S("level_read"), 8)
            pe.wait_ge(S("hi_read"), 2)
            ps = aux_open("O")
            for h in range(HG_H):
                e = slice(h * HG_D, (h + 1) * HG_D)
                mm(ps[:, e], ATd[:, h * TT, :], hi_sb[:, 0, e], True, True)
                e1 = slice(512 + h * HG_D, 512 + (h + 1) * HG_D)
                mm(ps[:, e1], AT01[:, h, :], hi_sb[:, 0, e], True, False)
                last = mm(ps[:, e1], ATd[:, h * TT + 1, :], hi_sb[:, 1, e], False, True)
            last.then_inc(aux_full, 1)
            pe.wait_ge(S("hn_ready"), 4)
            turn("tm0", hn, range(0, 4))
            turn("tm1", hn, range(4, 8))
            project("gb1", hT)
            pe.wait_ge(S("o_ready"), 1)
            ps = aux_open("TY")
            for h in range(HG_H):
                for t in range(TT):
                    last = nc.tensor.transpose(ps[:, h * T + t * P:h * T + (t + 1) * P], osb[:, t, h, :], ident[:, :])
            last.then_inc(aux_full, 1)
            pe.wait_ge(S("hT_ready"), 4)
            project("kx0", memT)
            pe.wait_ge(S("yaT_ready"), 1)
            project("upa0", yaT)
            pe.wait_ge(S("ybT_ready"), 1)
            project("upb0", ybT)
            project("kx1", memT)
            pe.wait_ge(S("z_ready"), 4)
            project("out0", zT)
            project("out1", zT)
            project("vx0", memT)
            pe.wait_ge(S("hn_ready"), 6)
            turn("tc0", hn, range(0, 4))
            turn("tc1", hn, range(4, 8))
            pe.wait_ge(S("hT_ready"), 6)
            project("qx0", hT)
            project("qx1", hT)
            pe.wait_ge(S("qx_read"), 4)
            pe.wait_ge(S("kx_read"), 4)
            for t in range(TT):
                ps = aux_open(f"CS{t}")
                for h in range(X_H):
                    for k in range(2):
                        last = mm(ps[:, h * T:(h + 1) * T], qxT[:, 2 * h + k, t * P:(t + 1) * P],
                                  kxT[:, 2 * h + k, :], k == 0, k == 1)
                last.then_inc(aux_full, 1)
            project("vx1", memT)
            pe.wait_ge(S("x_prob"), 2)
            for m in range(TT):
                ps = aux_open(f"CT{m}")
                for h in range(X_H):
                    for t in range(TT):
                        last = nc.tensor.transpose(ps[:, h * T + t * P:h * T + (t + 1) * P],
                                                   CS[:, t, h, m * P:(m + 1) * P], ident[:, :])
                last.then_inc(aux_full, 1)
            pe.wait_ge(S("CPT_read"), 2)
            for c in range(2):
                pe.wait_ge(S("vx_read"), 2 * c + 2)
                ps = aux_open(f"CV{c}")
                for j in range(4):
                    f = 4 * c + j
                    for m in range(TT):
                        last = mm(ps[:, j * T:(j + 1) * T], vx[:, m, f * P:(f + 1) * P], CPT[:, m, f // 2, :], m == 0, m == 1)
                last.then_inc(aux_full, 1)
            pe.wait_ge(S("oxT_ready"), 2)
            project("wo0", oxT)
            project("wo1", oxT)
            pe.wait_ge(S("hn_ready"), 8)
            turn("tf0", hn, range(0, 4))
            turn("tf1", hn, range(4, 8))
            pe.wait_ge(S("hT_ready"), 8)
            for c in range(4):
                project(f"pq{c}", hT)
            pe.wait_ge(S("pq_read"), 8)
            pe.wait_ge(S("sub_here"), 16)
            for n in range(4):
                ps = aux_open(f"PS{n}")
                t = n // 2
                for j in range(8):
                    hc = 8 * (n % 2) + j
                    last = mm(ps[:, j * P:(j + 1) * P], qhT[:, hc, t * P:(t + 1) * P], subT[:, hc, :], True, True)
                last.then_inc(aux_full, 1)
            def acts(k, n, reused):
                if reused:
                    pe.wait_ge(gelu_done, n - 1)
                ps = gb_[2 + k][:, 0:T]
                for a in range(2):
                    slot = 2 * k + a
                    pe.wait_ge(u_low, 2 * n + a + 1)
                    for c in range(4):
                        u = Us[:, slot, :, c * P:(c + 1) * P]
                        hk = hTs[:, :, 4 * a + c, :]
                        mm(ps, u[:, 0], hk[:, 0], a == 0 and c == 0, False)
                        mm(ps, u[:, 0], hk[:, 1], False, False)
                        last = mm(ps, u[:, 1], hk[:, 0], False, a == 1 and c == 3)
                    last.then_inc(u_used, 1)

            pe.wait_ge(h_low, 1)
            for k in range(2):
                acts(k, k, False)
            with pe.Fori(1, EARLY // 2) as r:
                for k in range(2):
                    acts(k, 2 * r + k, True)
            pe.wait_ge(S("rIJW_ready"), 6)
            ps = aux_open("TR")
            for a in range(3):
                for t in range(TT):
                    last = nc.tensor.transpose(ps[:, a * T + t * P:a * T + (t + 1) * P], rIJW[:, a, t, :], ident[:, :])
            last.then_inc(aux_full, 1)
            y = [[aux[t][:, 512 * c:512 * c + 512] for c in range(2)] for t in range(TT)]
            pe.wait_ge(S("IJW_ready"), 1)
            for t in range(TT):
                for c in range(2):
                    last = nc.tensor.matmul(y[t][c], ident[:, :], x_sb[:, t, 512 * c:512 * (c + 1)],
                                            start=True, stop=False, skip_group_check=True)
            last.then_inc(injected, 1)

            def spread(g, q, firsts):
                pe.wait_ge(weighted, q + 1)
                if g == 0:
                    pe.wait_ge(S("first_ready"), firsts)
                for j in range(TOK):
                    last = mm(gb_[g][:, j * P:(j + 1) * P], rows_[g][:, 1, j, :], rows_[g][:, 0, j, :], True, True)
                last.then_inc(spread_done, 1)

            def spread_again(g, q, firsts):
                pe.wait_ge(early_gated, q - ROWS + 1)
                spread(g, q, firsts)
            assert ROWS == NG
            for g in range(ROWS):
                spread(g, g, 1)
            with pe.Fori(1, T // TOK // ROWS) as r:
                for g in range(ROWS):
                    spread_again(g, ROWS * r + g, r + 1)

            def outs(k, n, final):
                pe.wait_ge(coef_done, n + 1)
                for c in range(2):
                    pe.wait_ge(v_low, 2 * n + c + 1)
                    v = Vs[:, 2 * k + c]
                    for t in range(TT):
                        w = Cs[:, k, :, t * P:(t + 1) * P]
                        for i, (cp, vp) in enumerate(((0, 0), (0, 1), (1, 0))):
                            last = nc.tensor.matmul(y[t][c], w[:, cp], v[:, vp], start=False, stop=final and i == 2,
                                                    skip_group_check=True)
                    last.then_inc(v_used, 1)
            with pe.Fori(0, (EARLY - 2) // 2) as r:
                for k in range(2):
                    outs(k, 2 * r + k, False)
            with pe.Fori((EARLY - 2) // 2, (NT - 2) // 2) as r:
                for k in range(2):
                    acts(k, 2 * r + 2 + k, True)
                    outs(k, 2 * r + k, False)
            for k in range(2):
                outs(k, NT - 2 + k, k == 1)

        @block.scalar
        def _(act):
            def bank(name, b):
                g = bank_no[name] + b
                act.wait_ge(proj_full, g + 1)
                return gb_[g % NG], S(bank_reader[g][0])

            def copy_banks(names, dst, func=ACT.Copy, scale=1.0):
                for i, (n, b) in enumerate([(n, b) for n in names for b in range(2)]):
                    ps, read = bank(n, b)
                    nc.scalar.activation(dst(i), ps[:, :], func, scale=scale).then_inc(read, 1)

            def aux_take(name):
                act.wait_ge(aux_full, aux_no[name] + 1)
                return aux[aux_no[name] % 2]

            def aux_copy(name, dst, view=lambda p: p[:, :]):
                nc.scalar.activation(dst, view(aux_take(name)), ACT.Copy).then_inc(S(aux_uses[aux_no[name]][1]), 1)

            def flat(v):
                names = "abc"[:len(v.shape) - 1]
                return v.rearrange(f"p {' '.join(names)} -> p ({' '.join(names)})")

            def halves(v):
                return lambda i: flat(v)[:, 512 * i:512 * (i + 1)]

            def ssq(src, junk_, n):
                for t in range(TT):
                    nc.scalar.activation(junk_[:, t, :], src[:, t, :], ACT.Square,
                                         accum_out=stat[:, n, t:t + 1]).then_inc(S("ssq"), 1)

            def root(n, w, cnt):
                act.wait_ge(S("var"), cnt)
                nc.scalar.activation(stat[:, n, 8:8 + w], stat[:, n, 8:8 + w], ACT.Sqrt).then_inc(S("root"), 1)

            act.wait_ge(x_here, 16)
            ssq(x_sb, hn, 0)
            root(0, 2, 1)
            for n in range(4):
                aux_copy(f"bias{n}", bias_rows[:, 2 * n:2 * n + 2, :],
                         lambda p: p[:, :].rearrange("p (h c) -> p h c", h=2)[:, :, 0:ROW])
            act.wait_ge(mem_here, 16)
            act.wait_ge(aux_full, aux_no["tx1"] + 1)
            ssq(mem_sb, hn, 1)
            root(1, 2, 2)
            nc.scalar.preload_act_table_set("natural_log_exp_and_others")
            act.wait_ge(S("low_ready"), 1)
            nc.scalar.activation(tiny[:, 0:2, :], tiny[:, 0:2, :], ACT.Exp).then_inc(S("low_exp"), 1)
            copy_banks(["hf0"], halves(DI.rearrange("p (a b) -> p a b", a=HG_H)), ACT.Exp, -1.0)
            copy_banks(["hq0"], halves(hqT))
            act.wait_ge(S("k_ready"), 1)
            nc.scalar.activation(E_, E_, ACT.Ln).then_inc(S("lf_ready"), 1)
            copy_banks(["mq0"], halves(mqT))

            def decay(i):
                act.wait_ge(S("diff"), 2 * i + 2 if i < len(LEVELS) else 2 * i + 4)
                if i >= 1:
                    act.wait_ge(S("QK"), i)
                nc.scalar.activation(E_, DI, ACT.Exp).then_inc(S("decay"), 1)
            decay(0)
            copy_banks(["mk0"], halves(mkT))
            decay(1)
            act.wait_ge(S("mb_max"), 2)
            for t, s_ in ((0, S0), (1, S1)):
                for h in range(MB_H):
                    nc.scalar.activation(s_[:, h, :], s_[:, h, :], ACT.Exp, bias=smx[:, t, h:h + 1],
                                         accum_out=smx[:, 2 + t, h:h + 1]).then_inc(S("mb_exp"), 1)
            decay(2)
            copy_banks(["hi0"], halves(hi_sb))
            decay(3)
            for b in range(2):
                g = bank_no["hg0"] + b
                act.wait_ge(proj_full, g + 1)
                nc.scalar.activation(hgtmp[:, b, :], gb_[g % NG][:, :], ACT.Exp, scale=-1.0).then_inc(S("act_chain"), 1)
                nc.scalar.activation(hg_sb[:, b, :], gb_[g % NG][:, :], ACT.Copy).then_inc(S("hg_read"), 1)
            decay(4)
            copy_banks(["mv0"], halves(mv_sb))
            decay(5)
            copy_banks(["ga0"], halves(sgA[:, 0:4, :]), ACT.Exp, -1.0)
            decay(6)
            act.wait_ge(S("silu_ready"), 1)
            copy_banks(["ga1"], halves(sgA[:, 4:8, :]), ACT.Exp, -1.0)
            decay(7)
            aux_copy("PTa", flat(PT0[:, 0:4, :]))
            aux_copy("PTb", flat(PT0[:, 4:8, :]))
            aux_copy("PTc", flat(PT1))
            aux_copy("L128", flat(AT01), lambda p: p[:, 0:HG_H * P])
            copy_banks(["gb0"], halves(sgB[:, 0:4, :]), ACT.Exp, -1.0)
            aux_copy("PV", flat(ybT))
            aux_copy("O", osb.rearrange("p t h e -> p (t h e)"))
            root(2, 8, 3)
            copy_banks(["gb1"], halves(sgB[:, 4:8, :]), ACT.Exp, -1.0)
            copy_banks(["kx0", "kx1"], halves(kxT))

            def copy_vx(c):
                for t in range(TT):
                    ps, read = bank(f"vx{c}", t)
                    nc.scalar.activation(vx[:, t, 512 * c:512 * (c + 1)], ps[:, :], ACT.Copy).then_inc(read, 1)
            act.wait_ge(S("x_new"), 4)
            ssq(x_sb, hn, 3)
            root(3, 2, 4)
            copy_vx(0)
            copy_banks(["qx0", "qx1"], halves(qxT))
            for t in range(TT):
                act.wait_ge(S("x_max"), t + 1)
                ps = aux_take(f"CS{t}")
                for h in range(X_H):
                    nc.scalar.activation(CS[:, t, h, :], ps[:, h * T:(h + 1) * T], ACT.Exp, bias=smx[:, 4, 4 * t + h:4 * t + h + 1],
                                         scale=X_D ** -0.5, accum_out=smx[:, 5, 4 * t + h:4 * t + h + 1]).then_inc(S("xexp"), 1)
            copy_vx(1)
            for m in range(TT):
                aux_copy(f"CT{m}", flat(CPT[:, m]))
            for c in range(2):
                aux_copy(f"CV{c}", flat(oxT[:, 4 * c:4 * c + 4, :]))
            act.wait_ge(aux_full, aux_no["tc1"] + 1)
            act.wait_ge(S("x_new"), 8)
            ssq(x_sb, hn, 4)
            root(4, 2, 5)
            act.wait_ge(S("hT_ready"), 8)
            nc.scalar.activation(hTs[:, 0], hT, ACT.Copy).then_inc(h_high, 1)

            def high_u(k, h, load, again):
                act.wait_ge(u_here[k], load)
                if again:
                    act.wait_ge(u_used, h - 3)
                nc.scalar.activation(Us[:, k, 0, :], uraw[k // 2][:, HALF * (k % 2):HALF * (k % 2 + 1)], ACT.Copy).then_inc(u_high, 1)

            def gelu(k, m, dst):
                act.wait_ge(u_used, 2 * m + 2)
                nc.scalar.activation(dst, gb_[2 + k][:, 0:T], ACT.Gelu_apprx_tanh).then_inc(gelu_done, 1)

            def early(r):
                for k in range(2):
                    high_u(2 * k, 4 * r + 4 + 2 * k, 16 * r + 32, True)
                    gelu(k, 2 * r + k, gate[:, bass.ds(2 * r + k, 1), :].rearrange("p o t -> p (o t)"))
                    high_u(2 * k + 1, 4 * r + 5 + 2 * k, 16 * r + 32, True)

            nc.scalar.preload_act_table(ACT.Gelu_apprx_tanh)
            for c in range(4):
                copy_banks([f"pq{c}"], halves(qhT[:, 4 * c:4 * c + 4, :]))
                high_u(c, c, 16, False)
            for n in range(4):
                aux_copy(f"PS{n}", flat(sc[:, n // 2, 8 * (n % 2):8 * (n % 2) + 8, :]))
            with act.Fori(0, EARLY_A // 2) as r:
                early(r)
            act.wait_ge(S("w_diff"), 1)
            nc.scalar.activation(flat(fv[:, 0]), flat(fv[:, 0]), ACT.Exp).then_inc(S("w_exp"), 1)
            nc.scalar.preload_act_table(ACT.Gelu_apprx_tanh)
            with act.Fori(EARLY_A // 2, EARLY // 2) as r:
                early(r)
            act.wait_ge(S("w_diff"), 2)
            nc.scalar.activation(flat(fv[:, 1]), flat(fv[:, 1]), ACT.Exp).then_inc(S("w_exp"), 1)

            def spread_copy(g, q):
                act.wait_ge(spread_done, q + 1)
                nc.scalar.activation(gate[:, EARLY:NT, bass.ds(TOK * q, TOK)],
                                     gb_[g][:, :].rearrange("p (t i) -> p i t", t=TOK)[:, EARLY:NT, :], ACT.Copy).then_inc(spread_out, 1)

            def first_keys(g, q, n):
                if not isinstance(n, int) or n > 0:
                    act.wait_ge(S("first_ready"), n)
                for j in range(TOK):
                    tok = slice(TOK * q + j, TOK * q + j + 1) if isinstance(q, int) else bass.ds(TOK * q + j, 1)
                    last = nc.scalar.activation(apart[:, j, :], iota_sb[:, :], ACT.Abs, bias=IJW[:, 0, tok], scale=-1.0)
                    last.then_inc(S("apart_ready"), 1)
                act.wait_ge(S("apart_ready"), TOK * n + TOK)
                nc.scalar.activation(rows_[g][:, 0], apart, ACT.Relu, bias=1.0, scale=-1.0).then_inc(S("first_ready"), 1)
            act.wait_ge(S("IJW_ready"), 1)
            first_keys(0, 0, 0)
            with act.Fori(0, T // TOK // ROWS - 1) as r:
                for g in range(ROWS):
                    spread_copy(g, ROWS * r + g)
                    if g == 0:
                        first_keys(g, ROWS * (r + 1), r + 1)
            for g in range(ROWS):
                spread_copy(g, T // TOK - ROWS + g)

            def high_v(k, h, load, again):
                act.wait_ge(v_here[k], load)
                if again:
                    act.wait_ge(v_used, h - 3)
                nc.scalar.activation(Vs[:, k, 0, :], vraw[k // 2][:, HALF * (k % 2):HALF * (k % 2 + 1)], ACT.Copy).then_inc(v_high, 1)
            nc.scalar.preload_act_table(ACT.Gelu_apprx_tanh)
            for k in range(4):
                high_v(k, k, 16, False)
            with act.Fori(0, (EARLY - 2) // 2) as r:
                for k in range(4):
                    high_v(k, 4 * r + 4 + k, 16 * r + 32, True)

            def fused(r, more_u):
                for k in range(2):
                    m = 2 * r + 2 + k
                    if more_u:
                        high_u(2 * k, 2 * m + 4, 16 * r + 48, True)
                    if not isinstance(r, int) or r > EARLY // 2:
                        act.wait_ge(coef_done, m - 1)
                    gelu(k, m, actr[k])
                    if more_u:
                        high_u(2 * k + 1, 2 * m + 5, 16 * r + 48, True)
                    for a in range(2):
                        high_v(2 * k + a, 2 * m + a, 16 * r + 32, True)
            fused((EARLY - 2) // 2, True)
            with act.Fori(EARLY // 2, (NT - 4) // 2) as r:
                fused(r, True)
            fused((NT - 4) // 2, False)
            act.wait_ge(v_used, 2 * NT)
            for t in range(TT):
                nc.scalar.activation(yfin[:, t, :], aux[t][:, :], ACT.Square, accum_out=stat[:, 5, t:t + 1]).then_inc(S("ssq"), 1)
            root(5, 2, 6)

        @block.vector
        def _(dve):
            TTn, TS = nc.vector.tensor_tensor, nc.vector.tensor_scalar
            links = [0]

            def link(ins):
                links[0] += 1
                ins.then_inc(S("dve_chain"), 1)
                dve.wait_ge(S("dve_chain"), links[0])

            def flat(v):
                names = "abc"[:len(v.shape) - 1]
                return v.rearrange(f"p {' '.join(names)} -> p ({' '.join(names)})")

            def over(v, n):
                return v.unsqueeze(len(v.shape)).to_broadcast([*v.shape, n])

            def mean(n, w, scale, ssqs):
                dve.wait_ge(S("ssq"), ssqs)
                TS(stat[:, n, 8:8 + w], stat[:, n, 0:w], scale, EPS, ALU.mult, ALU.add).then_inc(S("var"), 1)

            def normed(src, n, roots):
                dve.wait_ge(S("root"), roots)
                link(nc.vector.reciprocal(stat[:, n, 8:10], stat[:, n, 8:10]))
                for t in range(TT):
                    TS(hn[:, t, :], src[:, t, :], stat[:, n, 8 + t:9 + t], None, ALU.mult).then_inc(S("hn_ready"), 1)

            def aux_take(name):
                dve.wait_ge(aux_full, aux_no[name] + 1)
                return aux[aux_no[name] % 2]

            def turned(names, gain, proj_before, dst=hT):
                if proj_before:
                    dve.wait_ge(proj_full, bank_end(proj_before))
                for i, n in enumerate(names):
                    ps = aux_take(n)
                    TTn(dst[:, 4 * i:4 * i + 4, :], ps[:, :].rearrange("p (k t) -> p k t", k=4),
                        over(gain_sb[:, gain, 4 * i:4 * i + 4], T), ALU.mult).then_inc(S("hT_ready"), 1)

            mean(0, 2, 1.0 / D, 2)
            dve.wait_ge(const_here, 16 * 7)
            nc.vector.tensor_copy(relbb[0:BUCKETS + 1, :, :], over(relb[:, :], P)).then_inc(S("relbb_ready"), 1)
            normed(x_sb, 0, 1)
            link(TTn(tiny[:, 2, :], low_sb[:, 0, :], low_sb[:, 1, :], ALU.max))
            TTn(tiny[:, 0, :], low_sb[:, 0, :], tiny[:, 2, :], ALU.subtract)
            TTn(tiny[:, 1, :], low_sb[:, 1, :], tiny[:, 2, :], ALU.subtract).then_inc(S("low_ready"), 1)
            turned(["tx0", "tx1"], 0, None)
            mean(1, 2, 1.0 / D, 4)
            dve.wait_ge(S("low_exp"), 1)
            link(TTn(tiny[:, 2, :], tiny[:, 0, :], tiny[:, 1, :], ALU.add))
            link(nc.vector.reciprocal(tiny[:, 3, :], tiny[:, 2, :]))
            TTn(lb[:, 0, :], tiny[:, 0, :], tiny[:, 3, :], ALU.mult)
            link(TTn(lb[:, 1, :], tiny[:, 1, :], tiny[:, 3, :], ALU.mult))
            dve.wait_ge(S("hf_read"), 2)
            link(TS(DI, DI, 1.0, None, ALU.add))
            link(nc.vector.reciprocal(DI, DI))
            for h in range(HG_H):
                last = TS(E_[:, h * T:(h + 1) * T], DI[:, h * T:(h + 1) * T], lb[:, 1, h:h + 1], lb[:, 0, h:h + 1], ALU.mult, ALU.add)
            link(last)
            TS(flat(kT), E_, -1.0, 1.0, ALU.mult, ALU.add).then_inc(S("k_ready"), 1)
            dve.wait_ge(S("lf_ready"), 1)
            dve.wait_ge(S("restart_ready"), 1)
            nc.vector.tensor_tensor_scan(bsum, restart, E_, 0.0, ALU.mult, ALU.add).then_inc(S("b_ready"), 1)
            dve.wait_ge(S("b_ready"), 1)

            def level_diff(i):
                if i >= 1:
                    dve.wait_ge(S("decay"), i)
                if i < len(LEVELS):
                    L = LEVELS[i]
                    b = bsum.rearrange("p (n a l) -> p n a l", a=2, l=L)
                    d = DI.rearrange("p (n a l) -> p n a l", a=2, l=L)
                    mid = b[:, :, 0, L - 1:L].to_broadcast([P, T * HG_H // (2 * L), L])
                    if L < CHUNK:
                        TTn(d[:, :, 1, :], b[:, :, 1, :], mid, ALU.subtract).then_inc(S("diff"), 1)
                    else:
                        nc.vector.tensor_copy(d[:, :, 1, :], b[:, :, 1, :]).then_inc(S("diff"), 1)
                    TTn(d[:, :, 0, :], mid, b[:, :, 0, :], ALU.subtract).then_inc(S("diff"), 1)
                else:
                    b = bsum.rearrange("p (h n l) -> p h n l", n=4, l=CHUNK)
                    d = DI.rearrange("p (h n l) -> p h n l", n=4, l=CHUNK)
                    end = [b[:, :, c, CHUNK - 1:CHUNK].to_broadcast([P, HG_H, CHUNK]) for c in range(4)]
                    nc.vector.tensor_copy(d[:, :, 2, :], b[:, :, 2, :]).then_inc(S("diff"), 1)
                    TTn(d[:, :, 3, :], b[:, :, 3, :], end[2], ALU.add).then_inc(S("diff"), 1)
                    TTn(d[:, :, 1, :], end[1], b[:, :, 1, :], ALU.subtract).then_inc(S("diff"), 1)
                    TTn(d[:, :, 0, :], end[0], b[:, :, 0, :], ALU.subtract).then_inc(S("dve_chain"), 1)
                    links[0] += 1
                    dve.wait_ge(S("dve_chain"), links[0])
                    TTn(d[:, :, 0, :], d[:, :, 0, :], end[1], ALU.add).then_inc(S("diff"), 1)

            def level_qk(i):
                dve.wait_ge(S("decay"), i + 1)
                if i == 0:
                    dve.wait_ge(S("cleared"), 5)
                    dve.wait_ge(S("hq_read"), 2)
                if i >= 2:
                    L = (LEVELS + [128])[i - 2]
                    dve.wait_ge(aux_full, aux_no[f"L{L}"] + 1)
                L = (LEVELS + [128])[i]
                half = lambda v, a: v.rearrange("p (n a l) -> p n a l", a=2, l=L)[:, :, a, :]
                TTn(half(flat(QE[i % 2]), 1), half(flat(hqT), 1), half(E_, 1), ALU.mult)
                TTn(half(flat(KE[i % 2]), 0), half(flat(kT), 0), half(E_, 0), ALU.mult).then_inc(S("QK"), 1)

            def level_take(name):
                ps = aux_take(f"L{name}")
                m = ident[:, :] if name == "diag" else mask_sb[:, LEVELS.index(name), :]
                m = m.bitcast(u32).unsqueeze(1).to_broadcast([P, HG_H * TT, P])
                nc.vector.copy_predicated(ATd, m, ps[:, :].rearrange("p (b t) -> p b t", b=HG_H * TT)).then_inc(S("level_read"), 1)
                dve.wait_ge(S("level_read"), ([*["diag"], *LEVELS]).index(name) + 1)

            level_diff(0)
            level_qk(0)
            dve.wait_ge(masks_here, 16)
            level_take("diag")
            level_diff(1)
            level_qk(1)
            level_take(1)
            dve.wait_ge(S("bias_here"), 16)
            for name, s_, bb in (("S0", S0, biasB[:, :, P:T]), ("S1a", S1[:, 0:4, :], biasB[:, 0:4, :]), ("S1b", S1[:, 4:8, :], biasB[:, 4:8, :])):
                ps = aux_take(name)
                for odd in range(2):
                    nc.vector.scalar_tensor_tensor(
                        out=s_[:, odd::2, :], in0=ps[:, 512 * odd:512 * odd + 512].rearrange("p (h k) -> p h k", k=s_.shape[2]),
                        scalar=MB_D ** -0.5, in1=bb[:, odd::2, :], op0=ALU.mult, op1=ALU.add).then_inc(S("biased"), 1)
            dve.wait_ge(S("biased"), 6)
            for t, s_ in ((0, S0), (1, S1)):
                nc.vector.tensor_reduce(smx[:, t, 0:MB_H], s_, AX.X, ALU.max, negate=True).then_inc(S("mb_max"), 1)
            for i, before in ((2, 2), (3, 4), (4, 8)):
                level_diff(i)
                level_qk(i)
                level_take(before)
            dve.wait_ge(S("mb_exp"), 16)
            link(nc.vector.reciprocal(smx[:, 2:4, 0:MB_H], smx[:, 2:4, 0:MB_H]))
            TTn(S0, S0, over(smx[:, 2, 0:MB_H], P), ALU.mult).then_inc(S("mb_prob"), 1)
            TTn(S1, S1, over(smx[:, 3, 0:MB_H], T), ALU.mult).then_inc(S("mb_prob"), 1)
            level_diff(5)
            level_qk(5)
            level_take(16)
            level_diff(6)
            level_qk(6)
            dve.wait_ge(S("hg_read"), 2)
            link(TS(flat(hgtmp), flat(hgtmp), 1.0, None, ALU.add))
            link(nc.vector.reciprocal(flat(hgtmp), flat(hgtmp)))
            TTn(flat(hg_sb), flat(hg_sb), flat(hgtmp), ALU.mult).then_inc(S("silu_ready"), 1)
            level_take(32)
            level_diff(7)
            level_qk(7)
            level_take(64)
            dve.wait_ge(aux_full, aux_no["PTc"] + 1)
            normed(mem_sb, 1, 2)

            def sigmoid(v, fam, i):
                dve.wait_ge(S(f"{fam}_read"), 2 * i + 2)
                v = flat(v[:, 4 * i:4 * i + 4, :])
                link(TS(v, v, 1.0, None, ALU.add))
                nc.vector.reciprocal(v, v).then_inc(S("sig_ready"), 1)
            sigmoid(sgA, "ga", 0)
            sigmoid(sgA, "ga", 1)
            dve.wait_ge(S("o_read"), 1)
            link(TTn(osq, osb, osb, ALU.mult))
            nc.vector.tensor_reduce(stat[:, 2, 0:8], osq.rearrange("p t h e -> p (t h) e"), AX.X, ALU.add).then_inc(S("ssq"), 1)
            mean(2, 8, 1.0 / HG_D, 5)
            turned(["tm0", "tm1"], 3, None, memT)
            dve.wait_ge(S("root"), 3)
            link(nc.vector.reciprocal(stat[:, 2, 8:16], stat[:, 2, 8:16]))
            o3 = osb.rearrange("p t h e -> p (t h) e")
            dve.wait_ge(S("silu_ready"), 1)
            link(TTn(o3, o3, over(stat[:, 2, 8:16], HG_D), ALU.mult))
            of = osb.rearrange("p t h e -> p (t h e)")
            TTn(of, of, flat(hg_sb), ALU.mult).then_inc(S("o_ready"), 1)
            TTn(yaT, aux_take("TY")[:, :].rearrange("p (h t) -> p h t", h=HG_H), over(hgn_sb[:, :], T), ALU.mult).then_inc(S("yaT_ready"), 1)
            sigmoid(sgB, "gb", 0)
            sigmoid(sgB, "gb", 1)
            dve.wait_ge(S("sig_ready"), 4)
            for b in range(4):
                g = bank_no["upa0"] + b
                dve.wait_ge(proj_full, g + 1)
                TTn(flat(sgA[:, 2 * b:2 * b + 2, :]), flat(sgA[:, 2 * b:2 * b + 2, :]), gb_[g % NG][:, :], ALU.mult).then_inc(S("upa_read"), 1)
            for b in range(4):
                g = bank_no["upb0"] + b
                dve.wait_ge(proj_full, g + 1)
                TTn(flat(sgB[:, 2 * b:2 * b + 2, :]), flat(sgB[:, 2 * b:2 * b + 2, :]), gb_[g % NG][:, :], ALU.mult).then_inc(S("upb_read"), 1)
                dve.wait_ge(S("upb_read"), b + 1)
                TTn(flat(zT[:, 2 * b:2 * b + 2, :]), flat(sgA[:, 2 * b:2 * b + 2, :]), flat(sgB[:, 2 * b:2 * b + 2, :]), ALU.add).then_inc(S("z_ready"), 1)

            def add_to_x(fam):
                for c in range(2):
                    for t in range(TT):
                        g = bank_no[f"{fam}{c}"] + t
                        dve.wait_ge(proj_full, g + 1)
                        xs = x_sb[:, t, 512 * c:512 * (c + 1)]
                        TTn(xs, xs, gb_[g % NG][:, :], ALU.add).then_inc(S(bank_reader[g][0]), 1)
                dve.wait_ge(S(f"{fam}_read"), 4)
                nc.vector.engine_nop().then_inc(S("x_new"), 4)
            add_to_x("out")
            mean(3, 2, 1.0 / D, 7)
            normed(x_sb, 3, 4)
            turned(["tc0", "tc1"], 1, "gb1")
            for t in range(TT):
                ps = aux_take(f"CS{t}")
                m = smx[:, 4, 4 * t:4 * t + 4]
                link(nc.vector.tensor_reduce(m, ps[:, :].rearrange("p (h m) -> p h m", h=X_H), AX.X, ALU.max, negate=True))
                TS(m, m, X_D ** -0.5, None, ALU.mult).then_inc(S("x_max"), 1)
            for t in range(TT):
                dve.wait_ge(S("xexp"), 4 * t + 4)
                r_ = smx[:, 5, 4 * t:4 * t + 4]
                link(nc.vector.reciprocal(r_, r_))
                TTn(CS[:, t], CS[:, t], over(r_, T), ALU.mult).then_inc(S("x_prob"), 1)
            add_to_x("wo")
            mean(4, 2, 1.0 / D, 9)
            normed(x_sb, 4, 5)
            turned(["tf0", "tf1"], 2, "qx1")

            def top16(rows, src, spare, vals, idx):
                for r in rows:
                    last = nc.vector.max(vals(r)[:, 0:8], src(r))
                link(last)
                for r in rows:
                    nc.vector.max_index(idx(r)[:, 0:8], vals(r)[:, 0:8], src(r))
                    last = nc.vector.match_replace(spare(r), vals(r)[:, 0:8], src(r), LOWEST)
                link(last)
                for r in rows:
                    last = nc.vector.max(vals(r)[:, 8:16], spare(r))
                link(last)
                for r in rows:
                    last = nc.vector.max_index(idx(r)[:, 8:16], vals(r)[:, 8:16], spare(r))
                link(last)

            dve.wait_ge(proj_full, bank_end("pq3"))
            dve.wait_ge(aux_full, aux_no["PS3"] + 1)
            for t in range(TT):
                dve.wait_ge(S("sc_read"), 2 * t + 2)
                top16(range(2 * PH), lambda r: sc[:, t, r, :], lambda r: sc2[:, t, r, :],
                      lambda r: sv[:, t, r, :], lambda r: si[:, t, r, :].bitcast(u32))
                link(nc.vector.tensor_copy(flat(sif[:, t]), flat(si[:, t]).bitcast(u32)))
                s4 = sv[:, t].rearrange("p (h c) k -> p h c k", c=2)
                i4 = sif[:, t].rearrange("p (h c) k -> p h c k", c=2)
                link(TTn(cand.rearrange("p h (a b) -> p h a b", a=PK), over(s4[:, :, 0, :], PK),
                         s4[:, :, 1, :].unsqueeze(2).to_broadcast([P, PH, PK, PK]), ALU.add))
                top16(range(PH), lambda r: cand[:, r, :], lambda r: cand2[:, r, :],
                      lambda r: fv[:, t, r, :], lambda r: pos[:, t, r, :].bitcast(u32))
                m = fv[:, t, :, 0:1]
                nc.vector.tensor_copy(wsum[:, t, :], m.rearrange("p h o -> p (h o)")).then_inc(S("dve_chain"), 1)
                pf = flat(pos[:, t]).bitcast(u32)
                TS(ab[:, 0, :].bitcast(u32), pf, 4, None, ALU.logical_shift_right).then_inc(S("dve_chain"), 1)
                TS(ab[:, 1, :].bitcast(u32), pf, PK - 1, None, ALU.bitwise_and).then_inc(S("dve_chain"), 1)
                links[0] += 3
                dve.wait_ge(S("dve_chain"), links[0])
                TTn(fv[:, t], fv[:, t], over(wsum[:, t, :], PK), ALU.subtract).then_inc(S("w_diff"), 1)
                link(nc.vector.tensor_copy(flat(abf), flat(ab).bitcast(u32)))
                for c in range(2):
                    link(TTn(eq, over(abf[:, c, :], PK), iota_sb[:, 0:PK].unsqueeze(1).to_broadcast([P, PH * PK, PK]), ALU.is_equal))
                    link(TTn(eq2.rearrange("p (h k) a -> p h k a", h=PH), eq.rearrange("p (h k) a -> p h k a", h=PH),
                             i4[:, :, c, :].unsqueeze(2).to_broadcast([P, PH, PK, PK]), ALU.mult))
                    nc.vector.tensor_reduce(rIJW[:, c, t, :], eq2, AX.X, ALU.add).then_inc(S("rIJW_ready"), 1)
            for t in range(TT):
                dve.wait_ge(S("w_exp"), t + 1)
                link(nc.vector.tensor_reduce(wsum[:, t, :], fv[:, t], AX.X, ALU.add))
                link(nc.vector.reciprocal(wsum[:, t, :], wsum[:, t, :]))
                TTn(rIJW[:, 2, t, :].rearrange("p (h k) -> p h k", h=PH), fv[:, t], over(wsum[:, t, :], PK), ALU.mult).then_inc(S("rIJW_ready"), 1)
            nc.vector.tensor_copy(flat(IJW), aux_take("TR")[:, 0:3 * T]).then_inc(S("IJW_ready"), 1)
            dve.wait_ge(S("IJW_ready"), 1)

            def rows(g, tok):
                if g == 0:
                    TTn(rows_[g][:, 1], iota_sb[:, :].unsqueeze(1).to_broadcast([P, TOK, NKEY]),
                        IJW[:, 1, tok].unsqueeze(2).to_broadcast([P, TOK, NKEY]), ALU.is_equal).then_inc(onehots, 1)
                    return
                TTn(rows_[g], iota_sb[:, :].unsqueeze(1).unsqueeze(1).to_broadcast([P, 2, TOK, NKEY]),
                    IJW[:, 0:2, tok].unsqueeze(3).to_broadcast([P, 2, TOK, NKEY]), ALU.is_equal).then_inc(onehots, 1)

            def gate_early(g, q):
                dve.wait_ge(spread_out, q + 1)
                v = gate[:, 0:EARLY, bass.ds(TOK * q, TOK)]
                TTn(v, v, gb_[g][:, :].rearrange("p (t i) -> p i t", t=TOK)[:, 0:EARLY, :], ALU.mult).then_inc(early_gated, 1)
            dve.wait_ge(gelu_done, EARLY)
            for g in range(ROWS):
                rows(g, slice(TOK * g, TOK * (g + 1)))
            with dve.Fori(0, T // TOK // ROWS - 1) as r:
                for g in range(ROWS):
                    dve.wait_ge(spread_done, ROWS * r + g + 1)
                    rows(g, bass.ds(TOK * (ROWS * (r + 1) + g), TOK))
                    gate_early(g, ROWS * r + g)
            for g in range(ROWS):
                gate_early(g, T // TOK - ROWS + g)

            dve.wait_ge(spread_out, T // TOK)
            dve.wait_ge(early_gated, T // TOK)

            def low_v(k, h):
                dve.wait_ge(v_high, h + 1)
                TTn(Vs[:, k, 1, :], vraw[k // 2][:, HALF * (k % 2):HALF * (k % 2 + 1)], Vs[:, k, 0, :].bitcast(f32),
                    ALU.subtract).then_inc(v_low, 1)

            def split_coef(k, m, src, again):
                if again:
                    dve.wait_ge(v_used, 2 * m - 2)
                nc.vector.tensor_copy(Cs[:, k, 0, :].unsqueeze(1), src).then_inc(S("coef_high"), 1)
                dve.wait_ge(S("coef_high"), m + 1)
                TTn(Cs[:, k, 1, :].unsqueeze(1), src, Cs[:, k, 0, :].bitcast(f32).unsqueeze(1), ALU.subtract).then_inc(coef_done, 1)
            for k in range(2):
                split_coef(k, k, gate[:, k:k + 1, :], False)
                for a in range(2):
                    low_v(2 * k + a, 2 * k + a)
            with dve.Fori(0, (EARLY - 2) // 2) as r:
                for k in range(2):
                    m = 2 * r + 2 + k
                    low_v(2 * k, 2 * m)
                    split_coef(k, m, gate[:, bass.ds(m, 1), :], True)
                    low_v(2 * k + 1, 2 * m + 1)
            with dve.Fori((EARLY - 2) // 2, (NT - 2) // 2) as r:
                for k in range(2):
                    m = 2 * r + 2 + k
                    low_v(2 * k, 2 * m)
                    dve.wait_ge(gelu_done, m + 1)
                    TTn(actr[k].unsqueeze(1), actr[k].unsqueeze(1), gate[:, bass.ds(m, 1), :], ALU.mult).then_inc(product, 1)
                    dve.wait_ge(product, m + 1 - EARLY)
                    split_coef(k, m, actr[k].unsqueeze(1), True)
                    low_v(2 * k + 1, 2 * m + 1)
            mean(5, 2, 1.0 / D, 11)
            dve.wait_ge(S("root"), 6)
            link(nc.vector.reciprocal(stat[:, 5, 8:10], stat[:, 5, 8:10]))
            dve.wait_ge(S("fgain_here"), 16)
            for t in range(TT):
                nc.vector.scalar_tensor_tensor(out=yfin[:, t, :], in0=aux[t][:, :], scalar=stat[:, 5, 8 + t:9 + t],
                                               in1=fgain, op0=ALU.mult, op1=ALU.mult).then_inc(S("y_ready"), 1)


def level_masks():
    s, t = np.arange(P)[:, None], np.arange(P)[None, :]
    rows = [(s // (2 * L) == t // (2 * L)) & (s // L % 2 == 0) & (t // L % 2 == 1) for L in LEVELS]
    return np.stack(rows + [s == t]).astype(np.float32)


def bucket_onehot():
    import math
    dist = 255 - np.arange(ROW)
    exact = BUCKETS // 2
    d = np.maximum(dist, 1).astype(np.float32)
    scaled = np.log(d / np.float32(exact)) / np.float32(math.log(MAX_DIST / exact))
    large = np.minimum(exact + (scaled * np.float32(BUCKETS - exact)).astype(np.int32), BUCKETS - 1)
    b = np.where(dist < exact, dist, large)
    b = np.where(dist < 0, BUCKETS, b)
    return (np.arange(BUCKETS + 1)[:, None] == b[None, :]).astype(np.float32)


def kernel(**inputs):
    import concourse.bacc as bacc
    from concourse.bass_utils import run_bass_kernel_spmd

    a = {k: np.asarray(v) for k, v in inputs.items()}

    def chunked(w):
        k, n = w.shape
        c = 512 if k == D else n
        return np.ascontiguousarray(w.reshape(k // P, P, n // c, c).transpose(2, 1, 0, 3)).reshape(n // c, P, WSLOT)

    def columns(v):
        return v.reshape(-1, P).T

    arrays = {
        "x": a["x"][0], "mem": a["mem"][0], "rel_bias": a["rel_bias"],
        "w_in": chunked(a["w_in"][0]), "w_up_a": chunked(a["w_up_a"][0]), "w_up_b": chunked(a["w_up_b"][0]),
        "w_out": chunked(a["w_out"][0]), "wq_x": chunked(a["wq_x"][0]), "wk_x": chunked(a["wk_x"][0]),
        "wv_x": chunked(a["wv_x"][0]), "wo_x": chunked(a["wo_x"][0]), "peer_query": chunked(a["peer_query"][0]),
        "subkeys": a["peer_subkeys"][0].reshape(2 * PH, NKEY, P).transpose(2, 0, 1),
        "peer_u": a["peer_u"][0].reshape(NT, P, KD, P).transpose(0, 3, 2, 1).reshape(NT, P, D),
        "peer_v": a["peer_v"][0].reshape(NT, P, D),
        "gains": np.stack([columns(a[k][0]) for k in ("ln_mix", "ln_cross", "ln_ffn", "ln_mem")], axis=1),
        "hg_lower": np.stack([columns(a["hg_lower"][i]) for i in range(2)], axis=1),
        "hg_norm": columns(a["hg_norm"][0]),
        "ln_final": a["ln_final"],
        "onehot": bucket_onehot(), "masks": level_masks(),
        "iota": np.tile(np.arange(NKEY, dtype=np.float32), (P, 1)),
    }
    nc = bacc.Bacc("TRN2", target_bir_lowering=False, num_devices=1)
    arrays = {k: np.ascontiguousarray(v) for k, v in arrays.items()}
    args = {k: nc.dram_tensor(f"in_{k}", v.shape, mybir.dt.from_np(v.dtype), kind="ExternalInput").ap() for k, v in arrays.items()}
    out = nc.dram_tensor("out", (T, D), mybir.dt.float32, kind="ExternalOutput").ap()
    hybrid_layer(nc, **args, out=out)
    got = run_bass_kernel_spmd(nc, [{f"in_{k}": v for k, v in arrays.items()}], core_ids=[0])
    return got.results[0]["out"].reshape(1, T, D)
```

```python
import numpy as np
import concourse.bass as bass
from concourse import mybir
from contextlib import ExitStack

D = 1024
T = 256
P = 128
KD = D // P
TT = T // P
HG_H, HG_D = 4, 128
CHUNK = 64
MB_H, MB_D = 8, 64
X_H, X_D = 4, 256
PH, PK = 8, 16
NKEY = 128
EPS = 1e-6
BUCKETS, MAX_DIST = 32, 2048
ROW = 384
NEG = -1e30
LOWEST = -3e38
LEVELS = [1, 2, 4, 8, 16, 32, 64]
NG = 4
NT = NKEY
HALF = D // 2
FIRST = [("hf0", 1, "T"), ("hq0", 0, "T"), ("mq0", 4, "T"), ("mk0", 5, "T"), ("hi0", 2, "N"), ("hg0", 3, "N"), ("mv0", 6, "N"),
         ("ga0", 7, "T"), ("ga1", 8, "T"), ("gb0", 9, "T")]
SECOND = [("gb1", 10, "T"), ("kx0", 0, "T"), ("upa0", 0, "U"), ("upb0", 0, "U"), ("kx1", 1, "T"), ("out0", 0, "N"), ("out1", 1, "N"),
          ("vx0", 0, "N"), ("qx0", 0, "T"), ("qx1", 1, "T"), ("vx1", 1, "N"), ("wo0", 0, "N"), ("wo1", 1, "N")]
NF = 8 * len(FIRST)
NP = 8 * len(SECOND)
PTILES = NP // 2
RAW = 8
QT = 2 * PH
EARLY = 38
EXP_AT = (20, 32)
TOK = 4
ROWS = 4


def hybrid_layer(nc, x, mem, rel_bias, first_pieces, pieces,
                 peer_query, subkeys, peer_u, peer_v, gains, hg_lower, hg_norm, ln_final,
                 onehot, masks, iota, out):
    f32, u32 = mybir.dt.float32, mybir.dt.uint32
    ALU, ACT, AX = mybir.AluOpType, mybir.ActivationFunctionType, mybir.AxisListType

    chunks = [(name, form) for name, _, form in FIRST + SECOND]
    chunk_no = {c[0]: n for n, c in enumerate(chunks)}
    banks_of = {"T": 2, "N": 2, "U": 4}
    bank_no, bank_reader, seen = {}, [], {}
    for name, form in chunks:
        bank_no[name] = len(bank_reader)
        for _ in range(banks_of[form]):
            fam = name[:-1]
            seen[fam] = seen.get(fam, 0) + 1
            bank_reader.append((f"{fam}_read", seen[fam]))
    bank_full = []
    for n, (_, form) in enumerate(chunks):
        for b in range(banks_of[form]):
            done = 8 if form == "N" else (b + 1) * 8 // banks_of[form]
            bank_full.append(("w_used", 8 * n + done) if n < len(FIRST) else ("u_used", 8 * (n - len(FIRST)) + done))
    split_no = {n: i + 1 for i, n in enumerate(["tx0", "tx1", "yb", "mem0", "mem1", "ya", "z0", "z1", "z2", "z3", "tc0", "tc1", "ox0", "ox1", "tf0", "tf1"])}
    aux_uses = [("tx0", "hT_ready", 1), ("tx1", "hT_ready", 2), ("bias0", "bias_read", 1), ("bias1", "bias_read", 2),
                ("bias2", "bias_read", 3), ("bias3", "bias_read", 4), ("Ldiag", "level_read", 1), ("L1", "level_read", 2),
                ("S0", "biased", 2), ("S1a", "biased", 4), ("S1b", "biased", 6),
                ("L2", "level_read", 3), ("L4", "level_read", 4), ("L8", "level_read", 5), ("L16", "level_read", 6),
                ("L32", "level_read", 7), ("PTa", "PT_read", 1), ("PTb", "PT_read", 2), ("PTc", "PT_read", 3),
                ("L64", "level_read", 8), ("L128", "far_read", 1), ("PV", "ybT_ready", 1),
                ("O", "o_read", 1), ("tm0", "hT_ready", 3), ("tm1", "hT_ready", 4), ("TY", "yaT_ready", 1),
                ("tc0", "hT_ready", 5), ("tc1", "hT_ready", 6), ("CS0", "xexp", 4), ("CS1", "xexp", 8),
                ("CT0", "CPT_read", 1), ("CT1", "CPT_read", 2), ("CV0", "oxT_ready", 1), ("CV1", "oxT_ready", 2),
                ("tf0", "hT_ready", 7), ("tf1", "hT_ready", 8),
                ("PS0", "sc_read", 1), ("PS1", "sc_read", 2), ("PS2", "sc_read", 3), ("PS3", "sc_read", 4),
                ("TR", "IJW_ready", 1)]
    aux_no = {n: i for i, (n, _, _) in enumerate(aux_uses)}

    ctx = ExitStack()
    with ctx:
        def sb(name, shape, dt=f32):
            return ctx.enter_context(nc.sbuf_tensor(name, shape, dt))

        ident = sb("ident", [P, P])
        gain_sb = sb("gain_sb", [P, 4, KD])
        hgn_sb = sb("hgn_sb", [P, HG_H])
        low_sb = sb("low_sb", [P, 2, HG_H])
        lb = sb("lb", [P, 2, HG_H])
        tiny = sb("tiny", [P, 4, HG_H])
        stat = sb("stat", [P, 6, 16])
        smx = sb("smx", [P, 6, 16])
        relb = sb("relb", [BUCKETS + 1, MB_H])
        onehot_sb = sb("onehot_sb", [BUCKETS + 1, ROW])
        iota_sb = sb("iota_sb", [P, NKEY])
        LOW, SIZE = 38144, 51456
        with nc.sbuf_tensor("arena", [P, SIZE], f32) as arena:
            pass
        f32r = mybir.dt.float32r
        As = sb("As", [P, 2, KD, T], f32r)
        sb("arena_gap", [P, 4096])
        xTs = sb("xTs", [P, 2, KD, T], f32r)
        sb("arena_low", [P, LOW - 12288])
        hTs = sb("hTs", [P, 2, KD, T], f32r)
        Us = sb("Us", [P, 4, 2, HALF], f32r)
        Cs = sb("Cs", [P, 2, 2, T], f32r)
        Vs = sb("Vs", [P, 4, 2, HALF], f32r)

        def at_(off, *dims):
            n = int(np.prod(dims))
            v = arena[:, off:off + n]
            if len(dims) == 1:
                return v
            names = "abcd"[:len(dims)]
            return v.rearrange(f"p ({' '.join(names)}) -> p {' '.join(names)}", **dict(zip(names, dims)))

        wraw = [at_(4096 + HALF * s, HALF) for s in range(RAW)]
        Ws = As.rearrange("p a k t -> p (a k t)").rearrange("p (s a c) -> p s a c", s=4, a=2)
        kxT = at_(28672, KD, T)
        vx = at_(14336, TT, D)
        x_sb = at_(34816, TT, D)
        hT = at_(49408, KD, T)
        o = 16384

        def take(*dims):
            nonlocal o
            if o < 36864 and o + int(np.prod(dims)) > 34816:
                o = 36864
            v = at_(o, *dims)
            o += int(np.prod(dims))
            return v
        hqT = take(HG_H, T)
        kT = take(HG_H, T)
        bsum = take(HG_H * T)
        E_ = take(HG_H * T)
        DI = take(HG_H * T)
        assert o + 4 * HG_H * T <= 34816
        sgB = at_(o, KD, T)
        QE = [take(HG_H, T) for _ in range(2)]
        AT01 = at_(o, HG_H, P)
        yaT = at_(o, HG_H, T)
        KE = [take(HG_H, T) for _ in range(2)]
        ATd = take(HG_H * TT, P)
        hi_sb = take(TT, HG_H * HG_D)
        hg_sb = take(TT, HG_H * HG_D)
        mask_sb = take(len(LEVELS), P)
        mqT = take(MB_H // 2, T)
        mkT = take(MB_H // 2, T)
        mv_sb = take(TT, MB_H * MB_D)
        S0 = take(MB_H, P)
        bias_rows = take(MB_H, ROW)
        biasB = take(MB_H, T)
        S1 = take(MB_H, T)
        mem_sb = take(TT, D)
        sgA = at_(12288, KD, T)
        zT = sgA
        ybT = at_(14336, MB_H // 2, T)
        assert o <= 49408, o
        hn = S1.rearrange("p a b -> p (a b)").rearrange("p (t d) -> p t d", t=TT)
        PT0 = bias_rows.rearrange("p a b -> p (a b)")[:, 0:2048].rearrange("p (h q) -> p h q", h=MB_H)
        PT1 = bias_rows.rearrange("p a b -> p (a b)")[:, 2048:3072].rearrange("p (h q) -> p h q", h=MB_H)
        relbb = ybT.rearrange("p a b -> p (a b)").rearrange("p (h q) -> p h q", h=MB_H)
        hgtmp = sgA.rearrange("p a b -> p (a b)")[:, HG_H * T:].rearrange("p (t q) -> p t q", t=TT)
        restart = sgA.rearrange("p a b -> p (a b)")[:, 0:HG_H * T]
        hnM = at_(46336, TT, D)
        hnF = at_(26624, TT, D)
        memT = at_(16384, KD, T)
        osb = E_.rearrange("p (t h e) -> p t h e", t=TT, h=HG_H)
        osq = DI.rearrange("p (t h e) -> p t h e", t=TT, h=HG_H)
        qxT = at_(18432, KD, T)
        CS = at_(20480, TT, X_H, T)
        CPT = at_(22528, TT, X_H, T)
        oxT = at_(24576, KD, T)
        qhT = at_(16384, 2 * PH, T)
        subT = at_(20480, 2 * PH, NKEY)
        sc = at_(22528, TT, 2 * PH, NKEY)
        gate = at_(0, NT, T)
        uraw = [at_(32768 + D * s, D) for s in range(2)]
        vraw = [at_(34816 + D * s, D) for s in range(2)]
        actr = [at_(36864 + T * s, T) for s in range(2)]
        IJW = at_(37376, 3, T)
        apart = at_(36864, TOK, NKEY)
        rows_ = [at_(47360 + 1024 * s, 2, TOK, NKEY) for s in range(ROWS)]
        fgain = at_(32768, D)
        yfin = at_(0, TT, D)
        assert EARLY * T <= 10240
        sc2 = at_(26624, TT, 2 * PH, NKEY)
        cand = at_(10240, PH, PK * PK)
        cand2 = at_(12288, PH, PK * PK)
        eq = at_(14336, PH * PK, PK)
        eq2 = at_(16384, PH * PK, PK)
        at_small = 18432
        sv = at_(at_small, TT, 2 * PH, PK)
        si = at_(at_small + 512, TT, 2 * PH, PK)
        sif = at_(at_small + 1024, TT, 2 * PH, PK)
        fv = at_(at_small + 1536, TT, PH, PK)
        pos = at_(at_small + 1792, TT, PH, PK)
        ab = at_(at_small + 2048, 2, PH * PK)
        abf = at_(at_small + 2304, 2, PH * PK)
        rIJW = at_(at_small + 2560, 3, TT, P)
        wsum = at_(at_small + 3328, TT, PH)

        bias_d = nc.dram_tensor("bias_rows_dram", (MB_H, P, ROW), f32, kind="Internal")

        gb_ = [ctx.enter_context(nc.psum_tensor(f"proj{i}", [P, 512], f32)) for i in range(NG)]
        aux = [ctx.enter_context(nc.psum_tensor(f"aux{i}", [P, 1024], f32)) for i in range(2)]

        sems = {}

        def S(name):
            if name not in sems:
                sems[name] = ctx.enter_context(nc.semaphore(name))
            return sems[name]

        w_here = [S(f"w_here{s}") for s in range(RAW)]
        w_high, w_low, w_used = S("w_high"), S("w_low"), S("w_used")
        u_here = [S(f"u_here{s}") for s in range(4)]
        v_here = [S(f"v_here{s}") for s in range(4)]
        x_here = [S(f"x_here{t}") for t in range(TT)]
        mem_here, const_here, masks_here = S("mem_here"), S("const_here"), S("masks_here")
        aux_full = S("aux_full")
        u_high, u_low, u_used = S("u_high"), S("u_low"), S("u_used")
        v_high, v_low, v_used = S("v_high"), S("v_low"), S("v_used")
        tile_out, product, coef_done = S("tile_out"), S("product"), S("coef_done")
        h_high, h_low, injected, weighted, early_gated = map(S, ["h_high", "h_low", "injected", "weighted", "early_gated"])
        onehots, spread_done, spread_out = S("onehots_ready"), S("spread_done"), S("spread_out")
        for _, r, _ in aux_uses:
            S(r)
        for r, _ in bank_reader:
            S(r)
        for n in ["bias_rows_out", "bias_here", "sub_here", "fgain_here", "out_done", "cleared", "restart_ones",
                  "restart_ready", "neg_ready", "relbb_ready", "ssq", "var", "root", "hn_ready",
                  "low_ready", "low_exp", "k_ready", "lf_ready", "b_ready", "diff", "decay", "QK",
                  "mb_max", "mb_exp", "mb_prob", "silu_ready", "sig_ready", "z_ready", "x_new",
                  "o_ready", "x_max", "x_prob", "w_diff", "w_exp", "rIJW_ready", "y_ready",
                  "dve_chain", "hg_exp", "coef_high", "apart_ready", "first_ready"]:
            S(n)
        block = ctx.enter_context(nc.Block())

        def full(eng, name, b=-1):
            sem_, count = bank_full[bank_no[name] + b % banks_of[chunks[chunk_no[name]][1]]]
            eng.wait_ge(S(sem_), count)

        @block.sync
        def _(sp):
            for t in range(TT):
                sp.dma_start(x_sb[:, t, :], x[t * P:(t + 1) * P, :]).then_inc(x_here[t], 16)
            sp.wait_ge(S("neg_ready"), 1)
            sp.dma_start(relb[0:BUCKETS, :], rel_bias).then_inc(const_here, 16)
            sp.dma_start(onehot_sb[:, :], onehot).then_inc(const_here, 16)
            sp.dma_start(ident[:, :], masks[len(LEVELS)]).then_inc(const_here, 16)
            sp.dma_start(gain_sb[:, :, :], gains).then_inc(const_here, 16)
            sp.dma_start(hgn_sb[:, :], hg_norm).then_inc(const_here, 16)
            sp.dma_start(low_sb[:, :, :], hg_lower).then_inc(const_here, 16)
            sp.dma_start(iota_sb[:, :], iota).then_inc(const_here, 16)

            def load_w(n, k, again):
                if again:
                    sp.wait_ge(w_low, 8 * n + k - RAW + 1)
                sp.dma_start(wraw[k], first_pieces[bass.ds(8 * n + k, 1)].rearrange("o p c -> (o p) c")).then_inc(w_here[k], 16)
            for k in range(8):
                load_w(0, k, False)
            sp.dma_start(mem_sb, mem.rearrange("(t p) d -> p t d", p=P)).then_inc(mem_here, 16)
            sp.dma_start(mask_sb, masks[0:len(LEVELS)].rearrange("l s t -> s l t")).then_inc(masks_here, 16)
            for k in range(8):
                load_w(1, k, True)
            sp.wait_ge(S("bias_read"), 4)
            sp.dma_start(bias_d.ap().rearrange("h p r -> p h r"), bias_rows).then_inc(S("bias_rows_out"), 16)
            for k in range(8):
                load_w(2, k, True)
            sp.wait_ge(S("bias_rows_out"), 16)
            skew = bass.AP(tensor=bias_d, offset=P - 1, ap=[[ROW - 1, P], [P * ROW, MB_H], [1, T]])
            sp.dma_start(biasB, skew).then_inc(S("bias_here"), 16)
            with sp.Fori(3, NF // 8) as r:
                for k in range(8):
                    load_w(r, k, True)
            def load_u(src, n, s, c):
                h = slice(HALF * c, HALF * (c + 1))
                sp.dma_start(uraw[s][:, h], src[n].rearrange("o p c -> (o p) c")[:, h]).then_inc(u_here[2 * s + c], 16)

            def load_v(n, s, c):
                h = slice(HALF * c, HALF * (c + 1))
                sp.dma_start(vraw[s][:, h], peer_v[n].rearrange("o p d -> (o p) d")[:, h]).then_inc(v_here[2 * s + c], 16)

            def more_u(src, n, s, before):
                for c in range(2):
                    sp.wait_ge(u_low, 2 * (n + before) - 3 + c)
                    load_u(src, bass.ds(n, 1), s, c)
            sp.wait_ge(aux_full, aux_no["PTc"] + 1)
            for s in range(2):
                for c in range(2):
                    load_u(pieces, slice(s, s + 1), s, c)
            with sp.Fori(1, PTILES // 2) as r:
                for s in range(2):
                    more_u(pieces, 2 * r + s, s, 0)
            sp.wait_ge(aux_full, aux_no["CV1"] + 1)
            sp.dma_start(subT, subkeys).then_inc(S("sub_here"), 16)
            with sp.Fori(0, QT // 2) as r:
                for s in range(2):
                    more_u(peer_query, 2 * r + s, s, PTILES)

            def more_v(n, s):
                for c in range(2):
                    sp.wait_ge(v_low, 2 * n - 3 + c)
                    load_v(bass.ds(n, 1), s, c)
            with sp.Fori(0, (EARLY + 4) // 2) as r:
                for s in range(2):
                    more_u(peer_u, 2 * r + s, s, PTILES + QT)
            sp.wait_ge(injected, 1)
            for s in range(2):
                for c in range(2):
                    load_v(slice(s, s + 1), s, c)
            with sp.Fori(1, (EARLY + 2) // 2) as r:
                for s in range(2):
                    more_v(2 * r + s, s)
            with sp.Fori((EARLY + 2) // 2, (NT - 2) // 2) as r:
                for s in range(2):
                    more_u(peer_u, 2 * r + 2 + s, s, PTILES + QT)
                    more_v(2 * r + s, s)
            for n in range(NT - 2, NT):
                for c in range(2):
                    sp.wait_ge(v_low, 2 * n - 3 + c)
                    load_v(slice(n, n + 1), n % 2, c)
            sp.wait_ge(u_low, 2 * (PTILES + QT + NT))
            sp.dma_start(fgain, ln_final.partition_broadcast(P)).then_inc(S("fgain_here"), 16)
            for t in range(TT):
                sp.wait_ge(S("y_ready"), t + 1)
                sp.dma_start(out[t * P:(t + 1) * P, :], yfin[:, t, :]).then_inc(S("out_done"), 16)
            sp.wait_ge(S("out_done"), 16 * TT)

        @block.gpsimd
        def _(pool):
            nc.gpsimd.memset(relb[:, :], NEG).then_inc(S("neg_ready"), 1)
            nc.gpsimd.memset(restart, 1.0).then_inc(S("restart_ones"), 1)
            for b in (QE[0], QE[1], KE[0], KE[1], ATd):
                nc.gpsimd.memset(b, 0.0).then_inc(S("cleared"), 1)
            pool.wait_ge(S("restart_ones"), 1)
            nc.gpsimd.memset(restart.rearrange("p (n c) -> p n c", c=CHUNK)[:, :, 0:1], 0.0).then_inc(S("restart_ready"), 1)

            def low(k, h):
                pool.wait_ge(u_high, h + 1)
                nc.gpsimd.tensor_tensor(Us[:, k, 1, :], uraw[k // 2][:, HALF * (k % 2):HALF * (k % 2 + 1)],
                                        Us[:, k, 0, :].bitcast(f32), ALU.subtract).then_inc(u_low, 1)
            with pool.Fori(0, NF // 8) as r:
                for k in range(8):
                    pool.wait_ge(w_high, 8 * r + k + 1)
                    nc.gpsimd.tensor_tensor(Ws[:, k % 4, 1], wraw[k], Ws[:, k % 4, 0].bitcast(f32), ALU.subtract).then_inc(w_low, 1)
            with pool.Fori(0, (PTILES + QT + EARLY + 2) // 2) as r:
                for k in range(4):
                    low(k, 4 * r + k)

            def weigh_rows(g, q, tok):
                pool.wait_ge(onehots, q + 1)
                rows = rows_[g][:, 1]
                nc.gpsimd.tensor_tensor(rows, rows, IJW[:, 2, tok].unsqueeze(2).to_broadcast([P, TOK, NKEY]),
                                        ALU.mult).then_inc(weighted, 1)
            with pool.Fori(0, T // TOK // ROWS) as r:
                for g in range(ROWS):
                    weigh_rows(g, ROWS * r + g, bass.ds(TOK * (ROWS * r + g), TOK))
            with pool.Fori((PTILES + QT + EARLY + 2) // 2, (PTILES + QT + NT) // 2) as r:
                for k in range(4):
                    low(k, 4 * r + k)

        @block.tensor
        def _(pe):
            def aux_open(name):
                n = aux_no[name]
                if n >= 2:
                    pe.wait_ge(S(aux_uses[n - 2][1]), aux_uses[n - 2][2])
                return aux[n % 2]

            def mm(o_, l, r, start, stop):
                return nc.tensor.matmul(o_, l, r, start=start, stop=stop)

            def three(ps, a, b, start, stop):
                for i, (x, y) in enumerate(((0, 0), (0, 1), (1, 0))):
                    last = mm(ps, a(x), b(y), start and i == 0, stop and i == 2)
                return last

            def project(name, act, parts, pieces=range(8)):
                n, form = chunk_no[name], chunks[chunk_no[name]][1]
                slots, low, used = (Ws, w_low, w_used) if n < len(FIRST) else (Us, u_low, u_used)
                for i in pieces:
                    h = 8 * (n if n < len(FIRST) else n - len(FIRST)) + i
                    w = slots[:, h % 4]
                    for b in {"T": [i // 4] if i % 4 == 0 else [], "U": [i // 2] if i % 2 == 0 else [], "N": [0, 1] if i == 0 else []}[form]:
                        g = bank_no[name] + b
                        if g >= NG:
                            pe.wait_ge(S(bank_reader[g - NG][0]), bank_reader[g - NG][1])
                    pe.wait_ge(low, h + 1)
                    if form == "N":
                        pe.wait_ge(h_low, split_no[parts[i]])
                        for t in range(TT):
                            last = three(gb_[(bank_no[name] + t) % NG][:, :], lambda x: act[:, x, i, t * P:(t + 1) * P],
                                         lambda y: w[:, y, :], i == 0, i == 7)
                    else:
                        c, k0 = (i // 2, 4 * (i % 2)) if form == "T" else (i, 0)
                        ps = gb_[(bank_no[name] + c // 2) % NG][:, (c % 2) * T:(c % 2 + 1) * T]
                        pe.wait_ge(h_low, split_no[parts[k0]])
                        for k in range(4):
                            last = three(ps, lambda x: w[:, x, k * P:(k + 1) * P], lambda y: act[:, y, k0 + k, :],
                                         k0 + k == 0, k == 3 and (form == "U" or k0 == 4))
                    last.then_inc(used, 1)

            def turn(name, src, ks):
                ps = aux_open(name)
                for i, k in enumerate(ks):
                    for t in range(TT):
                        last = nc.tensor.transpose(ps[:, i * T + t * P:i * T + (t + 1) * P],
                                                   src[:, t, k * P:(k + 1) * P], ident[:, :])
                last.then_inc(aux_full, 1)

            pe.wait_ge(const_here, 16 * 7)
            pe.wait_ge(S("hn_ready"), 2)
            turn("tx0", hn, range(0, 4))
            turn("tx1", hn, range(4, 8))
            x_parts = ["tx0"] * 4 + ["tx1"] * 4
            project("hf0", xTs, x_parts)
            pe.wait_ge(S("relbb_ready"), 1)
            for n in range(4):
                ps = aux_open(f"bias{n}")
                for j in range(2):
                    last = mm(ps[:, 512 * j:512 * j + ROW], relbb[0:BUCKETS + 1, 2 * n + j, :],
                              onehot_sb[:, :], True, True)
                last.then_inc(aux_full, 1)
            project("hq0", xTs, x_parts)
            project("mq0", xTs, x_parts)

            def level(L):
                ps = aux_open(f"L{L}")
                if L == "diag":
                    pe.wait_ge(S("hq_read"), 2)
                    pe.wait_ge(S("k_ready"), 1)
                    q, k = hqT, kT
                else:
                    i = (LEVELS + [128]).index(L)
                    pe.wait_ge(S("QK"), i + 1)
                    i %= 2
                    q, k = QE[i], KE[i]
                for h in range(HG_H):
                    if L == 128:
                        last = mm(ps[:, h * P:(h + 1) * P], k[:, h, 0:P], q[:, h, P:T], True, True)
                    else:
                        for t in range(TT):
                            b = h * TT + t
                            last = mm(ps[:, b * P:(b + 1) * P], k[:, h, t * P:(t + 1) * P],
                                      q[:, h, t * P:(t + 1) * P], True, True)
                last.then_inc(aux_full, 1)

            level("diag")
            project("mk0", xTs, x_parts)
            level(1)
            pe.wait_ge(S("mq_read"), 2)
            pe.wait_ge(S("mk_read"), 2)
            for name, t, heads, nk in (("S0", 0, range(8), P), ("S1a", 1, range(4), T), ("S1b", 1, range(4, 8), T)):
                ps = aux_open(name)
                for i, h in enumerate(heads):
                    r = slice((h % 2) * MB_D, (h % 2 + 1) * MB_D)
                    c = 512 * (h % 2) + (i // 2) * nk
                    last = mm(ps[:, c:c + nk], mqT[r, h // 2, t * P:(t + 1) * P],
                              mkT[r, h // 2, 0:nk], True, True)
                last.then_inc(aux_full, 1)
            project("hi0", xTs, x_parts)
            level(2)
            project("hg0", xTs, x_parts)
            level(4)
            project("mv0", xTs, x_parts)
            level(8)
            project("ga0", xTs, x_parts)
            level(16)
            project("ga1", xTs, x_parts)
            level(32)
            pe.wait_ge(S("mb_prob"), 2)
            for name, items in (("PTa", [(S0, S1, h) for h in range(4)]), ("PTb", [(S0, S1, h) for h in range(4, 8)])):
                ps = aux_open(name)
                for i, (p0, p1, h) in enumerate(items):
                    nc.tensor.transpose(ps[:, i * T:i * T + P], p0[:, h, :], ident[:, :])
                    last = nc.tensor.transpose(ps[:, i * T + P:i * T + T], p1[:, h, 0:P], ident[:, :])
                last.then_inc(aux_full, 1)
            ps = aux_open("PTc")
            for h in range(MB_H):
                last = nc.tensor.transpose(ps[:, h * P:(h + 1) * P], S1[:, h, P:T], ident[:, :])
            last.then_inc(aux_full, 1)
            level(64)
            level(128)
            project("gb0", xTs, x_parts)
            pe.wait_ge(S("PT_read"), 3)
            pe.wait_ge(S("mv_read"), 2)
            ps = aux_open("PV")
            for h in range(MB_H):
                r = slice((h % 2) * MB_D, (h % 2 + 1) * MB_D)
                c = (h // 2) * T
                mm(ps[r, c:c + T], mv_sb[:, 0, h * MB_D:(h + 1) * MB_D], PT0[:, h, :], True, False)
                last = mm(ps[r, c + P:c + T], mv_sb[:, 1, h * MB_D:(h + 1) * MB_D], PT1[:, h, :], False, True)
            last.then_inc(aux_full, 1)
            pe.wait_ge(S("far_read"), 1)
            pe.wait_ge(S("level_read"), 8)
            pe.wait_ge(S("hi_read"), 2)
            ps = aux_open("O")
            for h in range(HG_H):
                e = slice(h * HG_D, (h + 1) * HG_D)
                mm(ps[:, e], ATd[:, h * TT, :], hi_sb[:, 0, e], True, True)
                e1 = slice(512 + h * HG_D, 512 + (h + 1) * HG_D)
                mm(ps[:, e1], AT01[:, h, :], hi_sb[:, 0, e], True, False)
                last = mm(ps[:, e1], ATd[:, h * TT + 1, :], hi_sb[:, 1, e], False, True)
            last.then_inc(aux_full, 1)
            pe.wait_ge(S("hn_ready"), 4)
            turn("tm0", hnM, range(0, 4))
            turn("tm1", hnM, range(4, 8))
            project("gb1", xTs, x_parts)
            pe.wait_ge(S("o_ready"), 1)
            ps = aux_open("TY")
            for h in range(HG_H):
                for t in range(TT):
                    last = nc.tensor.transpose(ps[:, h * T + t * P:h * T + (t + 1) * P], osb[:, t, h, :], ident[:, :])
            last.then_inc(aux_full, 1)
            mem_parts = ["mem0"] * 4 + ["mem1"] * 4
            project("kx0", hTs, mem_parts)
            project("upa0", As[:, :, 0:4], ["ya"] * 4)
            project("upb0", As[:, :, 4:8], ["yb"] * 4)
            project("kx1", hTs, mem_parts)
            z_parts = [f"z{k // 2}" for k in range(8)]
            project("out0", As, z_parts)
            project("out1", As, z_parts)
            project("vx0", hTs, mem_parts, range(0, 4))
            pe.wait_ge(S("hn_ready"), 6)
            turn("tc0", hnF, range(0, 4))
            turn("tc1", hnF, range(4, 8))
            project("vx0", hTs, mem_parts, range(4, 8))
            for c in range(2):
                project(f"qx{c}", xTs, ["tc0"] * 4 + ["tc1"] * 4)
            project("vx1", hTs, mem_parts, range(0, 2))
            pe.wait_ge(S("qx_read"), 4)
            pe.wait_ge(S("kx_read"), 4)
            for t in range(TT):
                ps = aux_open(f"CS{t}")
                for h in range(X_H):
                    for k in range(2):
                        last = mm(ps[:, h * T:(h + 1) * T], qxT[:, 2 * h + k, t * P:(t + 1) * P],
                                  kxT[:, 2 * h + k, :], k == 0, k == 1)
                last.then_inc(aux_full, 1)
            project("vx1", hTs, mem_parts, range(2, 6))
            pe.wait_ge(S("x_prob"), 2)
            for m in range(TT):
                ps = aux_open(f"CT{m}")
                for h in range(X_H):
                    for t in range(TT):
                        last = nc.tensor.transpose(ps[:, h * T + t * P:h * T + (t + 1) * P],
                                                   CS[:, t, h, m * P:(m + 1) * P], ident[:, :])
                last.then_inc(aux_full, 1)
            pe.wait_ge(S("CPT_read"), 2)
            for c in range(2):
                if c:
                    project("vx1", hTs, mem_parts, range(6, 8))
                pe.wait_ge(S("vx_read"), 2 * c + 2)
                ps = aux_open(f"CV{c}")
                for j in range(4):
                    f = 4 * c + j
                    for m in range(TT):
                        last = mm(ps[:, j * T:(j + 1) * T], vx[:, m, f * P:(f + 1) * P], CPT[:, m, f // 2, :], m == 0, m == 1)
                last.then_inc(aux_full, 1)
            for c in range(2):
                project(f"wo{c}", As, ["ox0"] * 4 + ["ox1"] * 4)
            pe.wait_ge(S("hn_ready"), 8)
            turn("tf0", hnF, range(0, 4))
            turn("tf1", hnF, range(4, 8))
            def acts(k, n, reused, first=False):
                if reused:
                    pe.wait_ge(tile_out, n - 1)
                ps = gb_[2 + k][:, 0:T]
                for a in range(2):
                    if first:
                        pe.wait_ge(h_low, split_no[f"tf{a}"])
                    slot = 2 * k + a
                    pe.wait_ge(u_low, 2 * (n + PTILES) + a + 1)
                    for c in range(4):
                        u = Us[:, slot, :, c * P:(c + 1) * P]
                        hk = hTs[:, :, 4 * a + c, :]
                        mm(ps, u[:, 0], hk[:, 0], a == 0 and c == 0, False)
                        mm(ps, u[:, 0], hk[:, 1], False, False)
                        last = mm(ps, u[:, 1], hk[:, 0], False, a == 1 and c == 3)
                    last.then_inc(u_used, 1)

            for k in range(2):
                acts(k, k, False, k == 0)
            with pe.Fori(1, QT // 2) as r:
                for k in range(2):
                    acts(k, 2 * r + k, True)
            pe.wait_ge(tile_out, QT)
            pe.wait_ge(S("sub_here"), 16)
            for n in range(4):
                ps = aux_open(f"PS{n}")
                t = n // 2
                for j in range(8):
                    hc = 8 * (n % 2) + j
                    last = mm(ps[:, j * P:(j + 1) * P], qhT[:, hc, t * P:(t + 1) * P], subT[:, hc, :], True, True)
                last.then_inc(aux_full, 1)
            with pe.Fori(QT // 2, (QT + EARLY) // 2) as r:
                for k in range(2):
                    acts(k, 2 * r + k, True)
            pe.wait_ge(S("rIJW_ready"), 6)
            ps = aux_open("TR")
            for a in range(3):
                for t in range(TT):
                    last = nc.tensor.transpose(ps[:, a * T + t * P:a * T + (t + 1) * P], rIJW[:, a, t, :], ident[:, :])
            last.then_inc(aux_full, 1)
            y = [[aux[t][:, 512 * c:512 * c + 512] for c in range(2)] for t in range(TT)]
            pe.wait_ge(S("IJW_ready"), 1)
            for t in range(TT):
                for c in range(2):
                    last = nc.tensor.matmul(y[t][c], ident[:, :], x_sb[:, t, 512 * c:512 * (c + 1)],
                                            start=True, stop=False, skip_group_check=True)
            last.then_inc(injected, 1)

            def spread(g, q, firsts):
                pe.wait_ge(weighted, q + 1)
                if g == 0:
                    pe.wait_ge(S("first_ready"), firsts)
                for j in range(TOK):
                    last = mm(gb_[g][:, j * P:(j + 1) * P], rows_[g][:, 1, j, :], rows_[g][:, 0, j, :], True, True)
                last.then_inc(spread_done, 1)

            def spread_again(g, q, firsts):
                pe.wait_ge(early_gated, q - ROWS + 1)
                spread(g, q, firsts)
            assert ROWS == NG
            for g in range(ROWS):
                spread(g, g, 1)
            with pe.Fori(1, T // TOK // ROWS) as r:
                for g in range(ROWS):
                    spread_again(g, ROWS * r + g, r + 1)

            def outs(k, n, final):
                pe.wait_ge(coef_done, n + 1)
                for c in range(2):
                    pe.wait_ge(v_low, 2 * n + c + 1)
                    v = Vs[:, 2 * k + c]
                    for t in range(TT):
                        w = Cs[:, k, :, t * P:(t + 1) * P]
                        for i, (cp, vp) in enumerate(((0, 0), (0, 1), (1, 0))):
                            last = nc.tensor.matmul(y[t][c], w[:, cp], v[:, vp], start=False, stop=final and i == 2,
                                                    skip_group_check=True)
                    last.then_inc(v_used, 1)
            with pe.Fori(0, (EARLY - 2) // 2) as r:
                for k in range(2):
                    outs(k, 2 * r + k, False)
            with pe.Fori((EARLY - 2) // 2, (NT - 2) // 2) as r:
                for k in range(2):
                    acts(k, 2 * r + 2 + k + QT, True)
                    outs(k, 2 * r + k, False)
            for k in range(2):
                outs(k, NT - 2 + k, k == 1)

        @block.scalar
        def _(act):
            def bank(name, b):
                g = bank_no[name] + b
                full(act, name, b)
                return gb_[g % NG], S(bank_reader[g][0])

            def copy_banks(names, dst, func=ACT.Copy, scale=1.0):
                for i, (n, b) in enumerate([(n, b) for n in names for b in range(2)]):
                    ps, read = bank(n, b)
                    nc.scalar.activation(dst(i), ps[:, :], func, scale=scale).then_inc(read, 1)

            def aux_take(name):
                act.wait_ge(aux_full, aux_no[name] + 1)
                return aux[aux_no[name] % 2]

            def aux_copy(name, dst, view=lambda p: p[:, :]):
                nc.scalar.activation(dst, view(aux_take(name)), ACT.Copy).then_inc(S(aux_uses[aux_no[name]][1]), 1)

            def flat(v):
                names = "abc"[:len(v.shape) - 1]
                return v.rearrange(f"p {' '.join(names)} -> p ({' '.join(names)})")

            def halves(v):
                return lambda i: flat(v)[:, 512 * i:512 * (i + 1)]

            def ssq(src, junk_, n, here=None):
                for t in range(TT):
                    if here is not None:
                        act.wait_ge(here[t], 16)
                    nc.scalar.activation(junk_[:, t, :], src[:, t, :], ACT.Square,
                                         accum_out=stat[:, n, t:t + 1]).then_inc(S("ssq"), 1)

            def ssq_added(junk_, n, before, at):
                for c in range(2):
                    if c:
                        highs(at)
                    act.wait_ge(S("x_new"), before + c + 1)
                    for t in range(TT):
                        h = slice(HALF * c, HALF * (c + 1))
                        nc.scalar.activation(junk_[:, t, h], x_sb[:, t, h], ACT.Square,
                                             accum_out=stat[:, n, 2 * c + t:2 * c + t + 1]).then_inc(S("ssq"), 1)

            def root(n, w, cnt):
                act.wait_ge(S("var"), cnt)
                nc.scalar.activation(stat[:, n, 8:8 + w], stat[:, n, 8:8 + w], ACT.Sqrt).then_inc(S("root"), 1)

            nc.scalar.preload_act_table(ACT.Sqrt)
            def high_u(k, h, load, again):
                act.wait_ge(u_here[k], load)
                if again:
                    act.wait_ge(u_used, h - 3)
                nc.scalar.activation(Us[:, k, 0, :], uraw[k // 2][:, HALF * (k % 2):HALF * (k % 2 + 1)], ACT.Copy).then_inc(u_high, 1)
            made = [0]

            def highs(n):
                for h in range(made[0], n):
                    high_u(h % 4, h, 16 * (h // 4 + 1), h >= 4)
                made[0] = n

            made_first = [0]

            def highs_first(n):
                for h in range(made_first[0], n):
                    act.wait_ge(w_here[h % RAW], 16 * (h // RAW + 1))
                    if h >= 4:
                        act.wait_ge(w_used, h - 3)
                    nc.scalar.activation(Ws[:, h % 4, 0], wraw[h % RAW], ACT.Copy).then_inc(w_high, 1)
                made_first[0] = n

            def high_act(dst, src):
                nc.scalar.activation(flat(dst), flat(src), ACT.Copy).then_inc(h_high, 1)

            ssq(x_sb, hn, 0, x_here)
            root(0, 2, 1)
            highs_first(4)
            for i in range(2):
                act.wait_ge(S("hT_ready"), 1 + i)
                high_act(xTs[:, 0, 4 * i:4 * i + 4], hT[:, 4 * i:4 * i + 4])
            act.wait_ge(mem_here, 16)
            ssq(mem_sb, hnM, 1)
            highs_first(6)
            root(1, 2, 2)
            nc.scalar.preload_act_table_set("natural_log_exp_and_others")
            act.wait_ge(S("low_ready"), 1)
            nc.scalar.activation(tiny[:, 0:2, :], tiny[:, 0:2, :], ACT.Exp).then_inc(S("low_exp"), 1)
            highs_first(12)
            copy_banks(["hf0"], halves(DI.rearrange("p (a b) -> p a b", a=HG_H)), ACT.Exp, -1.0)
            for n in range(4):
                aux_copy(f"bias{n}", bias_rows[:, 2 * n:2 * n + 2, :],
                         lambda p: p[:, :].rearrange("p (h c) -> p h c", h=2)[:, :, 0:ROW])
            highs_first(20)
            copy_banks(["hq0"], halves(hqT))
            act.wait_ge(S("k_ready"), 1)
            nc.scalar.activation(E_, E_, ACT.Ln).then_inc(S("lf_ready"), 1)
            highs_first(28)
            copy_banks(["mq0"], halves(mqT))

            def decay(i):
                act.wait_ge(S("diff"), 2 * i + 2 if i < len(LEVELS) else 2 * i + 4)
                if i >= 1:
                    act.wait_ge(S("QK"), i)
                nc.scalar.activation(E_, DI, ACT.Exp).then_inc(S("decay"), 1)
            highs_first(32)
            decay(0)
            highs_first(36)
            copy_banks(["mk0"], halves(mkT))
            decay(1)
            highs_first(38)
            act.wait_ge(S("mb_max"), 2)
            for t, s_ in ((0, S0), (1, S1)):
                for h in range(MB_H):
                    nc.scalar.activation(s_[:, h, :], s_[:, h, :], ACT.Exp, bias=smx[:, t, h:h + 1],
                                         accum_out=smx[:, 2 + t, h:h + 1]).then_inc(S("mb_exp"), 1)
                    if h % 3 == 2:
                        highs_first(made_first[0] + 1)
            decay(2)
            highs_first(44)
            copy_banks(["hi0"], halves(hi_sb))
            highs_first(48)
            decay(3)
            highs_first(52)
            for b in range(2):
                g = bank_no["hg0"] + b
                full(act, "hg0", b)
                nc.scalar.activation(hgtmp[:, b, :], gb_[g % NG][:, :], ACT.Exp, scale=-1.0).then_inc(S("hg_exp"), 1)
                nc.scalar.activation(hg_sb[:, b, :], gb_[g % NG][:, :], ACT.Copy).then_inc(S("hg_read"), 1)
            highs_first(60)
            decay(4)
            copy_banks(["mv0"], halves(mv_sb))
            highs_first(64)
            decay(5)
            highs_first(68)
            copy_banks(["ga0"], halves(sgA[:, 0:4, :]), ACT.Exp, -1.0)
            highs_first(72)
            decay(6)
            highs_first(74)
            decay(7)
            highs_first(76)
            act.wait_ge(S("silu_ready"), 1)
            copy_banks(["ga1"], halves(sgA[:, 4:8, :]), ACT.Exp, -1.0)
            aux_copy("PTa", flat(PT0[:, 0:4, :]))
            aux_copy("PTb", flat(PT0[:, 4:8, :]))
            aux_copy("PTc", flat(PT1))
            aux_copy("L128", flat(AT01), lambda p: p[:, 0:HG_H * P])
            highs_first(NF)
            act.wait_ge(S("hn_ready"), 4)
            highs(4)
            copy_banks(["gb0"], halves(sgB[:, 0:4, :]), ACT.Exp, -1.0)
            aux_copy("PV", flat(ybT))
            aux_copy("O", osb.rearrange("p t h e -> p (t h e)"))
            root(2, 8, 3)
            act.wait_ge(S("ybT_ready"), 1)
            high_act(As[:, 0, 4:8], ybT)
            highs(5)
            for i in range(2):
                act.wait_ge(S("hT_ready"), 3 + i)
                high_act(hTs[:, 0, 4 * i:4 * i + 4], memT[:, 4 * i:4 * i + 4])
                highs(6 + i)
            highs(12)
            copy_banks(["gb1"], halves(sgB[:, 4:8, :]), ACT.Exp, -1.0)
            highs(14)
            act.wait_ge(S("yaT_ready"), 1)
            high_act(As[:, 0, 0:4], yaT)
            highs(20)
            copy_banks(["kx0"], halves(kxT[:, 0:4, :]))
            highs(36)
            for b in range(4):
                act.wait_ge(S("z_ready"), b + 1)
                high_act(As[:, 0, 2 * b:2 * b + 2], zT[:, 2 * b:2 * b + 2])
            highs(44)
            copy_banks(["kx1"], halves(kxT[:, 4:8, :]))
            highs(52)

            def copy_vx(c):
                for t in range(TT):
                    ps, read = bank(f"vx{c}", t)
                    nc.scalar.activation(vx[:, t, 512 * c:512 * (c + 1)], ps[:, :], ACT.Copy).then_inc(read, 1)
            nc.scalar.preload_act_table(ACT.Sqrt)
            ssq_added(hnF, 3, 0, 60)
            root(3, 2, 4)
            highs(64)
            for i in range(2):
                act.wait_ge(S("hT_ready"), 5 + i)
                high_act(xTs[:, 0, 4 * i:4 * i + 4], hT[:, 4 * i:4 * i + 4])
            highs(68)
            copy_vx(0)
            highs(76)
            copy_banks(["qx0"], halves(qxT[:, 0:4, :]))
            highs(84)
            copy_banks(["qx1"], halves(qxT[:, 4:8, :]))
            highs(86)
            for t in range(TT):
                act.wait_ge(S("x_max"), t + 1)
                ps = aux_take(f"CS{t}")
                for h in range(X_H):
                    nc.scalar.activation(CS[:, t, h, :], ps[:, h * T:(h + 1) * T], ACT.Exp, bias=smx[:, 4, 4 * t + h:4 * t + h + 1],
                                         scale=X_D ** -0.5, accum_out=smx[:, 5, 4 * t + h:4 * t + h + 1]).then_inc(S("xexp"), 1)
            highs(88)
            for m in range(TT):
                aux_copy(f"CT{m}", flat(CPT[:, m]))
            for c in range(2):
                if c:
                    highs(90)
                    copy_vx(1)
                    highs(92)
                aux_copy(f"CV{c}", flat(oxT[:, 4 * c:4 * c + 4, :]))
                act.wait_ge(S("oxT_ready"), c + 1)
                high_act(As[:, 0, 4 * c:4 * c + 4], oxT[:, 4 * c:4 * c + 4])
            highs(100)
            nc.scalar.preload_act_table(ACT.Sqrt)
            ssq_added(hnF, 4, 2, 106)
            root(4, 2, 5)
            nc.scalar.preload_act_table(ACT.Gelu_apprx_tanh)
            highs(NP + 4)
            for i in range(2):
                act.wait_ge(S("hT_ready"), 7 + i)
                high_act(hTs[:, 0, 4 * i:4 * i + 4], hT[:, 4 * i:4 * i + 4])

            def take_tile(k, m, dst, func=ACT.Gelu_apprx_tanh):
                act.wait_ge(u_used, 2 * (m + PTILES) + 2)
                nc.scalar.activation(dst, gb_[2 + k][:, 0:T], func).then_inc(tile_out, 1)

            def early(r, before, out_, func):
                for k in range(2):
                    high_u(2 * k, 4 * r + 2 * (before + PTILES) + 4 + 2 * k, 16 * r + 8 * (before + PTILES) + 32, True)
                    take_tile(k, 2 * r + k + before, out_[:, bass.ds(2 * r + k, 1), :].rearrange("p o t -> p (o t)"), func)
                    high_u(2 * k + 1, 4 * r + 2 * (before + PTILES) + 5 + 2 * k, 16 * r + 8 * (before + PTILES) + 32, True)

            with act.Fori(0, QT // 2) as r:
                early(r, 0, qhT, ACT.Copy)
            for n in range(4):
                aux_copy(f"PS{n}", flat(sc[:, n // 2, 8 * (n % 2):8 * (n % 2) + 8, :]))
            done = 0
            for t in range(TT):
                with act.Fori(done // 2, EXP_AT[t] // 2) as r:
                    early(r, QT, gate, ACT.Gelu_apprx_tanh)
                done = EXP_AT[t]
                act.wait_ge(S("w_diff"), t + 1)
                nc.scalar.activation(flat(fv[:, t]), flat(fv[:, t]), ACT.Exp).then_inc(S("w_exp"), 1)
                nc.scalar.preload_act_table(ACT.Gelu_apprx_tanh)
            with act.Fori(done // 2, EARLY // 2) as r:
                early(r, QT, gate, ACT.Gelu_apprx_tanh)

            def spread_copy(g, q):
                act.wait_ge(spread_done, q + 1)
                nc.scalar.activation(gate[:, EARLY:NT, bass.ds(TOK * q, TOK)],
                                     gb_[g][:, :].rearrange("p (t i) -> p i t", t=TOK)[:, EARLY:NT, :], ACT.Copy).then_inc(spread_out, 1)

            def first_keys(g, q, n):
                if not isinstance(n, int) or n > 0:
                    act.wait_ge(S("first_ready"), n)
                for j in range(TOK):
                    tok = slice(TOK * q + j, TOK * q + j + 1) if isinstance(q, int) else bass.ds(TOK * q + j, 1)
                    last = nc.scalar.activation(apart[:, j, :], iota_sb[:, :], ACT.Abs, bias=IJW[:, 0, tok], scale=-1.0)
                    last.then_inc(S("apart_ready"), 1)
                act.wait_ge(S("apart_ready"), TOK * n + TOK)
                nc.scalar.activation(rows_[g][:, 0], apart, ACT.Relu, bias=1.0, scale=-1.0).then_inc(S("first_ready"), 1)
            act.wait_ge(S("IJW_ready"), 1)
            first_keys(0, 0, 0)
            with act.Fori(0, T // TOK // ROWS - 1) as r:
                for g in range(ROWS):
                    spread_copy(g, ROWS * r + g)
                    if g == 0:
                        first_keys(g, ROWS * (r + 1), r + 1)
            def high_v(k, h, load, again):
                act.wait_ge(v_here[k], load)
                if again:
                    act.wait_ge(v_used, h - 3)
                nc.scalar.activation(Vs[:, k, 0, :], vraw[k // 2][:, HALF * (k % 2):HALF * (k % 2 + 1)], ACT.Copy).then_inc(v_high, 1)
            for g in range(ROWS):
                spread_copy(g, T // TOK - ROWS + g)
                high_v(g, g, 16, False)

            nc.scalar.preload_act_table(ACT.Gelu_apprx_tanh)
            with act.Fori(0, (EARLY - 2) // 2) as r:
                for k in range(4):
                    high_v(k, 4 * r + 4 + k, 16 * r + 32, True)

            def fused(r, more_u):
                for k in range(2):
                    m = 2 * r + 2 + k
                    if more_u:
                        high_u(2 * k, 2 * (m + PTILES + QT) + 4, 16 * r + 48 + 8 * (PTILES + QT), True)
                    if not isinstance(r, int) or r > EARLY // 2:
                        act.wait_ge(coef_done, m - 1)
                    take_tile(k, m + QT, actr[k])
                    if more_u:
                        high_u(2 * k + 1, 2 * (m + PTILES + QT) + 5, 16 * r + 48 + 8 * (PTILES + QT), True)
                    for a in range(2):
                        high_v(2 * k + a, 2 * m + a, 16 * r + 32, True)
            fused((EARLY - 2) // 2, True)
            with act.Fori(EARLY // 2, (NT - 4) // 2) as r:
                fused(r, True)
            fused((NT - 4) // 2, False)
            nc.scalar.preload_act_table(ACT.Sqrt)
            act.wait_ge(v_used, 2 * NT)
            for t in range(TT):
                nc.scalar.activation(yfin[:, t, :], aux[t][:, :], ACT.Square, accum_out=stat[:, 5, t:t + 1]).then_inc(S("ssq"), 1)
            root(5, 2, 6)

        @block.vector
        def _(dve):
            TTn, TS = nc.vector.tensor_tensor, nc.vector.tensor_scalar
            links = [0]

            def link(ins):
                links[0] += 1
                ins.then_inc(S("dve_chain"), 1)
                dve.wait_ge(S("dve_chain"), links[0])

            def flat(v):
                names = "abc"[:len(v.shape) - 1]
                return v.rearrange(f"p {' '.join(names)} -> p ({' '.join(names)})")

            def over(v, n):
                return v.unsqueeze(len(v.shape)).to_broadcast([*v.shape, n])

            def mean(n, w, scale, ssqs, halves=False):
                dve.wait_ge(S("ssq"), ssqs)
                if halves:
                    link(TTn(stat[:, n, 0:w], stat[:, n, 0:w], stat[:, n, w:2 * w], ALU.add))
                TS(stat[:, n, 8:8 + w], stat[:, n, 0:w], scale, EPS, ALU.mult, ALU.add).then_inc(S("var"), 1)

            def normed(src, n, roots, hn=hn):
                dve.wait_ge(S("root"), roots)
                link(nc.vector.reciprocal(stat[:, n, 8:10], stat[:, n, 8:10]))
                for t in range(TT):
                    TS(hn[:, t, :], src[:, t, :], stat[:, n, 8 + t:9 + t], None, ALU.mult).then_inc(S("hn_ready"), 1)

            def low_act(name, dst, src):
                dve.wait_ge(h_high, split_no[name])
                TTn(dst[:, 1], src, dst[:, 0].bitcast(f32), ALU.subtract).then_inc(h_low, 1)

            def aux_take(name):
                dve.wait_ge(aux_full, aux_no[name] + 1)
                return aux[aux_no[name] % 2]

            def turned(names, gain, proj_before, dst=hT):
                if proj_before:
                    full(dve, proj_before)
                for i, n in enumerate(names):
                    ps = aux_take(n)
                    TTn(dst[:, 4 * i:4 * i + 4, :], ps[:, :].rearrange("p (k t) -> p k t", k=4),
                        over(gain_sb[:, gain, 4 * i:4 * i + 4], T), ALU.mult).then_inc(S("hT_ready"), 1)

            mean(0, 2, 1.0 / D, 2)
            dve.wait_ge(const_here, 16 * 7)
            normed(x_sb, 0, 1)
            nc.vector.tensor_copy(relbb[0:BUCKETS + 1, :, :], over(relb[:, :], P)).then_inc(S("relbb_ready"), 1)
            link(TTn(tiny[:, 2, :], low_sb[:, 0, :], low_sb[:, 1, :], ALU.max))
            TTn(tiny[:, 0, :], low_sb[:, 0, :], tiny[:, 2, :], ALU.subtract)
            TTn(tiny[:, 1, :], low_sb[:, 1, :], tiny[:, 2, :], ALU.subtract).then_inc(S("low_ready"), 1)
            turned(["tx0", "tx1"], 0, None)
            for i in range(2):
                low_act(f"tx{i}", xTs[:, :, 4 * i:4 * i + 4], hT[:, 4 * i:4 * i + 4])
            mean(1, 2, 1.0 / D, 4)
            dve.wait_ge(S("low_exp"), 1)
            link(TTn(tiny[:, 2, :], tiny[:, 0, :], tiny[:, 1, :], ALU.add))
            link(nc.vector.reciprocal(tiny[:, 3, :], tiny[:, 2, :]))
            TTn(lb[:, 0, :], tiny[:, 0, :], tiny[:, 3, :], ALU.mult)
            link(TTn(lb[:, 1, :], tiny[:, 1, :], tiny[:, 3, :], ALU.mult))
            dve.wait_ge(S("hf_read"), 2)
            link(TS(DI, DI, 1.0, None, ALU.add))
            link(nc.vector.reciprocal(DI, DI))
            for h in range(HG_H):
                last = TS(E_[:, h * T:(h + 1) * T], DI[:, h * T:(h + 1) * T], lb[:, 1, h:h + 1], lb[:, 0, h:h + 1], ALU.mult, ALU.add)
            link(last)
            TS(flat(kT), E_, -1.0, 1.0, ALU.mult, ALU.add).then_inc(S("k_ready"), 1)
            dve.wait_ge(S("lf_ready"), 1)
            dve.wait_ge(S("restart_ready"), 1)
            nc.vector.tensor_tensor_scan(bsum, restart, E_, 0.0, ALU.mult, ALU.add).then_inc(S("b_ready"), 1)
            dve.wait_ge(S("b_ready"), 1)

            def level_diff(i):
                if i >= 1:
                    dve.wait_ge(S("decay"), i)
                if i < len(LEVELS):
                    L = LEVELS[i]
                    b = bsum.rearrange("p (n a l) -> p n a l", a=2, l=L)
                    d = DI.rearrange("p (n a l) -> p n a l", a=2, l=L)
                    mid = b[:, :, 0, L - 1:L].to_broadcast([P, T * HG_H // (2 * L), L])
                    if L < CHUNK:
                        TTn(d[:, :, 1, :], b[:, :, 1, :], mid, ALU.subtract).then_inc(S("diff"), 1)
                    else:
                        nc.vector.tensor_copy(d[:, :, 1, :], b[:, :, 1, :]).then_inc(S("diff"), 1)
                    TTn(d[:, :, 0, :], mid, b[:, :, 0, :], ALU.subtract).then_inc(S("diff"), 1)
                else:
                    b = bsum.rearrange("p (h n l) -> p h n l", n=4, l=CHUNK)
                    d = DI.rearrange("p (h n l) -> p h n l", n=4, l=CHUNK)
                    end = [b[:, :, c, CHUNK - 1:CHUNK].to_broadcast([P, HG_H, CHUNK]) for c in range(4)]
                    nc.vector.tensor_copy(d[:, :, 2, :], b[:, :, 2, :]).then_inc(S("diff"), 1)
                    TTn(d[:, :, 3, :], b[:, :, 3, :], end[2], ALU.add).then_inc(S("diff"), 1)
                    TTn(d[:, :, 1, :], end[1], b[:, :, 1, :], ALU.subtract).then_inc(S("diff"), 1)
                    TTn(d[:, :, 0, :], end[0], b[:, :, 0, :], ALU.subtract).then_inc(S("dve_chain"), 1)
                    links[0] += 1
                    dve.wait_ge(S("dve_chain"), links[0])
                    TTn(d[:, :, 0, :], d[:, :, 0, :], end[1], ALU.add).then_inc(S("diff"), 1)

            def level_qk(i):
                dve.wait_ge(S("decay"), i + 1)
                if i == 0:
                    dve.wait_ge(S("cleared"), 5)
                    dve.wait_ge(S("hq_read"), 2)
                if i >= 2:
                    L = (LEVELS + [128])[i - 2]
                    dve.wait_ge(aux_full, aux_no[f"L{L}"] + 1)
                L = (LEVELS + [128])[i]
                half = lambda v, a: v.rearrange("p (n a l) -> p n a l", a=2, l=L)[:, :, a, :]
                TTn(half(flat(QE[i % 2]), 1), half(flat(hqT), 1), half(E_, 1), ALU.mult)
                TTn(half(flat(KE[i % 2]), 0), half(flat(kT), 0), half(E_, 0), ALU.mult).then_inc(S("QK"), 1)

            def level_take(name):
                ps = aux_take(f"L{name}")
                m = ident[:, :] if name == "diag" else mask_sb[:, LEVELS.index(name), :]
                m = m.bitcast(u32).unsqueeze(1).to_broadcast([P, HG_H * TT, P])
                nc.vector.copy_predicated(ATd, m, ps[:, :].rearrange("p (b t) -> p b t", b=HG_H * TT)).then_inc(S("level_read"), 1)
                dve.wait_ge(S("level_read"), ([*["diag"], *LEVELS]).index(name) + 1)

            level_diff(0)
            level_qk(0)
            dve.wait_ge(masks_here, 16)
            level_take("diag")
            level_diff(1)
            level_qk(1)
            level_take(1)
            dve.wait_ge(S("bias_here"), 16)
            for name, s_, bb in (("S0", S0, biasB[:, :, P:T]), ("S1a", S1[:, 0:4, :], biasB[:, 0:4, :]), ("S1b", S1[:, 4:8, :], biasB[:, 4:8, :])):
                ps = aux_take(name)
                for odd in range(2):
                    nc.vector.scalar_tensor_tensor(
                        out=s_[:, odd::2, :], in0=ps[:, 512 * odd:512 * odd + 512].rearrange("p (h k) -> p h k", k=s_.shape[2]),
                        scalar=MB_D ** -0.5, in1=bb[:, odd::2, :], op0=ALU.mult, op1=ALU.add).then_inc(S("biased"), 1)
            dve.wait_ge(S("biased"), 6)
            for t, s_ in ((0, S0), (1, S1)):
                nc.vector.tensor_reduce(smx[:, t, 0:MB_H], s_, AX.X, ALU.max, negate=True).then_inc(S("mb_max"), 1)
            for i, before in ((2, 2), (3, 4)):
                level_diff(i)
                level_qk(i)
                level_take(before)
            dve.wait_ge(S("hg_read"), 2)
            link(TS(flat(hgtmp), flat(hgtmp), 1.0, None, ALU.add))
            link(nc.vector.reciprocal(flat(hgtmp), flat(hgtmp)))
            TTn(flat(hg_sb), flat(hg_sb), flat(hgtmp), ALU.mult).then_inc(S("silu_ready"), 1)
            level_diff(4)
            level_qk(4)
            level_take(8)
            dve.wait_ge(S("mb_exp"), 16)
            link(nc.vector.reciprocal(smx[:, 2:4, 0:MB_H], smx[:, 2:4, 0:MB_H]))
            TTn(S0, S0, over(smx[:, 2, 0:MB_H], P), ALU.mult).then_inc(S("mb_prob"), 1)
            TTn(S1, S1, over(smx[:, 3, 0:MB_H], T), ALU.mult).then_inc(S("mb_prob"), 1)
            level_diff(5)
            level_qk(5)
            level_take(16)
            level_diff(6)
            level_qk(6)
            level_diff(7)
            level_take(32)
            level_qk(7)
            level_take(64)
            dve.wait_ge(aux_full, aux_no["PTc"] + 1)
            normed(mem_sb, 1, 2, hnM)

            def sigmoid(v, fam, i):
                dve.wait_ge(S(f"{fam}_read"), 2 * i + 2)
                v = flat(v[:, 4 * i:4 * i + 4, :])
                link(TS(v, v, 1.0, None, ALU.add))
                nc.vector.reciprocal(v, v).then_inc(S("sig_ready"), 1)
            sigmoid(sgA, "ga", 0)
            dve.wait_ge(S("o_read"), 1)
            link(TTn(osq, osb, osb, ALU.mult))
            nc.vector.tensor_reduce(stat[:, 2, 0:8], osq.rearrange("p t h e -> p (t h) e"), AX.X, ALU.add).then_inc(S("ssq"), 1)
            mean(2, 8, 1.0 / HG_D, 5)
            turned(["tm0", "tm1"], 3, None, memT)
            dve.wait_ge(S("root"), 3)
            link(nc.vector.reciprocal(stat[:, 2, 8:16], stat[:, 2, 8:16]))
            o3 = osb.rearrange("p t h e -> p (t h) e")
            dve.wait_ge(S("silu_ready"), 1)
            link(TTn(o3, o3, over(stat[:, 2, 8:16], HG_D), ALU.mult))
            of = osb.rearrange("p t h e -> p (t h e)")
            TTn(of, of, flat(hg_sb), ALU.mult).then_inc(S("o_ready"), 1)
            low_act("yb", As[:, :, 4:8], ybT)
            for i in range(2):
                low_act(f"mem{i}", hTs[:, :, 4 * i:4 * i + 4], memT[:, 4 * i:4 * i + 4])
            sigmoid(sgA, "ga", 1)
            TTn(yaT, aux_take("TY")[:, :].rearrange("p (h t) -> p h t", h=HG_H), over(hgn_sb[:, :], T), ALU.mult).then_inc(S("yaT_ready"), 1)
            low_act("ya", As[:, :, 0:4], yaT)
            sigmoid(sgB, "gb", 0)
            dve.wait_ge(S("sig_ready"), 2)
            for b in range(4):
                g = bank_no["upa0"] + b
                full(dve, "upa0", b)
                TTn(flat(sgA[:, 2 * b:2 * b + 2, :]), flat(sgA[:, 2 * b:2 * b + 2, :]), gb_[g % NG][:, :], ALU.mult).then_inc(S("upa_read"), 1)
            sigmoid(sgB, "gb", 1)
            dve.wait_ge(S("sig_ready"), 4)
            for b in range(4):
                g = bank_no["upb0"] + b
                full(dve, "upb0", b)
                TTn(flat(sgB[:, 2 * b:2 * b + 2, :]), flat(sgB[:, 2 * b:2 * b + 2, :]), gb_[g % NG][:, :], ALU.mult).then_inc(S("upb_read"), 1)
                dve.wait_ge(S("upb_read"), b + 1)
                TTn(flat(zT[:, 2 * b:2 * b + 2, :]), flat(sgA[:, 2 * b:2 * b + 2, :]), flat(sgB[:, 2 * b:2 * b + 2, :]), ALU.add).then_inc(S("z_ready"), 1)
            for b in range(4):
                low_act(f"z{b}", As[:, :, 2 * b:2 * b + 2], zT[:, 2 * b:2 * b + 2])

            def add_to_x(fam):
                for c in range(2):
                    for t in range(TT):
                        g = bank_no[f"{fam}{c}"] + t
                        full(dve, f"{fam}{c}", t)
                        xs = x_sb[:, t, 512 * c:512 * (c + 1)]
                        TTn(xs, xs, gb_[g % NG][:, :], ALU.add).then_inc(S(bank_reader[g][0]), 1)
                    dve.wait_ge(S(f"{fam}_read"), 2 * c + 2)
                    nc.vector.engine_nop().then_inc(S("x_new"), 1)
            add_to_x("out")
            mean(3, 2, 1.0 / D, 9, True)
            normed(x_sb, 3, 4, hnF)
            turned(["tc0", "tc1"], 1, "gb1")
            for i in range(2):
                low_act(f"tc{i}", xTs[:, :, 4 * i:4 * i + 4], hT[:, 4 * i:4 * i + 4])
            for t in range(TT):
                ps = aux_take(f"CS{t}")
                m = smx[:, 4, 4 * t:4 * t + 4]
                link(nc.vector.tensor_reduce(m, ps[:, :].rearrange("p (h m) -> p h m", h=X_H), AX.X, ALU.max, negate=True))
                TS(m, m, X_D ** -0.5, None, ALU.mult).then_inc(S("x_max"), 1)
            for t in range(TT):
                dve.wait_ge(S("xexp"), 4 * t + 4)
                r_ = smx[:, 5, 4 * t:4 * t + 4]
                link(nc.vector.reciprocal(r_, r_))
                TTn(CS[:, t], CS[:, t], over(r_, T), ALU.mult).then_inc(S("x_prob"), 1)
            for c in range(2):
                low_act(f"ox{c}", As[:, :, 4 * c:4 * c + 4], oxT[:, 4 * c:4 * c + 4])
            add_to_x("wo")
            mean(4, 2, 1.0 / D, 13, True)
            normed(x_sb, 4, 5, hnF)
            turned(["tf0", "tf1"], 2, "qx1")
            for i in range(2):
                low_act(f"tf{i}", hTs[:, :, 4 * i:4 * i + 4], hT[:, 4 * i:4 * i + 4])

            def top16(rows, src, spare, vals, idx):
                for r in rows:
                    last = nc.vector.max(vals(r)[:, 0:8], src(r))
                link(last)
                for r in rows:
                    nc.vector.max_index(idx(r)[:, 0:8], vals(r)[:, 0:8], src(r))
                    last = nc.vector.match_replace(spare(r), vals(r)[:, 0:8], src(r), LOWEST)
                link(last)
                for r in rows:
                    last = nc.vector.max(vals(r)[:, 8:16], spare(r))
                link(last)
                for r in rows:
                    last = nc.vector.max_index(idx(r)[:, 8:16], vals(r)[:, 8:16], spare(r))
                link(last)

            full(dve, "wo1")
            dve.wait_ge(aux_full, aux_no["PS3"] + 1)
            for t in range(TT):
                dve.wait_ge(S("sc_read"), 2 * t + 2)
                top16(range(2 * PH), lambda r: sc[:, t, r, :], lambda r: sc2[:, t, r, :],
                      lambda r: sv[:, t, r, :], lambda r: si[:, t, r, :].bitcast(u32))
                link(nc.vector.tensor_copy(flat(sif[:, t]), flat(si[:, t]).bitcast(u32)))
                s4 = sv[:, t].rearrange("p (h c) k -> p h c k", c=2)
                i4 = sif[:, t].rearrange("p (h c) k -> p h c k", c=2)
                link(TTn(cand.rearrange("p h (a b) -> p h a b", a=PK), over(s4[:, :, 0, :], PK),
                         s4[:, :, 1, :].unsqueeze(2).to_broadcast([P, PH, PK, PK]), ALU.add))
                top16(range(PH), lambda r: cand[:, r, :], lambda r: cand2[:, r, :],
                      lambda r: fv[:, t, r, :], lambda r: pos[:, t, r, :].bitcast(u32))
                m = fv[:, t, :, 0:1]
                nc.vector.tensor_copy(wsum[:, t, :], m.rearrange("p h o -> p (h o)")).then_inc(S("dve_chain"), 1)
                pf = flat(pos[:, t]).bitcast(u32)
                TS(ab[:, 0, :].bitcast(u32), pf, 4, None, ALU.logical_shift_right).then_inc(S("dve_chain"), 1)
                TS(ab[:, 1, :].bitcast(u32), pf, PK - 1, None, ALU.bitwise_and).then_inc(S("dve_chain"), 1)
                links[0] += 3
                dve.wait_ge(S("dve_chain"), links[0])
                TTn(fv[:, t], fv[:, t], over(wsum[:, t, :], PK), ALU.subtract).then_inc(S("w_diff"), 1)
                link(nc.vector.tensor_copy(flat(abf), flat(ab).bitcast(u32)))
                for c in range(2):
                    link(TTn(eq, over(abf[:, c, :], PK), iota_sb[:, 0:PK].unsqueeze(1).to_broadcast([P, PH * PK, PK]), ALU.is_equal))
                    link(TTn(eq2.rearrange("p (h k) a -> p h k a", h=PH), eq.rearrange("p (h k) a -> p h k a", h=PH),
                             i4[:, :, c, :].unsqueeze(2).to_broadcast([P, PH, PK, PK]), ALU.mult))
                    nc.vector.tensor_reduce(rIJW[:, c, t, :], eq2, AX.X, ALU.add).then_inc(S("rIJW_ready"), 1)
            for t in range(TT):
                dve.wait_ge(S("w_exp"), t + 1)
                link(nc.vector.tensor_reduce(wsum[:, t, :], fv[:, t], AX.X, ALU.add))
                link(nc.vector.reciprocal(wsum[:, t, :], wsum[:, t, :]))
                TTn(rIJW[:, 2, t, :].rearrange("p (h k) -> p h k", h=PH), fv[:, t], over(wsum[:, t, :], PK), ALU.mult).then_inc(S("rIJW_ready"), 1)
            nc.vector.tensor_copy(flat(IJW), aux_take("TR")[:, 0:3 * T]).then_inc(S("IJW_ready"), 1)
            dve.wait_ge(S("IJW_ready"), 1)

            def rows(g, tok):
                if g == 0:
                    TTn(rows_[g][:, 1], iota_sb[:, :].unsqueeze(1).to_broadcast([P, TOK, NKEY]),
                        IJW[:, 1, tok].unsqueeze(2).to_broadcast([P, TOK, NKEY]), ALU.is_equal).then_inc(onehots, 1)
                    return
                TTn(rows_[g], iota_sb[:, :].unsqueeze(1).unsqueeze(1).to_broadcast([P, 2, TOK, NKEY]),
                    IJW[:, 0:2, tok].unsqueeze(3).to_broadcast([P, 2, TOK, NKEY]), ALU.is_equal).then_inc(onehots, 1)

            def gate_early(g, q):
                dve.wait_ge(spread_out, q + 1)
                v = gate[:, 0:EARLY, bass.ds(TOK * q, TOK)]
                TTn(v, v, gb_[g][:, :].rearrange("p (t i) -> p i t", t=TOK)[:, 0:EARLY, :], ALU.mult).then_inc(early_gated, 1)
            dve.wait_ge(tile_out, QT + EARLY)
            for g in range(ROWS):
                rows(g, slice(TOK * g, TOK * (g + 1)))
            with dve.Fori(0, T // TOK // ROWS - 1) as r:
                for g in range(ROWS):
                    dve.wait_ge(spread_done, ROWS * r + g + 1)
                    rows(g, bass.ds(TOK * (ROWS * (r + 1) + g), TOK))
                    gate_early(g, ROWS * r + g)
            def low_v(k, h):
                dve.wait_ge(v_high, h + 1)
                TTn(Vs[:, k, 1, :], vraw[k // 2][:, HALF * (k % 2):HALF * (k % 2 + 1)], Vs[:, k, 0, :].bitcast(f32),
                    ALU.subtract).then_inc(v_low, 1)

            for g in range(ROWS):
                gate_early(g, T // TOK - ROWS + g)
                if g:
                    low_v(g - 1, g - 1)

            dve.wait_ge(spread_out, T // TOK)
            dve.wait_ge(early_gated, T // TOK)

            def split_coef(k, m, src, again):
                if again:
                    dve.wait_ge(v_used, 2 * m - 2)
                nc.vector.tensor_copy(Cs[:, k, 0, :].unsqueeze(1), src).then_inc(S("coef_high"), 1)
                dve.wait_ge(S("coef_high"), m + 1)
                TTn(Cs[:, k, 1, :].unsqueeze(1), src, Cs[:, k, 0, :].bitcast(f32).unsqueeze(1), ALU.subtract).then_inc(coef_done, 1)
            for k in range(2):
                split_coef(k, k, gate[:, k:k + 1, :], False)
            low_v(ROWS - 1, ROWS - 1)
            with dve.Fori(0, (EARLY - 2) // 2) as r:
                for k in range(2):
                    m = 2 * r + 2 + k
                    low_v(2 * k, 2 * m)
                    split_coef(k, m, gate[:, bass.ds(m, 1), :], True)
                    low_v(2 * k + 1, 2 * m + 1)
            with dve.Fori((EARLY - 2) // 2, (NT - 2) // 2) as r:
                for k in range(2):
                    m = 2 * r + 2 + k
                    low_v(2 * k, 2 * m)
                    dve.wait_ge(tile_out, m + 1 + QT)
                    TTn(actr[k].unsqueeze(1), actr[k].unsqueeze(1), gate[:, bass.ds(m, 1), :], ALU.mult).then_inc(product, 1)
                    dve.wait_ge(product, m + 1 - EARLY)
                    split_coef(k, m, actr[k].unsqueeze(1), True)
                    low_v(2 * k + 1, 2 * m + 1)
            mean(5, 2, 1.0 / D, 15)
            dve.wait_ge(S("root"), 6)
            link(nc.vector.reciprocal(stat[:, 5, 8:10], stat[:, 5, 8:10]))
            dve.wait_ge(S("fgain_here"), 16)
            for t in range(TT):
                nc.vector.scalar_tensor_tensor(out=yfin[:, t, :], in0=aux[t][:, :], scalar=stat[:, 5, 8 + t:9 + t],
                                               in1=fgain, op0=ALU.mult, op1=ALU.mult).then_inc(S("y_ready"), 1)


def level_masks():
    s, t = np.arange(P)[:, None], np.arange(P)[None, :]
    rows = [(s // (2 * L) == t // (2 * L)) & (s // L % 2 == 0) & (t // L % 2 == 1) for L in LEVELS]
    return np.stack(rows + [s == t]).astype(np.float32)


def bucket_onehot():
    import math
    dist = 255 - np.arange(ROW)
    exact = BUCKETS // 2
    d = np.maximum(dist, 1).astype(np.float32)
    scaled = np.log(d / np.float32(exact)) / np.float32(math.log(MAX_DIST / exact))
    large = np.minimum(exact + (scaled * np.float32(BUCKETS - exact)).astype(np.int32), BUCKETS - 1)
    b = np.where(dist < exact, dist, large)
    b = np.where(dist < 0, BUCKETS, b)
    return (np.arange(BUCKETS + 1)[:, None] == b[None, :]).astype(np.float32)


def kernel(**inputs):
    import concourse.bacc as bacc
    from concourse.bass_utils import run_bass_kernel_spmd

    a = {k: np.asarray(v) for k, v in inputs.items()}

    def pieces(w, c, form):
        if form == "U":
            return w.reshape(4, P, 8, P).transpose(2, 1, 0, 3).reshape(8, P, HALF)
        w = w[:, 512 * c:512 * (c + 1)]
        if form == "N":
            return w.reshape(8, P, HALF)
        return w.reshape(2, 4, P, 4, P).transpose(3, 0, 2, 1, 4).reshape(8, P, HALF)
    source = {"gb": "w_in", "kx": "wk_x", "upa": "w_up_a", "upb": "w_up_b", "out": "w_out", "vx": "wv_x", "qx": "wq_x", "wo": "wo_x"}

    def columns(v):
        return v.reshape(-1, P).T

    arrays = {
        "x": a["x"][0], "mem": a["mem"][0], "rel_bias": a["rel_bias"],
        "first_pieces": np.concatenate([pieces(a["w_in"][0], c, form) for n, c, form in FIRST]),
        "pieces": np.concatenate([pieces(a[source[n[:-1]]][0], c, form) for n, c, form in SECOND]).reshape(PTILES, 2, P, HALF).transpose(0, 2, 1, 3).reshape(PTILES, P, D),
        "peer_query": a["peer_query"][0].reshape(KD, P, QT, P).transpose(2, 1, 0, 3).reshape(QT, P, D),
        "subkeys": a["peer_subkeys"][0].reshape(2 * PH, NKEY, P).transpose(2, 0, 1),
        "peer_u": a["peer_u"][0].reshape(NT, P, KD, P).transpose(0, 3, 2, 1).reshape(NT, P, D),
        "peer_v": a["peer_v"][0].reshape(NT, P, D),
        "gains": np.stack([columns(a[k][0]) for k in ("ln_mix", "ln_cross", "ln_ffn", "ln_mem")], axis=1),
        "hg_lower": np.stack([columns(a["hg_lower"][i]) for i in range(2)], axis=1),
        "hg_norm": columns(a["hg_norm"][0]),
        "ln_final": a["ln_final"],
        "onehot": bucket_onehot(), "masks": level_masks(),
        "iota": np.tile(np.arange(NKEY, dtype=np.float32), (P, 1)),
    }
    nc = bacc.Bacc("TRN2", target_bir_lowering=False, num_devices=1)
    arrays = {k: np.ascontiguousarray(v) for k, v in arrays.items()}
    args = {k: nc.dram_tensor(f"in_{k}", v.shape, mybir.dt.from_np(v.dtype), kind="ExternalInput").ap() for k, v in arrays.items()}
    out = nc.dram_tensor("out", (T, D), mybir.dt.float32, kind="ExternalOutput").ap()
    hybrid_layer(nc, **args, out=out)
    got = run_bass_kernel_spmd(nc, [{f"in_{k}": v for k, v in arrays.items()}], core_ids=[0])
    return got.results[0]["out"].reshape(1, T, D)
```
